# Optimizing a Trainium2 kernel written in Bass

```python
import jax
import jax.numpy as jnp
from jax import lax
import numpy as np

D_MODEL = 1024
BATCH = 1
SEQ = 256
DEPTH = 2
DEC_BATCH = 8
DEC_SEQ = 16
PAST_LEN = 512

CHUNK = 64
QBLK = 128
N_MIXERS = 2
N_MLA = (DEPTH + 1) // 2
N_RET = DEPTH // 2
MLA_HEADS = D_MODEL // 128
QK_NOPE = 128
QK_ROPE = 64
V_HEAD = 128
Q_LORA = 3 * D_MODEL // 8
KV_LORA = D_MODEL // 4
MLA_SCALE = (QK_NOPE + QK_ROPE) ** -0.5
RET_HEADS = 4
RET_DK = D_MODEL // RET_HEADS
RET_DV = 2 * D_MODEL // RET_HEADS
FFN_DIM = 256 * ((8 * D_MODEL // 3 + 255) // 256)
EPS = 1e-6
ROPE_THETA = 10000.0

kernel_name = 'mla_retention_macaron_stream_step'

def rmsnorm(x, g):
    xf = x.astype(jnp.float32)
    y = xf * lax.rsqrt(jnp.mean(xf * xf, axis=-1, keepdims=True) + EPS)
    return (y * g.astype(jnp.float32)).astype(x.dtype)

def rope(x, pos):
    d = x.shape[-1]
    inv = 1.0 / (ROPE_THETA ** (jnp.arange(0, d, 2, dtype=jnp.float32) / d))
    ang = pos.astype(jnp.float32)[:, None] * inv[None, :]
    ang = ang.reshape(ang.shape[:1] + (1,) * (x.ndim - 3) + ang.shape[1:])
    cos, sin = jnp.cos(ang), jnp.sin(ang)
    x1, x2 = x[..., : d // 2], x[..., d // 2:]
    return jnp.concatenate([x1 * cos - x2 * sin, x1 * sin + x2 * cos], axis=-1).astype(x.dtype)

def swiglu(h, wg, wu, wd):
    return (jax.nn.silu(h @ wg) * (h @ wu)) @ wd

def ffn_half(x, g, wg, wu, wd):
    return x + 0.5 * swiglu(rmsnorm(x, g), wg, wu, wd)

def mla_project(h, pos, w_dq, q_norm, w_uq, w_dkv, kv_norm):
    b, s, _ = h.shape
    cq = rmsnorm(h @ w_dq, q_norm)
    q = (cq @ w_uq).reshape(b, s, MLA_HEADS, QK_NOPE + QK_ROPE)
    q_nope, q_pe = q[..., :QK_NOPE], rope(q[..., QK_NOPE:], pos)
    kv = h @ w_dkv
    ckv = rmsnorm(kv[..., :KV_LORA], kv_norm)
    kpe = rope(kv[..., KV_LORA:], pos)
    return q_nope, q_pe, ckv, kpe

def mla_prompt(h, pos, w_dq, q_norm, w_uq, w_dkv, kv_norm, w_uk, w_uv, w_o):
    b, s, _ = h.shape
    q_nope, q_pe, ckv, kpe = mla_project(h, pos, w_dq, q_norm, w_uq, w_dkv, kv_norm)
    k_nope = jnp.einsum('bkl,lhn->bkhn', ckv, w_uk)
    v = jnp.einsum('bkl,lhv->bkhv', ckv, w_uv)
    outs = []
    for blk in range(s // QBLK):
        q0 = blk * QBLK
        kend = q0 + QBLK
        sc = (jnp.einsum('bqhn,bkhn->bhqk', q_nope[:, q0:kend], k_nope[:, :kend])
              + jnp.einsum('bqhr,bkr->bhqk', q_pe[:, q0:kend], kpe[:, :kend]))
        sc = sc.astype(jnp.float32) * MLA_SCALE
        q_chunk = (q0 + jnp.arange(QBLK)) // CHUNK
        k_chunk = jnp.arange(kend) // CHUNK
        mask = k_chunk[None, :] <= q_chunk[:, None]
        p = jax.nn.softmax(jnp.where(mask, sc, -jnp.inf), axis=-1).astype(v.dtype)
        outs.append(jnp.einsum('bhqk,bkhv->bqhv', p, v[:, :kend]))
    o = jnp.concatenate(outs, axis=1).reshape(b, s, MLA_HEADS * V_HEAD)
    return (o @ w_o).astype(h.dtype), ckv, kpe

def mla_sample(h, pos, c_ckv, c_kpe, w_dq, q_norm, w_uq, w_dkv, kv_norm, w_uk, w_uv, w_o):
    b, s, _ = h.shape
    past = c_ckv.shape[1]
    q_nope, q_pe, ckv, kpe = mla_project(h, pos, w_dq, q_norm, w_uq, w_dkv, kv_norm)
    q_lat = jnp.einsum('bqhn,lhn->bqhl', q_nope, w_uk)
    s_past = (jnp.einsum('bqhl,bkl->bhqk', q_lat, c_ckv)
              + jnp.einsum('bqhr,bkr->bhqk', q_pe, c_kpe))
    s_new = (jnp.einsum('bqhl,bkl->bhqk', q_lat, ckv)
             + jnp.einsum('bqhr,bkr->bhqk', q_pe, kpe))
    sc = jnp.concatenate([s_past, s_new], axis=-1).astype(jnp.float32) * MLA_SCALE
    p = jax.nn.softmax(sc, axis=-1).astype(ckv.dtype)
    o_lat = (jnp.einsum('bhqk,bkl->bqhl', p[..., :past], c_ckv)
             + jnp.einsum('bhqk,bkl->bqhl', p[..., past:], ckv))
    o = jnp.einsum('bqhl,lhv->bqhv', o_lat, w_uv).reshape(b, s, MLA_HEADS * V_HEAD)
    return (o @ w_o).astype(h.dtype), ckv, kpe

def ret_log_gamma():
    return jnp.log(1.0 - 2.0 ** (-5.0 - jnp.arange(RET_HEADS, dtype=jnp.float32)))

def ret_project(h, pos, w_in):
    b, s, _ = h.shape
    qk_w = RET_HEADS * RET_DK
    v_w = RET_HEADS * RET_DV
    q, k, v, g = jnp.split(h @ w_in, [qk_w, 2 * qk_w, 2 * qk_w + v_w], axis=-1)
    q = rope(q.reshape(b, s, RET_HEADS, RET_DK), pos)
    k = rope(k.reshape(b, s, RET_HEADS, RET_DK), pos) * (RET_DK ** -0.5)
    v = v.reshape(b, s, RET_HEADS, RET_DV)
    return q, k, v, g

def ret_chunk(state, qkv):
    q, k, v = (t.astype(jnp.float32) for t in qkv)
    state = state.astype(jnp.float32)
    L = q.shape[1]
    lg = ret_log_gamma()
    idx = jnp.arange(L, dtype=jnp.float32)
    diff = idx[:, None] - idx[None, :]
    decay = jnp.where(diff >= 0, jnp.exp(lg[:, None, None] * jnp.maximum(diff, 0.0)), 0.0)
    qk = jnp.einsum('bihd,bjhd->bhij', q, k) * decay
    o = jnp.einsum('bhij,bjhe->bihe', qk, v)
    xi = jnp.exp(lg[None, :] * (idx[:, None] + 1.0))
    o = o + jnp.einsum('bihd,bhde->bihe', q * xi[None, :, :, None], state)
    zeta = jnp.exp(lg[None, :] * (L - 1.0 - idx[:, None]))
    new_state = (jnp.exp(lg * L)[None, :, None, None] * state
                 + jnp.einsum('bjhd,bjhe->bhde', k * zeta[None, :, :, None], v))
    return new_state, o

def ret_output(o, g, ret_gn, w_out, dtype):
    b, s = o.shape[:2]
    y = rmsnorm(o, ret_gn.reshape(RET_HEADS, RET_DV)).reshape(b, s, RET_HEADS * RET_DV)
    return ((jax.nn.silu(g.astype(jnp.float32)) * y) @ w_out).astype(dtype)

def ret_prompt(h, pos, w_in, ret_gn, w_out):
    b, s, _ = h.shape
    q, k, v, g = ret_project(h, pos, w_in)
    n = s // CHUNK

    def to_chunks(t):
        return t.reshape((b, n, CHUNK) + t.shape[2:]).swapaxes(0, 1)

    s0 = jnp.zeros((b, RET_HEADS, RET_DK, RET_DV), jnp.float32)
    s_final, o = lax.scan(ret_chunk, s0, (to_chunks(q), to_chunks(k), to_chunks(v)))
    o = o.swapaxes(0, 1).reshape(b, s, RET_HEADS, RET_DV)
    return ret_output(o, g, ret_gn, w_out, h.dtype), s_final

def ret_sample(h, pos, state, w_in, ret_gn, w_out):
    q, k, v, g = ret_project(h, pos, w_in)
    new_state, o = ret_chunk(state, (q, k, v))
    return ret_output(o, g, ret_gn, w_out, h.dtype), new_state

def setup_inputs(seed: int = 0) -> dict:
    key = jax.random.key(seed)
    ks = iter(jax.random.split(key, 40))
    D, F = D_MODEL, FFN_DIM

    def nrm(shape, scale=1.0):
        return jax.random.normal(next(ks), shape, jnp.float32) * scale

    def gain(shape):
        return 1.0 + 0.01 * jax.random.normal(next(ks), shape, jnp.float32)

    return {
        'x_prompt': nrm((BATCH, SEQ, D)),
        'x_sample': nrm((DEC_BATCH, DEC_SEQ, D)),
        'cache_ckv': nrm((N_MLA, DEC_BATCH, PAST_LEN, KV_LORA)),
        'cache_kpe': nrm((N_MLA, DEC_BATCH, PAST_LEN, QK_ROPE)),
        'state_ret': nrm((N_RET, DEC_BATCH, RET_HEADS, RET_DK, RET_DV)),
        'norm_ffn1': gain((DEPTH, D)),
        'w_ffn1_gate': nrm((DEPTH, D, F), D ** -0.5),
        'w_ffn1_up': nrm((DEPTH, D, F), D ** -0.5),
        'w_ffn1_down': nrm((DEPTH, F, D), F ** -0.5),
        'norm_mix': gain((DEPTH, D)),
        'w_dq': nrm((N_MLA, D, Q_LORA), D ** -0.5),
        'q_norm': gain((N_MLA, Q_LORA)),
        'w_uq': nrm((N_MLA, Q_LORA, MLA_HEADS * (QK_NOPE + QK_ROPE)), Q_LORA ** -0.5),
        'w_dkv': nrm((N_MLA, D, KV_LORA + QK_ROPE), D ** -0.5),
        'kv_norm': gain((N_MLA, KV_LORA)),
        'w_uk': nrm((N_MLA, KV_LORA, MLA_HEADS, QK_NOPE), KV_LORA ** -0.5),
        'w_uv': nrm((N_MLA, KV_LORA, MLA_HEADS, V_HEAD), KV_LORA ** -0.5),
        'w_o_mla': nrm((N_MLA, MLA_HEADS * V_HEAD, D), (MLA_HEADS * V_HEAD) ** -0.5),
        'w_ret_in': nrm((N_RET, D, 2 * RET_HEADS * RET_DK + 2 * RET_HEADS * RET_DV), D ** -0.5),
        'ret_gn': gain((N_RET, RET_HEADS * RET_DV)),
        'w_ret_out': nrm((N_RET, RET_HEADS * RET_DV, D), (RET_HEADS * RET_DV) ** -0.5),
        'norm_ffn2': gain((DEPTH, D)),
        'w_ffn2_gate': nrm((DEPTH, D, F), D ** -0.5),
        'w_ffn2_up': nrm((DEPTH, D, F), D ** -0.5),
        'w_ffn2_down': nrm((DEPTH, F, D), F ** -0.5),
        'norm_final': gain((D,)),
    }

def reference(x_prompt, x_sample, cache_ckv, cache_kpe, state_ret,
              norm_ffn1, w_ffn1_gate, w_ffn1_up, w_ffn1_down, norm_mix,
              w_dq, q_norm, w_uq, w_dkv, kv_norm, w_uk, w_uv, w_o_mla,
              w_ret_in, ret_gn, w_ret_out,
              norm_ffn2, w_ffn2_gate, w_ffn2_up, w_ffn2_down, norm_final):
    seq = x_prompt.shape[1]
    past = cache_ckv.shape[2]
    dseq = x_sample.shape[1]
    pos_p = jnp.arange(seq)
    pos_s = past + jnp.arange(dseq)
    xp, xs = x_prompt, x_sample
    ckv_p, kpe_p, st_p = [], [], []
    ckv_s, kpe_s, st_s = [], [], []
    for i in range(DEPTH):
        f1 = (norm_ffn1[i], w_ffn1_gate[i], w_ffn1_up[i], w_ffn1_down[i])
        xp = ffn_half(xp, *f1)
        xs = ffn_half(xs, *f1)
        hp = rmsnorm(xp, norm_mix[i])
        hs = rmsnorm(xs, norm_mix[i])
        j = i // N_MIXERS
        if i % N_MIXERS == 0:
            mw = (w_dq[j], q_norm[j], w_uq[j], w_dkv[j], kv_norm[j], w_uk[j], w_uv[j], w_o_mla[j])
            mp, c_p, r_p = mla_prompt(hp, pos_p, *mw)
            ms, c_s, r_s = mla_sample(hs, pos_s, cache_ckv[j], cache_kpe[j], *mw)
            ckv_p.append(c_p)
            kpe_p.append(r_p)
            ckv_s.append(c_s)
            kpe_s.append(r_s)
        else:
            rw = (w_ret_in[j], ret_gn[j], w_ret_out[j])
            mp, s_p = ret_prompt(hp, pos_p, *rw)
            ms, s_s = ret_sample(hs, pos_s, state_ret[j], *rw)
            st_p.append(s_p)
            st_s.append(s_s)
        xp = xp + mp
        xs = xs + ms
        f2 = (norm_ffn2[i], w_ffn2_gate[i], w_ffn2_up[i], w_ffn2_down[i])
        xp = ffn_half(xp, *f2)
        xs = ffn_half(xs, *f2)
    y_prompt = rmsnorm(xp, norm_final)
    y_sample = rmsnorm(xs, norm_final)
    return (y_prompt, y_sample,
            jnp.stack(ckv_p), jnp.stack(kpe_p), jnp.stack(st_p),
            jnp.stack(ckv_s), jnp.stack(kpe_s), jnp.stack(st_s))


_drawn_inputs = setup_inputs


def setup_inputs(seed=0):
    import zlib

    import numpy as np

    out = dict(_drawn_inputs(seed))
    spreads = {}
    factors = {'norm_ffn1': 6.905,
     'norm_mix': 3.635,
     'q_norm': 8.0,
     'kv_norm': 5.83,
     'ret_gn': 64.0,
     'norm_ffn2': 21.911,
     'norm_final': 31.365}
    for name, (base, spread) in spreads.items():
        noise = np.random.default_rng([zlib.crc32(name.encode()), seed]).standard_normal(out[name].shape)
        drawn = base * np.exp(spread * noise) if base else spread * noise
        out[name] = jnp.asarray(drawn.astype(out[name].dtype))
    for name, factor in factors.items():
        out[name] = (out[name] * factor).astype(out[name].dtype)
    return out
```

```python
import math
from contextlib import ExitStack

import concourse.bass as bass
import numpy as np
from concourse import mybir
from concourse.alu_op_type import AluOpType as ALU

F32 = mybir.dt.float32
F32R = mybir.dt.float32r
ACT = mybir.ActivationFunctionType
AX = mybir.AxisListType
P = 128

D_MODEL, SEQ, DEPTH, DEC_BATCH, DEC_SEQ, PAST_LEN = 1024, 256, 2, 8, 16, 512
CHUNK, QBLK = 64, 128
MLA_HEADS, NOPE, ROPE, Q_LORA, KV_LORA = D_MODEL // 128, 128, 64, 3 * D_MODEL // 8, D_MODEL // 4
MLA_SCALE = (NOPE + ROPE) ** -0.5
RET_HEADS = 4
RET_DK, RET_DV = D_MODEL // RET_HEADS, 2 * D_MODEL // RET_HEADS
FFN_DIM = 256 * ((8 * D_MODEL // 3 + 255) // 256)
EPS = 1e-6
ROPE_THETA = 10000.0

T = SEQ + DEC_BATCH * DEC_SEQ
TT = T // P
KD = D_MODEL // P
KF = FFN_DIM // P
KQ = Q_LORA // P
KV = KV_LORA // P
SLOT = 2 * KD * P
UQ = 2 * (NOPE + ROPE)
HALF = KF // 2

GAINS = [("norm_ffn1", 0), ("norm_mix", 0), ("norm_ffn2", 0), ("norm_ffn1", 1), ("norm_mix", 1), ("norm_ffn2", 1),
         ("norm_final", None), ("q_norm", 0), ("kv_norm", 0), ("ret_gn", 0)]
FINAL_GAIN = 3 * DEPTH * KD
Q_GAIN = FINAL_GAIN + KD
KV_GAIN = Q_GAIN + KQ
RET_GAIN = KV_GAIN + KV
NG = RET_GAIN + RET_HEADS * RET_DV // P
N_NORMS = 3 * DEPTH + 1
STORES = 3 * TT


def stream_kernel(nc, a, out):
    ctx = ExitStack()
    with ctx:
        def sb(name, shape, dt=F32, where=ctx):
            return where.enter_context(nc.sbuf_tensor(name, shape, dt))

        def tile(t, i, n=T):
            flat = t[:, :, :].rearrange("p k n -> p (k n)")
            return flat[:, i * n:(i + 1) * n] if isinstance(i, int) else flat[:, bass.ds(i * n, n)]

        def gain(i):
            return gains[:, i:i + 1] if isinstance(i, int) else gains[:, bass.ds(i, 1)]

        sems = {}

        def sem(name):
            if name not in sems:
                sems[name] = ctx.enter_context(nc.semaphore(name))
            return sems[name]

        X = sb("X", [P, KD, T])
        XH = sb("XH", [P, KD, T], F32R)
        XL = sb("XL", [P, KD, T], F32R)
        RAW = sb("RAW", [P, 2, SLOT])
        WH = sb("WH", [P, 2, SLOT], F32R)
        WL = sb("WL", [P, 2, SLOT], F32R)
        gains = sb("gains", [P, NG])
        ident = sb("ident", [P, P])
        ones = sb("ones", [P, P])
        rsb = sb("rsb", [P, T + TT])
        var = sb("var", [P, T + TT])
        sq = sb("sq", [P, 1, T])
        acc = sb("acc", [P, T])
        upd = sb("upd", [P, T])
        bank = [ctx.enter_context(nc.psum_tensor(f"bank{i}", [P, 512], F32)) for i in range(8)]
        gate_ps, up_ps, down_ps, norm_ps, misc_ps = bank[0:2], bank[2:4], bank[4:6], bank[6], bank[7]

        with ExitStack() as r:
            AH = sb("AH", [P, KF, T], F32R, r)
            AL = sb("AL", [P, KF, T], F32R, r)
            gs = sb("gs", [P, 2, T], F32, r)
            si = sb("si", [P, 2, T], F32, r)
            au = sb("au", [P, 2, T], F32, r)
        with ExitStack() as r:
            xtok = sb("xtok", [P, TT, D_MODEL], F32, r)
            grow = sb("grow", [NG, P], F32, r)
        with ExitStack() as r:
            yf = sb("yf", [P, 2, T], F32, r)
            ytok = sb("ytok", [P, TT, D_MODEL], F32, r)

        raw_in = [sem("raw_in0"), sem("raw_in1")]
        hi_done, lo_done, multiplied = sem("hi_done"), sem("lo_done"), sem("multiplied")

        def load(sp, c, s, pieces):
            if not (isinstance(c, int) and c < 2):
                sp.wait_ge(lo_done, c - 1)
            for (lo, hi), src in pieces:
                dst = RAW[:, s, lo:hi].rearrange("p (k n) -> p k n", n=src.shape[2])
                sp.dma_start(dst, src).then_inc(raw_in[s], 16)

        def cuts(s, width):
            if width != KQ * UQ:
                return [(lambda W: W[:, s, 0:width], RAW[:, s, 0:width])]
            raw = RAW[:, s, 0:width].rearrange("p (c n) -> p c n", n=NOPE + ROPE)
            n = 2 * KQ * NOPE
            return [(lambda W: W[:, s, 0:n].rearrange("p (c n) -> p c n", n=NOPE), raw[:, :, 0:NOPE]),
                    (lambda W: W[:, s, n:width].rearrange("p (c n) -> p c n", n=ROPE), raw[:, :, NOPE:])]

        def split_hi(act, c, s, turn, width):
            act.wait_ge(raw_in[s], 32 * turn + 32)
            if not (isinstance(c, int) and c < 2):
                act.wait_ge(multiplied, c - 1)
            for dst, src in cuts(s, width):
                ins = act.activation(dst(WH), src, ACT.Copy)
            ins.then_inc(hi_done, 1)

        def split_lo(dve, c, s, width):
            dve.wait_ge(hi_done, c + 1)
            for dst, src in cuts(s, width):
                ins = dve.tensor_tensor(dst(WL), src, dst(WH).bitcast(F32), ALU.subtract)
            ins.then_inc(lo_done, 1)

        def product(pe, ps, w, k, xh, xl, first, last):
            wh, wl = w(WH, k), w(WL, k)
            pe.matmul(ps, wh, xh, start=first, stop=False)
            pe.matmul(ps, wh, xl, start=False, stop=False)
            return pe.matmul(ps, wl, xh, start=False, stop=last)

        def norm_tile_act(act, s, m, g, base=0):
            act.wait_ge(sem(f"x_ready{s}"), m + (base + 1))
            act.activation(tile(XH, m), tile(X, m), ACT.Copy, scale=g).then_inc(sem("xh"), 1)

        def norm_tile_dve(dve, s, m, g):
            dve.wait_ge(sem("xh"), m + (KD * s + 1))
            dve.scalar_tensor_tensor(tile(XL, m), tile(X, m), g, tile(XH, m).bitcast(F32),
                                     ALU.mult, ALU.subtract).then_inc(sem("xl"), 1)

        def norm_sums_pool(pool, s, base=0):
            pool.wait_ge(sem(f"x_ready{s}"), base + 1)
            pool.tensor_tensor(acc[:, :], X[:, 0, :], X[:, 0, :], ALU.mult).then_inc(sem("acc"), 1)
            with pool.Fori(1, KD) as m:
                pool.wait_ge(sem(f"x_ready{s}"), m + (base + 1))
                pool.wait_ge(sem("acc"), m + KD * s)
                pool.tensor_tensor(sq[:, 0, :], tile(X, m), tile(X, m), ALU.mult).then_inc(sem("sq"), 1)
                pool.wait_ge(sem("sq"), m + (KD - 1) * s)
                pool.tensor_tensor(acc[:, :], acc[:, :], sq[:, 0, :], ALU.add).then_inc(sem("acc"), 1)

        def norm_sum_pe(pe, s):
            pe.wait_ge(sem("acc"), KD * (s + 1))
            for t in range(TT):
                pe.matmul(norm_ps[:, T + t:T + t + 1], acc[:, t * P:(t + 1) * P], ones[:, 0:1], start=True, stop=True)
            pe.matmul(norm_ps[:, 0:T], ones[:, :], acc[:, :], start=True, stop=True).then_inc(sem("sum_done"), 1)

        def norm_root_dve(dve, s):
            dve.wait_ge(sem("sum_done"), s + 1)
            dve.tensor_scalar(var[:, :], norm_ps[:, 0:T + TT], 1.0 / D_MODEL, EPS, ALU.mult, ALU.add)\
               .then_inc(sem("var_done"), 1)
            dve.wait_ge(sem("var_done"), 2 * s + 1)
            dve.reciprocal(var[:, :], var[:, :]).then_inc(sem("var_done"), 1)

        def norm_root_act(act, s):
            act.wait_ge(sem("var_done"), 2 * s + 2)
            act.activation(rsb[:, :], var[:, :], ACT.Sqrt).then_inc(sem("rs"), 1)

        def start_sp(sp):
            for t in range(TT):
                src = a["x_prompt"][0, t * P:(t + 1) * P, :] if t < SEQ // P else \
                    a["x_sample"].rearrange("b s d -> (b s) d")
                sp.dma_start(xtok[:, t, :], src).then_inc(sem("xtok_in"), 16)
                if t == 0:
                    sp.dma_start(ident[:, :], a["c_ident"]).then_inc(sem("ident_in"), 16)
            row = 0
            for name, li in GAINS:
                src = a[name][li] if li is not None else a[name]
                src = src.rearrange("(k p) -> k p", p=P)
                sp.dma_start(grow[row:row + src.shape[0], :], src).then_inc(sem("gain_in"), 16)
                row += src.shape[0]

        def start_pool(pool):
            pool.memset(ones[:, :], 1.0).then_inc(sem("ones_set"), 1)

        def start_pe(pe):
            pe.wait_ge(sem("ident_in"), 16)
            pe.wait_ge(sem("gain_in"), 16 * len(GAINS))
            pe.transpose(misc_ps[:, 0:NG], grow[:, :], ident[0:NG, 0:NG]).then_inc(sem("gain_turned"), 1)
            pe.wait_ge(sem("xtok_in"), 16 * TT)
            for k in range(KD):
                if k >= 2:
                    pe.wait_ge(sem("x_ready0"), k - 1)
                for t in range(TT):
                    mm = pe.transpose(down_ps[k % 2][:, t * P:(t + 1) * P], xtok[:, t, k * P:(k + 1) * P],
                                      ident[:, :])
                mm.then_inc(sem("x_turned"), 1)

        def start_act(act):
            for c in (0, 1):
                split_hi(act, c, c, 0, SLOT)
            act.wait_ge(sem("gains_set"), 1)
            with act.Fori(0, KD) as m:
                norm_tile_act(act, 0, m, gain(m))
            norm_root_act(act, 0)

        def start_dve(dve):
            dve.wait_ge(sem("gain_turned"), 1)
            dve.tensor_copy(gains[:, :], misc_ps[:, 0:NG]).then_inc(sem("gains_set"), 1)
            for k in range(KD):
                dve.wait_ge(sem("x_turned"), k + 1)
                dve.tensor_copy(X[:, k, :], down_ps[k % 2][:, 0:T]).then_inc(sem("x_ready0"), 1)
            for c in (0, 1):
                split_lo(dve, c, c, SLOT)
            with dve.Fori(0, KD) as m:
                norm_tile_dve(dve, 0, m, gain(m))
            norm_root_dve(dve, 0)

        class Ffn:
            def __init__(self, f, li, which, s, c0, next_widths):
                self.f, self.s, self.c0, self.c1 = f, s, c0, c0 + KF
                self.wg = a[f"w_ffn{which}_gate"][li].rearrange("(k p) n -> p k n", p=P)
                self.wu = a[f"w_ffn{which}_up"][li].rearrange("(k p) n -> p k n", p=P)
                self.wd = a[f"w_ffn{which}_down"][li].rearrange("(k p) n -> p k n", p=P)
                self.next_widths = next_widths
                self.n0, self.m0 = f * KF, f * KD
                self.gate_done, self.scaled = sem("gate_done"), sem("gate_scaled")
                self.silu_done, self.act_done = sem("silu_done"), sem("act_done")
                self.ah_done, self.al_done, self.upd_done = sem("ah_done"), sem("al_done"), sem("upd_done")
                self.x_ready = sem(f"x_ready{s + 1}")

            def slot(self, c):
                return c % 2

            def sp(self, sp):
                def gate_pair(i):
                    for j in (0, 1):
                        c = self.c0 + j + 2 * i
                        cols = bass.ds((2 * i + j) * P, P)
                        load(sp, c, (self.c0 + j) % 2, [((0, KD * P), self.wg[:, :, cols]),
                                                        ((KD * P, 2 * KD * P), self.wu[:, :, cols])])
                first = 0
                if self.c0 == 0:
                    gate_pair(0)
                    first = 1
                with sp.Fori(first, KF // 2) as i:
                    gate_pair(i)
                with sp.Fori(0, KD) as m:
                    for j in (0, 1):
                        c = self.c1 + j + 2 * m
                        k0, k1 = j * HALF, j * HALF + HALF // 2
                        cols = bass.ds(m * P, P)
                        load(sp, c, (self.c1 + j) % 2,
                             [((0, HALF // 2 * P), self.wd[:, k0:k1, cols]),
                              ((HALF // 2 * P, HALF * P), self.wd[:, k1:k0 + HALF, cols])])

            def pe(self, pe):
                def gate_pair(i, first):
                    for j in (0, 1):
                        s = (self.c0 + j) % 2
                        pe.wait_ge(lo_done, self.c0 + j + 2 * i + 1)
                        for part, ps in ((0, gate_ps[j]), (1, up_ps[j])):
                            if not first:
                                pe.wait_ge(self.act_done if part else self.scaled, 2 * i + (self.n0 + j - 1))

                            def w(W, k):
                                at = (part * KD + k) * P
                                return W[:, s, at:at + P]
                            for k in range(KD):
                                if first and j == 0 and part == 0:
                                    pe.wait_ge(sem("xl"), KD * self.s + k + 1)
                                mm = product(pe, ps[:, 0:T], w, k, XH[:, k, :], XL[:, k, :], k == 0, k == KD - 1)
                            mm.then_inc(multiplied if part else self.gate_done, 1)
                            if first and j == 0 and part == 0:
                                norm_sum_pe(pe, self.s)
                gate_pair(0, True)
                with pe.Fori(1, KF // 2) as i:
                    gate_pair(i, False)

                def down_pair(i, first):
                    for mm_ in (0, 1):
                        for j in (0, 1):
                            s = (self.c1 + j) % 2
                            pe.wait_ge(lo_done, self.c1 + j + 2 * mm_ + 4 * i + 1)
                            if j == 0 and not first:
                                pe.wait_ge(self.upd_done, 2 * i + (self.m0 + mm_ - 1))

                            def w(W, k):
                                return W[:, s, k * P:(k + 1) * P]
                            for k in range(HALF):
                                kk = j * HALF + k
                                if first and mm_ == 0:
                                    pe.wait_ge(self.al_done, self.n0 + kk + 1)
                                mm = product(pe, down_ps[mm_][:, 0:T], w, k, AH[:, kk, :], AL[:, kk, :],
                                             kk == 0, kk == KF - 1)
                            mm.then_inc(multiplied, 1)
                down_pair(0, True)
                with pe.Fori(1, KD // 2) as i:
                    down_pair(i, False)

            def act(self, act):
                def gate_pair(i, widths):
                    for j in (0, 1):
                        n = 2 * i + j
                        act.wait_ge(self.scaled, n + (self.n0 + 1))
                        act.activation(si[:, j, :], gs[:, j, :], ACT.Silu).then_inc(self.silu_done, 1)
                        split_hi(act, self.c0 + 2 + j + 2 * i, (self.c0 + j) % 2, (self.c0 + j) // 2 + 1 + i, widths[j])
                        act.wait_ge(self.act_done, n + (self.n0 + 1))
                        act.activation(tile(AH, n), au[:, j, :], ACT.Copy).then_inc(self.ah_done, 1)
                with act.Fori(0, KF // 2 - 1) as i:
                    gate_pair(i, (SLOT, SLOT))
                gate_pair(KF // 2 - 1, (HALF * P, HALF * P))

                def down(m, widths):
                    for j in (0, 1):
                        if widths[j]:
                            split_hi(act, self.c1 + 2 + j + 2 * m, (self.c1 + j) % 2, (self.c1 + j) // 2 + 1 + m, widths[j])
                    if self.s + 1 < N_NORMS - 1:
                        norm_tile_act(act, self.s + 1, m, gain(m + KD * (self.s + 1)))
                with act.Fori(0, KD - 1) as m:
                    down(m, (HALF * P, HALF * P))
                down(KD - 1, self.next_widths)
                norm_root_act(act, self.s + 1)

            def dve(self, dve):
                def gate_pair(i, widths):
                    for j in (0, 1):
                        n, c = 2 * i + j, self.c0 + j + 2 * i
                        dve.wait_ge(self.gate_done, n + (self.n0 + 1))
                        if isinstance(i, int) and i == 0 and j == 0:
                            dve.wait_ge(sem("rs"), self.s + 1)
                        dve.tensor_tensor(gs[:, j, :], gate_ps[j][:, 0:T], rsb[:, 0:T], ALU.mult).then_inc(self.scaled, 1)
                        dve.wait_ge(self.silu_done, n + (self.n0 + 1))
                        dve.wait_ge(multiplied, c + 1)
                        dve.tensor_tensor(au[:, j, :], up_ps[j][:, 0:T], si[:, j, :], ALU.mult).then_inc(self.act_done, 1)
                        split_lo(dve, c + 2, (self.c0 + j) % 2, widths[j])
                        dve.wait_ge(self.ah_done, n + (self.n0 + 1))
                        dve.tensor_tensor(tile(AL, n), au[:, j, :], tile(AH, n).bitcast(F32), ALU.subtract).then_inc(self.al_done, 1)
                dve.wait_ge(sem("rs"), self.s + 1)
                with dve.Fori(0, KF // 2 - 1) as i:
                    gate_pair(i, (SLOT, SLOT))
                gate_pair(KF // 2 - 1, (HALF * P, HALF * P))

                def down(m, widths):
                    c = self.c1 + 2 * m
                    if widths[0]:
                        split_lo(dve, c + 2, self.c1 % 2, widths[0])
                    dve.wait_ge(multiplied, c + 2)
                    return c

                def down_pair(i, widths):
                    for q in (0, 1):
                        m = 2 * i + q
                        c = down(m, widths[q])
                        dve.scalar_tensor_tensor(upd[:, :], down_ps[q][:, 0:T], 0.5, rsb[:, 0:T], ALU.mult, ALU.mult)\
                           .then_inc(self.upd_done, 1)
                        dve.wait_ge(self.upd_done, m + (self.m0 + 1))
                        dve.tensor_tensor(tile(X, m), tile(X, m), upd[:, :], ALU.add).then_inc(self.x_ready, 1)
                        if widths[q][1]:
                            split_lo(dve, c + 3, (self.c1 + 1) % 2, widths[q][1])
                        if self.s + 1 < N_NORMS - 1:
                            norm_tile_dve(dve, self.s + 1, m, gain(m + KD * (self.s + 1)))
                w = (HALF * P, HALF * P)
                with dve.Fori(0, KD // 2 - 1) as i:
                    down_pair(i, (w, w))
                down_pair(KD // 2 - 1, (w, self.next_widths))
                norm_root_dve(dve, self.s + 1)

            def pool(self, pool):
                norm_sums_pool(pool, self.s + 1)

        def end_pe(pe):
            norm_sum_pe(pe, N_NORMS - 1)
            for k in range(KD):
                pe.wait_ge(sem("y_done"), k + 1)
                if k >= 2:
                    pe.wait_ge(sem("y_out"), k - 1)
                for t in range(TT):
                    mm = pe.transpose(gate_ps[k % 2][:, t * P:(t + 1) * P], yf[:, k % 2, t * P:(t + 1) * P], ident[:, :])
                mm.then_inc(sem("y_turned"), 1)

        def end_dve(dve):
            dve.wait_ge(sem("rs"), N_NORMS)
            for k in range(KD):
                if k >= 2:
                    dve.wait_ge(sem("y_turned"), k - 1)
                g = gain(FINAL_GAIN + k)
                dve.scalar_tensor_tensor(yf[:, k % 2, :], X[:, k, :], g, rsb[:, 0:T], ALU.mult, ALU.mult)\
                   .then_inc(sem("y_done"), 1)

        def end_act(act):
            for k in range(KD):
                act.wait_ge(sem("y_turned"), k + 1)
                act.activation(ytok[:, :, k * P:(k + 1) * P],
                               gate_ps[k % 2][:, 0:T].rearrange("p (t n) -> p t n", n=P), ACT.Copy)\
                   .then_inc(sem("y_out"), 1)

        def end_sp(sp):
            sp.wait_ge(sem("y_out"), KD)
            for t in range(TT):
                dst = out["y_prompt"][0, t * P:(t + 1) * P, :] if t < SEQ // P else \
                    out["y_sample"].rearrange("b s d -> (b s) d")
                sp.dma_start(dst, ytok[:, t, :]).then_inc(sem("stored"), 16)

        NP = SEQ // QBLK
        SC = NP * (NP + 1) // 2 * QBLK
        NC = PAST_LEN // P
        HQ = MLA_HEADS * DEC_SEQ
        PAST, NEW = slice(0, PAST_LEN), slice(PAST_LEN, PAST_LEN + P)
        LR = KV_LORA + ROPE
        with ExitStack() as r:
            mtab = sb("mtab", [P, P + 2 * T], F32, r)
            rot, mcos, msin = mtab[:, 0:P], mtab[:, P:P + T], mtab[:, P + T:P + 2 * T]
            mask_q = sb("mask_q", [1, P], F32, r)
            mask_k = sb("mask_k", [1, CHUNK], F32, r)
            qn = sb("qn", [P, MLA_HEADS, T], F32, r)
            qp = sb("qp", [ROPE, MLA_HEADS, T], F32, r)
            ckvT = sb("ckvT", [P, KV, T], F32, r)
            kpT = sb("kpT", [ROPE, T], F32, r)
            tok = sb("tok", [P, TT, LR], F32, r)
            wuk = sb("wuk", [P, KV, D_MODEL], F32, r)
            wuv = sb("wuv", [P, KV, D_MODEL], F32, r)
            wukT = sb("wukT", [P, MLA_HEADS, KV_LORA], F32, r)
            qps = sb("qps", [ROPE, DEC_BATCH, MLA_HEADS, DEC_SEQ], F32, r)
            lat = sb("lat", [P, KV, DEC_BATCH, MLA_HEADS, DEC_SEQ], F32, r)
            with ExitStack() as r1:
                cq = sb("cq", [P, KQ, T], F32, r1)
                cqh = sb("cqh", [P, KQ, T], F32R, r1)
                cql = sb("cql", [P, KQ, T], F32R, r1)
                ckv = sb("ckv", [P, KV, T], F32, r1)
                pe_raw = sb("pe_raw", [P, T], F32, r1)
                pe_cos = sb("pe_cos", [P, T], F32, r1)
                pe_sin = sb("pe_sin", [P, T], F32, r1)
                rq = sb("rq", [P, T], F32, r1)
                rkv = sb("rkv", [P, T], F32, r1)
                acc_q = sb("acc_q", [P, T], F32, r1)
                acc_kv = sb("acc_kv", [P, T], F32, r1)
            with ExitStack() as r2:
                NCB = 4
                cc = sb("cc", [P, NCB, NC, KV_LORA], F32, r2)
                cp = sb("cp", [P, NCB, NC, ROPE], F32, r2)
                stat = sb("stat", [P, 2, 8], F32, r2)
                with ExitStack() as r3:
                    val = sb("val", [P, NP, D_MODEL], F32, r3)
                    kn = sb("kn", [P, 2, SEQ], F32, r3)
                    pr = sb("pr", [P, 2, SC], F32, r3)
                    prT = sb("prT", [P, 2, SC], F32, r3)
                with ExitStack() as r3:
                    kt = sb("kt", [P, 2, KV + 1, PAST_LEN], F32, r3)
                    ps_ = sb("ps_", [P, 2, PAST_LEN + P], F32, r3)
                    psT = sb("psT", [P, 2, PAST_LEN + P], F32, r3)

        class Mla:
            N_CHUNKS = 7 + KD // 2

            def __init__(self, s, c0, next_widths):
                self.s, self.c0 = s, c0
                self.widths = [SLOT] * 3 + [KQ * UQ] * 4 + [SLOT] * (KD // 2) + list(next_widths)

            def look_act(self, act, q):
                c = self.c0 + q + 2
                if self.widths[q + 2]:
                    split_hi(act, c, c % 2, c // 2, self.widths[q + 2])

            def look_dve(self, dve, q):
                if self.widths[q + 2]:
                    split_lo(dve, self.c0 + q + 2, (self.c0 + q) % 2, self.widths[q + 2])

            def sp(self, sp):
                wdq = a["w_dq"][0].rearrange("(k p) n -> p k n", p=P)
                wdkv = a["w_dkv"][0].rearrange("(k p) n -> p k n", p=P)
                wuq = a["w_uq"][0].rearrange("(k p) n -> p k n", p=P)
                wo = a["w_o_mla"][0].rearrange("(k p) n -> p k n", p=P)
                first, second = (0, KD * P), (KD * P, 2 * KD * P)
                c = self.c0
                load(sp, c, c % 2, [(first, wdq[:, :, 0:P]), (second, wdq[:, :, P:2 * P])])
                load(sp, c + 1, (c + 1) % 2, [(first, wdq[:, :, 2 * P:3 * P]), (second, wdkv[:, :, 0:P])])
                sp.wait_ge(multiplied, c)
                sp.dma_start(mtab[:, :], a["c_mla"]).then_inc(sem("mtab_in"), 16)
                load(sp, c + 2, c % 2, [(first, wdkv[:, :, P:2 * P]), (second, wdkv[:, :, LR - P:LR])])
                sp.dma_start(wuk[:, :, :], a["w_uk"][0].rearrange("(k p) h n -> p k (h n)", p=P)).then_inc(sem("wuk_in"), 16)
                sp.dma_start(wuv[:, :, :], a["w_uv"][0].rearrange("(k p) h n -> p k (h n)", p=P)).then_inc(sem("wuv_in"), 16)
                for g in range(4):
                    load(sp, c + 3 + g, (c + 3 + g) % 2, [((0, 2 * UQ), wuq[:, 0:2, g * UQ:(g + 1) * UQ]),
                                                          ((2 * UQ, 3 * UQ), wuq[:, 2:3, g * UQ:(g + 1) * UQ])])
                for g in range(KD // 2):
                    load(sp, c + 7 + g, (c + 7 + g) % 2, [(first, wo[:, :, 2 * g * P:(2 * g + 1) * P]),
                                                          (second, wo[:, :, (2 * g + 1) * P:(2 * g + 2) * P])])
                    if g == 1:
                        self.sp_attention(sp)

            def sp_attention(self, sp):
                sp.wait_ge(multiplied, self.c0 + 7)
                sp.wait_ge(sem("m_rope"), 3 + 3 * 4)
                for b in range(DEC_BATCH):
                    if b == NCB:
                        for t in range(TT):
                            sp.wait_ge(sem("m_tok"), t + 1)
                            for o, n, lo, hi in (("ckv", KV_LORA, 0, KV_LORA), ("kpe", ROPE, KV_LORA, LR)):
                                if t < SEQ // P:
                                    dst = out[f"new_{o}_prompt"][0, 0, t * P:(t + 1) * P, :]
                                else:
                                    dst = out[f"new_{o}_sample"][0].rearrange("b s d -> (b s) d")
                                sp.dma_start(dst, tok[:, t, lo:hi]).then_inc(sem("stored"), 16)
                    if b >= NCB:
                        sp.wait_ge(sem("m_olat"), b - NCB + 1)
                    sp.dma_start(cc[:, b % NCB, :, :],
                                 a["cache_ckv"][0, b].rearrange("(p k) d -> p k d", k=NC)).then_inc(sem(f"cc_in{b % NCB}"), 16)
                    sp.dma_start(cp[:, b % NCB, :, :],
                                 a["cache_kpe"][0, b].rearrange("(p k) d -> p k d", k=NC)).then_inc(sem(f"cc_in{b % NCB}"), 16)

            def pe(self, pe):
                c0 = self.c0

                def projection(q, k_tiles, xh, xl, at, ready, before_last=None):
                    s = (c0 + q) % 2
                    pe.wait_ge(lo_done, c0 + q + 1)
                    banks = (gate_ps[q % 2], up_ps[q % 2])
                    for part, ps in enumerate(banks):
                        if part and before_last:
                            before_last()

                        def w(W, k):
                            return at(W[:, s, :], part, k)
                        for k in range(k_tiles):
                            if ready and part == 0:
                                pe.wait_ge(sem("xl"), KD * self.s + k + 1)
                            mm = product(pe, ps[:, 0:T], w, k, xh[:, k, :], xl[:, k, :], k == 0, k == k_tiles - 1)
                        mm.then_inc(multiplied if part else sem("m_part0"), 1)

                def two(W, part, k):
                    return W[:, (part * KD + k) * P:(part * KD + k + 1) * P]

                projection(0, KD, XH, XL, two, True, lambda: norm_sum_pe(pe, self.s))
                projection(1, KD, XH, XL, two, False)

                def q_sum():
                    pe.wait_ge(sem("m_acc_q"), KQ)
                    pe.matmul(norm_ps[:, 0:T], ones[:, :], acc_q[:, :], start=True, stop=True).then_inc(sem("m_ssq"), 1)
                pe.wait_ge(sem("m_proj"), 2)
                projection(2, KD, XH, XL, two, False, q_sum)

                def rotate(n):
                    pe.wait_ge(sem("m_proj"), 6 + 3 * n)
                    if n == 0:
                        pe.wait_ge(sem("mtab_in"), 16)
                    if n >= 1:
                        pe.wait_ge(sem("m_turn_read"), n)
                    pe.matmul(misc_ps[:, 0:T], rot, pe_raw[:, :], start=True, stop=True).then_inc(sem("m_turned"), 1)

                for g in range(4):
                    q, s = 3 + g, (c0 + 3 + g) % 2
                    pe.wait_ge(lo_done, c0 + q + 1)
                    for part in range(3):
                        ps = (gate_ps, up_ps, down_ps)[part][q % 2]

                        def w(Wt, k):
                            lo = (2 * k + part if part < 2 else 2 * KQ + k) * P
                            return Wt[:, s, lo:lo + P]
                        pe.wait_ge(sem("m_proj"), self.proj_before(g, part))
                        if part == 1:
                            rotate(g)
                        for k in range(KQ):
                            if g == 0 and part == 0:
                                pe.wait_ge(sem("m_cql"), k + 1)
                            mm = product(pe, ps[:, 0:T], w, k, cqh[:, k, :], cql[:, k, :], k == 0, k == KQ - 1)
                        mm.then_inc(multiplied if part == 2 else sem("m_part0"), 1)
                    if g == 0:
                        pe.wait_ge(sem("m_acc_kv"), KV)
                        pe.wait_ge(sem("m_var_q"), 1)
                        pe.matmul(norm_ps[:, 0:T], ones[:, :], acc_kv[:, :], start=True, stop=True).then_inc(sem("m_sskv"), 1)
                rotate(4)
                self.pe_prompt(pe)
                self.pe_sample(pe)

                for g in range(KD // 2):
                    q = 7 + g
                    pe.wait_ge(lo_done, c0 + q + 1)
                    s = (c0 + q) % 2
                    if g >= 2:
                        pe.wait_ge(sem(f"x_ready{self.s + 1}"), 2 * g - 2)
                    for part, ps in enumerate((gate_ps[g % 2], up_ps[g % 2])):
                        def w(W, k):
                            return two(W[:, s, :], part, k)
                        for k in range(KD):
                            if g == 0 and part == 0:
                                pe.wait_ge(sem("m_ol"), MLA_HEADS + k // 4 + 1)
                            mm = product(pe, ps[:, 0:T], w, k, XH[:, k, :], XL[:, k, :], k == 0, k == KD - 1)
                        mm.then_inc(multiplied if part else sem("m_o_part0"), 1)

            def proj_before(self, g, part):
                if g == 0:
                    return (3, 4, 1)[part]
                if g == 1:
                    return (5, 6, 1)[part]
                return 6 + 3 * (g - 2) + part + 1

            def pe_prompt(self, pe):
                pe.wait_ge(sem("wuk_in"), 16)
                pe.wait_ge(sem("wuv_in"), 16)
                pe.wait_ge(sem("m_proj"), 6 + 12)
                for i, ps in enumerate((gate_ps[0], gate_ps[1], up_ps[0], up_ps[1])):
                    for e in range(2):
                        for t in range(KV):
                            h = 2 * i + e
                            mm = pe.transpose(ps[:, (e * KV + t) * P:(e * KV + t + 1) * P],
                                              wuk[:, t, h * P:(h + 1) * P], ident[:, :])
                    mm.then_inc(sem("m_wukT"), 1)
                pe.wait_ge(sem("m_ckvT"), KV)
                pe.wait_ge(sem("m_rope"), 3 + 3 * 4)
                for i, ps in enumerate((down_ps[0], down_ps[1], norm_ps, misc_ps)):
                    kt_, half = i // 2, i % 2
                    for t in range(KV):
                        mm = pe.matmul(ps[:, 0:512], ckvT[:, t, kt_ * P:(kt_ + 1) * P],
                                       wuv[:, t, half * 512:(half + 1) * 512], start=(t == 0), stop=(t == KV - 1))
                    mm.then_inc(sem("m_val"), 1)
                for t in range(TT):
                    ps = down_ps[t % 2]
                    pe.wait_ge(sem("m_val_out"), t + 1 if t < 2 else 2)
                    if t == 2:
                        pe.wait_ge(sem("m_tok"), 1)
                    for k in range(KV):
                        pe.transpose(ps[:, k * P:(k + 1) * P], ckvT[:, k, t * P:(t + 1) * P], ident[:, :])
                    pe.transpose(ps[:, KV_LORA:LR], kpT[:, t * P:(t + 1) * P], ident[0:ROPE, 0:ROPE]).then_inc(sem("m_tok_turned"), 1)

                def keys(h):
                    if h == 0:
                        pe.wait_ge(sem("m_wukT_out"), 4)
                    if h >= 2:
                        pe.wait_ge(sem("m_kn"), h - 1)
                    for t in range(KV):
                        mm = pe.matmul(gate_ps[h % 2][:, 0:SEQ], wuk[:, t, h * P:(h + 1) * P], ckvT[:, t, 0:SEQ],
                                       start=(t == 0), stop=(t == KV - 1))
                    mm.then_inc(sem("m_keys"), 1)

                def scores(h):
                    pe.wait_ge(sem("m_kn"), h + 1)
                    if h == 0:
                        pe.wait_ge(sem("m_mask"), 3)
                    if h >= 2:
                        pe.wait_ge(sem("m_exp"), 2 * (h - 1))
                    ps = up_ps[h % 2]
                    at = 0
                    for blk in range(NP):
                        n, q0 = (blk + 1) * QBLK, blk * QBLK
                        pe.matmul(ps[:, at:at + n], qn[:, h, q0:q0 + QBLK], kn[:, h % 2, 0:n], start=True, stop=False)
                        pe.matmul(ps[:, at + n - CHUNK:at + n], mask_q[:, :], mask_k[:, :], start=False, stop=False,
                                  skip_group_check=True)
                        mm = pe.matmul(ps[:, at:at + n], qp[:, h, q0:q0 + QBLK], kpT[:, 0:n], start=False, stop=True)
                        at += n
                    mm.then_inc(sem("m_scores"), 1)

                def turn(h):
                    pe.wait_ge(sem("m_pr"), 2 * (h + 1))
                    if h < 2:
                        pe.wait_ge(sem("m_tok"), TT)
                    if h >= 2:
                        pe.wait_ge(sem("m_prT"), h - 1)
                    for i in range(SC // P):
                        mm = pe.transpose(down_ps[h % 2][:, i * P:(i + 1) * P], pr[:, h % 2, i * P:(i + 1) * P], ident[:, :])
                    mm.then_inc(sem("m_prTurned"), 1)

                def mix(h):
                    ps = (norm_ps, misc_ps)[h % 2]
                    pe.wait_ge(sem("m_prT"), h + 1)
                    if h < 2:
                        pe.wait_ge(sem("m_val_out"), 4)
                    if h >= 2:
                        pe.wait_ge(sem("m_ol"), h - 1)
                    at = 0
                    for blk in range(NP):
                        for k in range(blk + 1):
                            mm = pe.matmul(ps[:, blk * QBLK:(blk + 1) * QBLK], val[:, k, h * P:(h + 1) * P],
                                           prT[:, h % 2, at:at + P], start=(k == 0), stop=(k == blk))
                            at += P
                    mm.then_inc(sem("m_mixed"), 1)

                for i in range(MLA_HEADS + 3):
                    if i < MLA_HEADS:
                        keys(i)
                    if 0 <= i - 3:
                        mix(i - 3)
                    if 0 <= i - 1 < MLA_HEADS:
                        scores(i - 1)
                    if 0 <= i - 2 < MLA_HEADS:
                        turn(i - 2)

            def pe_sample(self, pe):
                for i in range(4):
                    ps = (gate_ps[0], gate_ps[1], up_ps[0], up_ps[1])[i]
                    pe.wait_ge(sem("m_exp"), 2 * MLA_HEADS)
                    for t in range(KV):
                        for e in range(2):
                            h = 2 * i + e
                            mm = pe.matmul(ps[:, (t * 2 + e) * P:(t * 2 + e + 1) * P], wukT[:, h, t * P:(t + 1) * P],
                                           qn[:, h, SEQ:T], start=True, stop=True)
                    mm.then_inc(sem("m_qlat"), 1)

                def turn_cache(b):
                    pe.wait_ge(sem(f"cc_in{b % NCB}"), 32 * (b // NCB + 1))
                    if b == 0:
                        pe.wait_ge(sem("m_lat"), 4 * KV)
                    if b >= 1:
                        pe.wait_ge(sem("m_kt_act"), 2 * b)
                        pe.wait_ge(sem("m_kt_dve"), b)
                    for t, ps in enumerate((gate_ps[0], gate_ps[1], up_ps[0])):
                        for k in range(NC):
                            if t < KV:
                                mm = pe.transpose(ps[:, k * P:(k + 1) * P], cc[:, b % NCB, k, t * P:(t + 1) * P], ident[:, :])
                            else:
                                mm = pe.transpose(ps[0:ROPE, k * P:(k + 1) * P], cp[:, b % NCB, k, :], ident[:, :])
                        mm.then_inc(sem("m_cturned"), 1)

                def scores(b):
                    pe.wait_ge(sem("m_kt_act"), 2 * (b + 1))
                    pe.wait_ge(sem("m_kt_dve"), b + 1)
                    if b == 0:
                        pe.wait_ge(sem("m_qps"), 1)
                        pe.wait_ge(sem("m_prT"), MLA_HEADS)
                    if b >= 1:
                        pe.wait_ge(sem("m_sexp"), 2 * b)
                    new = slice(SEQ + b * DEC_SEQ, SEQ + (b + 1) * DEC_SEQ)
                    for ps, n, ks in ((up_ps[1], PAST_LEN, [kt[:, b % 2, 0, :], kt[:, b % 2, 1, :], kt[0:ROPE, b % 2, 2, :]]),
                                      (down_ps[0], DEC_SEQ, [ckvT[:, 0, new], ckvT[:, 1, new], kpT[:, new]])):
                        qs = [x.rearrange("p h q -> p (h q)") for x in (lat[:, 0, b, :, :], lat[:, 1, b, :, :], qps[:, b, :, :])]
                        for i in range(3):
                            mm = pe.matmul(ps[:, 0:n], qs[i], ks[i], start=(i == 0), stop=(i == 2))
                    mm.then_inc(sem("m_sscores"), 1)

                def turn(b):
                    pe.wait_ge(sem("m_ps"), b + 1)
                    if b == 0:
                        pe.wait_ge(sem("m_ol"), MLA_HEADS)
                    if b >= 1:
                        pe.wait_ge(sem("m_psT"), 2 * b)
                    for k in range(NC + 1):
                        ps = down_ps[1][:, k * P:(k + 1) * P] if k < NC else norm_ps[:, 0:P]
                        mm = pe.transpose(ps, ps_[:, b % 2, k * P:(k + 1) * P], ident[:, :])
                    mm.then_inc(sem("m_psTurned"), 1)

                def mix(b):
                    pe.wait_ge(sem("m_psT"), 2 * (b + 1))
                    if b >= 1:
                        pe.wait_ge(sem("m_olat"), b)
                    for t in range(KV):
                        for k in range(NC + 1):
                            lhs = cc[:, b % NCB, k, t * P:(t + 1) * P] if k < NC else tok[:, TT - 1, t * P:(t + 1) * P]
                            mm = pe.matmul(misc_ps[:, t * P:(t + 1) * P], lhs, psT[:, b % 2, k * P:(k + 1) * P],
                                           start=(k == 0), stop=(k == NC))
                    mm.then_inc(sem("m_smixed"), 1)

                for i in range(DEC_BATCH + 3):
                    if i < DEC_BATCH:
                        turn_cache(i)
                    if 0 <= i - 3:
                        mix(i - 3)
                    if 0 <= i - 1 < DEC_BATCH:
                        scores(i - 1)
                    if 0 <= i - 2 < DEC_BATCH:
                        turn(i - 2)
                pe.wait_ge(sem("m_olat"), DEC_BATCH)
                for i, ps in enumerate(down_ps):
                    for e in range(4):
                        h = 4 * i + e
                        for t in range(KV):
                            mm = pe.matmul(ps[:, e * P:(e + 1) * P], wuv[:, t, h * P:(h + 1) * P], lat[:, t, :, h, :],
                                           start=(t == 0), stop=(t == KV - 1))
                    mm.then_inc(sem("m_vout"), 1)

            def act(self, act):
                for q in range(3):
                    self.look_act(act, q)
                    for t in ((0, 1), (2,), ())[q]:
                        act.wait_ge(sem("m_proj"), t + 1)
                        act.activation(cqh[:, t, :], cq[:, t, :], ACT.Copy, scale=gain(Q_GAIN + t)).then_inc(sem("m_cqh"), 1)
                act.wait_ge(sem("m_var_q"), 2)
                act.activation(rq[:, :], var[:, 0:T], ACT.Sqrt).then_inc(sem("m_rq"), 1)
                self.look_act(act, 3)
                act.wait_ge(sem("m_var_kv"), 2)
                act.activation(rkv[:, :], var[:, 0:T], ACT.Sqrt).then_inc(sem("m_rkv"), 1)
                for q in range(4, 7):
                    self.look_act(act, q)
                for i, ps in enumerate((gate_ps[0], gate_ps[1], up_ps[0], up_ps[1])):
                    act.wait_ge(sem("m_wukT"), i + 1)
                    act.activation(wukT[:, 2 * i:2 * i + 2, :].rearrange("p h n -> p (h n)"), ps[:, :], ACT.Copy).then_inc(sem("m_wukT_out"), 1)
                for i, ps in enumerate((down_ps[0], down_ps[1], norm_ps, misc_ps)):
                    act.wait_ge(sem("m_val"), i + 1)
                    act.activation(val[:, i // 2, (i % 2) * 512:(i % 2 + 1) * 512], ps[:, :], ACT.Copy).then_inc(sem("m_val_out"), 1)
                for t in range(TT):
                    act.wait_ge(sem("m_tok_turned"), t + 1)
                    act.activation(tok[:, t, :], down_ps[t % 2][:, 0:LR], ACT.Copy).then_inc(sem("m_tok"), 1)

                for i in range(MLA_HEADS + 3):
                    if i < MLA_HEADS:
                        act.wait_ge(sem("m_keys"), i + 1)
                        if i >= 2:
                            act.wait_ge(sem("m_scores"), i - 1)
                        act.activation(kn[:, i % 2, :], gate_ps[i % 2][:, 0:SEQ], ACT.Copy).then_inc(sem("m_kn"), 1)
                    h = i - 3
                    if h >= 0:
                        act.wait_ge(sem("m_mixed"), h + 1)
                        act.activation(XH[:, h, 0:SEQ], (norm_ps, misc_ps)[h % 2][:, 0:SEQ], ACT.Copy).then_inc(sem("m_oh"), 1)
                    h = i - 1
                    if 0 <= h < MLA_HEADS:
                        act.wait_ge(sem("m_negmax"), h + 1)
                        if h >= 2:
                            act.wait_ge(sem("m_prTurned"), h - 1)
                        at = 0
                        for blk in range(NP):
                            n = (blk + 1) * QBLK
                            act.activation(pr[:, h % 2, at:at + n], up_ps[h % 2][:, at:at + n], ACT.Exp,
                                           bias=stat[:, h % 2, 2 + blk:3 + blk], scale=MLA_SCALE,
                                           accum_out=stat[:, h % 2, 4 + blk:5 + blk]).then_inc(sem("m_exp"), 1)
                            at += n
                    h = i - 2
                    if 0 <= h < MLA_HEADS:
                        act.wait_ge(sem("m_prTurned"), h + 1)
                        if h >= 2:
                            act.wait_ge(sem("m_mixed"), h - 1)
                        act.activation(prT[:, h % 2, :], down_ps[h % 2][:, 0:SC], ACT.Copy).then_inc(sem("m_prT"), 1)

                for i, ps in enumerate((gate_ps[0], gate_ps[1], up_ps[0], up_ps[1])):
                    act.wait_ge(sem("m_qlat"), i + 1)
                    for t in range(KV):
                        act.activation(lat[:, t, :, 2 * i:2 * i + 2, :].rearrange("p b e q -> p e b q"),
                                       ps[:, t * 2 * P:(t + 1) * 2 * P].rearrange("p (e b q) -> p e b q", e=2, b=DEC_BATCH),
                                       ACT.Copy).then_inc(sem("m_lat"), 1)
                for i in range(DEC_BATCH + 3):
                    b = i
                    if b < DEC_BATCH:
                        for t in range(KV):
                            act.wait_ge(sem("m_cturned"), 3 * b + t + 1)
                            if b >= 2:
                                act.wait_ge(sem("m_sscores"), b - 1)
                            act.activation(kt[:, b % 2, t, :], gate_ps[t][:, :], ACT.Copy).then_inc(sem("m_kt_act"), 1)
                    b = i - 1
                    if 0 <= b < DEC_BATCH:
                        act.wait_ge(sem("m_snegmax"), b + 1)
                        act.wait_ge(sem("m_zero"), b + 1)
                        act.activation(ps_[:, b % 2, PAST], up_ps[1][:, :], ACT.Exp, bias=stat[:, b % 2, 2:3], scale=MLA_SCALE,
                                       accum_out=stat[:, b % 2, 4:5]).then_inc(sem("m_sexp"), 1)
                        at = PAST_LEN + b * DEC_SEQ
                        act.activation(ps_[:, b % 2, at:at + DEC_SEQ], down_ps[0][:, 0:DEC_SEQ], ACT.Exp,
                                       bias=stat[:, b % 2, 2:3], scale=MLA_SCALE,
                                       accum_out=stat[:, b % 2, 5:6]).then_inc(sem("m_sexp"), 1)
                    b = i - 2
                    if 0 <= b < DEC_BATCH:
                        act.wait_ge(sem("m_psTurned"), b + 1)
                        if b >= 2:
                            act.wait_ge(sem("m_smixed"), b - 1)
                        act.activation(psT[:, b % 2, PAST], down_ps[1][:, :], ACT.Copy).then_inc(sem("m_psT"), 1)
                        act.activation(psT[:, b % 2, NEW], norm_ps[:, 0:P], ACT.Copy).then_inc(sem("m_psT"), 1)
                for i in range(2):
                    act.wait_ge(sem("m_vout"), i + 1)
                    act.activation(XH[:, 4 * i:4 * i + 4, SEQ:T], down_ps[i][:, :].rearrange("p (h n) -> p h n", h=4),
                                   ACT.Copy).then_inc(sem("m_oh"), 1)
                for q in range(7, 7 + KD // 2):
                    self.look_act(act, q)
                act.wait_ge(sem("stored"), 16 * 2 * TT)
                act.wait_ge(multiplied, self.c0 + self.N_CHUNKS)
                for m in range(KD):
                    norm_tile_act(act, self.s + 1, m, gain(KD * (self.s + 1) + m))
                norm_root_act(act, self.s + 1)

            def dve(self, dve):
                c0 = self.c0
                dve.wait_ge(sem("rs"), self.s + 1)
                targets = [cq[:, 0, :], cq[:, 1, :], cq[:, 2, :], ckv[:, 0, :], ckv[:, 1, :], pe_raw[:, :]]
                for q in range(3):
                    for part in range(2):
                        t = 2 * q + part
                        dve.wait_ge(*((multiplied, c0 + q + 1) if part else (sem("m_part0"), q + 1)))
                        dve.tensor_tensor(targets[t], (gate_ps, up_ps)[part][q % 2][:, 0:T], rsb[:, 0:T], ALU.mult)\
                           .then_inc(sem("m_proj"), 1)
                    self.look_dve(dve, q)
                    for t in ((0, 1), (2,), ())[q]:
                        dve.wait_ge(sem("m_cqh"), t + 1)
                        dve.scalar_tensor_tensor(cql[:, t, :], cq[:, t, :], gain(Q_GAIN + t), cqh[:, t, :].bitcast(F32),
                                                 ALU.mult, ALU.subtract).then_inc(sem("m_cql"), 1)

                def root(ss, name, n):
                    dve.wait_ge(sem(ss), 1)
                    dve.tensor_scalar(var[:, 0:T], norm_ps[:, 0:T], 1.0 / n, EPS, ALU.mult, ALU.add).then_inc(sem(name), 1)
                    dve.wait_ge(sem(name), 1)
                    dve.reciprocal(var[:, 0:T], var[:, 0:T]).then_inc(sem(name), 1)

                def rope(n, outs):
                    if n == 0:
                        dve.wait_ge(sem("mtab_in"), 16)
                    dve.wait_ge(sem("m_proj"), 6 + 3 * n)
                    dve.wait_ge(sem("m_turned"), n + 1)
                    dve.tensor_tensor(pe_sin[:, :], misc_ps[:, 0:T], msin, ALU.mult).then_inc(sem("m_turn_read"), 1)
                    dve.tensor_tensor(pe_cos[:, :], pe_raw[:, :], mcos, ALU.mult).then_inc(sem("m_rope"), 1)
                    dve.wait_ge(sem("m_turn_read"), n + 1)
                    dve.wait_ge(sem("m_rope"), 3 * n + 1)
                    for lo, dst in outs:
                        ins = dve.tensor_tensor(dst, pe_cos[lo:lo + ROPE, :], pe_sin[lo:lo + ROPE, :], ALU.add)
                        ins.then_inc(sem("m_rope"), 1 if len(outs) == 2 else 2)
                root("m_ssq", "m_var_q", Q_LORA)
                rope(0, [(ROPE, kpT[:, :])])
                dve.wait_ge(sem("m_rq"), 1)
                for g in range(4):
                    q = 3 + g
                    for part in range(3):
                        dve.wait_ge(*((multiplied, c0 + q + 1) if part == 2 else (sem("m_part0"), 3 + 2 * g + part + 1)))
                        dst = qn[:, 2 * g + part, :] if part < 2 else pe_raw[:, :]
                        dve.tensor_tensor(dst, (gate_ps, up_ps, down_ps)[part][q % 2][:, 0:T], rq[:, :], ALU.mult)\
                           .then_inc(sem("m_proj"), 1)
                    self.look_dve(dve, q)
                    if g == 0:
                        root("m_sskv", "m_var_kv", KV_LORA)
                        dve.wait_ge(sem("m_rkv"), 1)
                        for t in range(KV):
                            dve.scalar_tensor_tensor(ckvT[:, t, :], ckv[:, t, :], gain(KV_GAIN + t), rkv[:, :],
                                                     ALU.mult, ALU.mult).then_inc(sem("m_ckvT"), 1)
                    rope(g + 1, [(0, qp[:, 2 * g, :]), (ROPE, qp[:, 2 * g + 1, :])])

                for i in range(MLA_HEADS + 3):
                    h = i - 3
                    if h >= 0:
                        dve.wait_ge(sem("m_oh"), h + 1)
                        dve.tensor_tensor(XL[:, h, 0:SEQ], (norm_ps, misc_ps)[h % 2][:, 0:SEQ], XH[:, h, 0:SEQ].bitcast(F32),
                                          ALU.subtract).then_inc(sem("m_ol"), 1)
                    h = i - 1
                    if 0 <= h < MLA_HEADS:
                        dve.wait_ge(sem("m_scores"), h + 1)
                        at = 0
                        for blk in range(NP):
                            n = (blk + 1) * QBLK
                            dve.tensor_reduce(stat[:, h % 2, blk:blk + 1], up_ps[h % 2][:, at:at + n], AX.X, ALU.max)\
                               .then_inc(sem("m_max"), 1)
                            at += n
                        dve.wait_ge(sem("m_max"), 2 * (h + 1))
                        dve.tensor_scalar(stat[:, h % 2, 2:4], stat[:, h % 2, 0:2], -MLA_SCALE, None, ALU.mult)\
                           .then_inc(sem("m_negmax"), 1)
                        dve.wait_ge(sem("m_exp"), 2 * (h + 1))
                        dve.reciprocal(stat[:, h % 2, 6:8], stat[:, h % 2, 4:6]).then_inc(sem("m_inv"), 1)
                        dve.wait_ge(sem("m_inv"), h + 1)
                        at = 0
                        for blk in range(NP):
                            n = (blk + 1) * QBLK
                            dve.tensor_scalar(pr[:, h % 2, at:at + n], pr[:, h % 2, at:at + n], stat[:, h % 2, 6 + blk:7 + blk],
                                              None, ALU.mult).then_inc(sem("m_pr"), 1)
                            at += n

                for i in range(DEC_BATCH + 3):
                    b = i
                    if b < DEC_BATCH:
                        dve.wait_ge(sem("m_cturned"), 3 * b + 3)
                        if b >= 2:
                            dve.wait_ge(sem("m_sscores"), b - 1)
                        dve.tensor_copy(kt[0:ROPE, b % 2, KV, :], up_ps[0][0:ROPE, :]).then_inc(sem("m_kt_dve"), 1)
                    b = i - 3
                    if b >= 0:
                        dve.wait_ge(sem("m_smixed"), b + 1)
                        dve.tensor_copy(lat[:, :, b, :, :].rearrange("p t h q -> p t (h q)"),
                                        misc_ps[:, 0:KV * P].rearrange("p (t n) -> p t n", t=KV))\
                           .then_inc(sem("m_olat"), 1)
                    b = i - 1
                    if 0 <= b < DEC_BATCH:
                        st = stat[:, b % 2, :]
                        dve.wait_ge(sem("m_sscores"), b + 1)
                        dve.tensor_reduce(st[:, 0:1], up_ps[1][:, :], AX.X, ALU.max).then_inc(sem("m_smax"), 1)
                        dve.tensor_reduce(st[:, 1:2], down_ps[0][:, 0:DEC_SEQ], AX.X, ALU.max).then_inc(sem("m_smax"), 1)
                        dve.wait_ge(sem("m_smax"), 3 * b + 2)
                        dve.tensor_tensor(st[:, 3:4], st[:, 0:1], st[:, 1:2], ALU.max).then_inc(sem("m_smax"), 1)
                        dve.wait_ge(sem("m_smax"), 3 * b + 3)
                        dve.tensor_scalar(st[:, 2:3], st[:, 3:4], -MLA_SCALE, None, ALU.mult).then_inc(sem("m_snegmax"), 1)
                        dve.wait_ge(sem("m_sexp"), 2 * (b + 1))
                        dve.tensor_tensor(st[:, 6:7], st[:, 4:5], st[:, 5:6], ALU.add).then_inc(sem("m_sinv"), 1)
                        dve.wait_ge(sem("m_sinv"), 2 * b + 1)
                        dve.reciprocal(st[:, 7:8], st[:, 6:7]).then_inc(sem("m_sinv"), 1)
                        dve.wait_ge(sem("m_sinv"), 2 * b + 2)
                        dve.tensor_scalar(ps_[:, b % 2, :], ps_[:, b % 2, :], st[:, 7:8], None, ALU.mult).then_inc(sem("m_ps"), 1)
                for i in range(2):
                    dve.wait_ge(sem("m_oh"), MLA_HEADS + i + 1)
                    dve.tensor_tensor(XL[:, 4 * i:4 * i + 4, SEQ:T], down_ps[i][:, :].rearrange("p (h n) -> p h n", h=4),
                                      XH[:, 4 * i:4 * i + 4, SEQ:T].bitcast(F32), ALU.subtract).then_inc(sem("m_ol"), 1)

                for g in range(KD // 2):
                    for part in range(2):
                        m = 2 * g + part
                        dve.wait_ge(*((multiplied, c0 + 7 + g + 1) if part else (sem("m_o_part0"), g + 1)))
                        dve.tensor_tensor(X[:, m, :], X[:, m, :], (gate_ps, up_ps)[part][g % 2][:, 0:T], ALU.add)\
                           .then_inc(sem(f"x_ready{self.s + 1}"), 1)
                    self.look_dve(dve, 7 + g)
                dve.wait_ge(sem("stored"), 16 * 2 * TT)
                for m in range(KD):
                    norm_tile_dve(dve, self.s + 1, m, gain(KD * (self.s + 1) + m))
                norm_root_dve(dve, self.s + 1)

            def pool(self, pool):
                pool.wait_ge(multiplied, self.c0)
                pool.memset(mask_q[:, :], 0.0).then_inc(sem("m_mask"), 1)
                pool.memset(mask_k[:, :], -1e30).then_inc(sem("m_mask"), 1)
                pool.wait_ge(sem("m_mask"), 2)
                pool.memset(mask_q[:, 0:CHUNK], 1.0).then_inc(sem("m_mask"), 1)
                for name, src, n, total, ready in (("q", cq, KQ, acc_q, 0), ("kv", ckv, KV, acc_kv, KQ)):
                    for t in range(n):
                        pool.wait_ge(sem("m_proj"), ready + t + 1)
                        if t:
                            pool.wait_ge(sem(f"m_acc_{name}"), t)
                        dst = sq[:, 0, :] if t else total[:, :]
                        pool.tensor_tensor(dst, src[:, t, :], src[:, t, :], ALU.mult)\
                            .then_inc(sem(f"m_sq_{name}" if t else f"m_acc_{name}"), 1)
                        if t:
                            pool.wait_ge(sem(f"m_sq_{name}"), t)
                            pool.tensor_tensor(total[:, :], total[:, :], sq[:, 0, :], ALU.add).then_inc(sem(f"m_acc_{name}"), 1)
                pool.wait_ge(sem("m_rope"), 3 + 3 * 4)
                pool.tensor_copy(qps[:, :, :, :], qp[:, :, SEQ:T].rearrange("p h (b q) -> p b h q", b=DEC_BATCH))\
                    .then_inc(sem("m_qps"), 1)
                for b in range(DEC_BATCH):
                    if b == 0:
                        pool.wait_ge(sem("m_prT"), MLA_HEADS)
                        pool.wait_ge(sem("m_ol"), MLA_HEADS)
                    if b >= 2:
                        pool.wait_ge(sem("m_psTurned"), b - 1)
                    pool.memset(ps_[:, b % 2, NEW], 0.0).then_inc(sem("m_zero"), 1)
                norm_sums_pool(pool, self.s + 1)

        HV, E, D = RET_DV, RET_DV // P, RET_DK // P
        ST_SLOTS = 4
        HC = 4 * P + P + 8
        DECAY, XI, ZETA = slice(0, 4 * P), slice(4 * P, 5 * P), 5 * P
        G16 = ZETA + 4
        with ExitStack() as r:
            rtab = sb("rtab", [P, 2, T], F32, r)
            rturn = sb("rturn", [P, 2, T], F32, r)
            hc = sb("hc", [P, HC], F32, r)
            rot4 = sb("rot4", [P, 4, T], F32, r)
            qT = sb("qT", [P, D, T], F32, r)
            kT = sb("kT", [P, D, T], F32, r)
            kz = sb("kz", [P, 4, RET_DK], F32, r)
            vt = sb("vt", [P, TT, HV], F32, r)
            gt = sb("gt", [P, 2, T], F32, r)
            sg = sb("sg", [P, E, T], F32, r)
            at_ = sb("at_", [P, 4 * P], F32, r)
            qz = sb("qz", [P, D, DEC_BATCH * (P + DEC_SEQ)], F32, r)
            st = sb("st", [P, ST_SLOTS, D, HV], F32, r)
            ns = sb("ns", [P, 2, D, HV], F32, r)
            nsp = sb("nsp", [P, D, HV], F32, r)
            on = sb("on", [P, TT, HV], F32, r)
            rst = sb("rst", [P, 3, 4], F32, r)
            zf = sb("zf", [P, 2, T], F32, r)
            zh = sb("zh", [P, E, T], F32R, r)
            zl = sb("zl", [P, E, T], F32R, r)

        class Retention:
            PER = 8
            STORES = (16 * (DEC_BATCH // 2 + 1), 16 * (DEC_BATCH // 2))

            def __init__(self, s, c0):
                self.s, self.c0 = s, c0
                self.stored = (sem("r_stored0"), sem("r_stored1"))
                self.x_base = 1 + KD * (RET_HEADS - 1)

            def look_act(self, act, h, q):
                c, s = self.c0 + q + 2, (self.c0 + q) % 2
                split_hi(act, c + self.PER * h, s, c // 2 + self.PER // 2 * h, SLOT)

            def look_dve(self, dve, h, q):
                split_lo(dve, self.c0 + q + 2 + self.PER * h, (self.c0 + q) % 2, SLOT)

            def sp(self, sp):
                win = a["w_ret_in"][0].rearrange("(k p) n -> p k n", p=P)
                wout = a["w_ret_out"][0].rearrange("(k p) n -> p k n", p=P)
                first, second = (0, KD * P), (KD * P, 2 * KD * P)
                k0, v0 = RET_HEADS * RET_DK, 2 * RET_HEADS * RET_DK
                g0 = v0 + RET_HEADS * HV

                def chunk(h, q, pieces):
                    load(sp, self.c0 + q + self.PER * h, (self.c0 + q) % 2, pieces)

                def tiles(col):
                    return [(first, win[:, :, bass.ds(col, P)]), (second, win[:, :, bass.ds(col + P, P)])]

                def head_of(x, h):
                    return x.rearrange("h (d p) e -> p (h d) e", p=P)[:, bass.ds(h * D, D), :]

                def state(src, b):
                    sp.dma_start(st[:, b % ST_SLOTS, :, :], src).then_inc(sem(f"r_st_in{b % ST_SLOTS}"), 16)

                with sp.Fori(0, RET_HEADS) as h:
                    chunk(h, 0, tiles(h * RET_DK))
                    chunk(h, 1, tiles(h * RET_DK + k0))
                    tables = a["c_ret"][:, bass.ds(h * HC, HC)]
                    old = [head_of(a["state_ret"][0, b], h) for b in range(DEC_BATCH)]
                    sp.wait_ge(self.x_done, KD * h + 1)
                    sp.dma_start(hc[:, :], tables).then_inc(sem("r_hc_in"), 16)
                    for b in range(ST_SLOTS):
                        state(old[b], b)
                    for j in range(2):
                        w = win[:, :, bass.ds(h * HV + (v0 + j * 2 * P), 2 * P)]
                        chunk(h, 2 + j, [(first, w[:, 0:KD // 2, :]), (second, w[:, KD // 2:KD, :])])
                    for j in range(2):
                        chunk(h, 4 + j, tiles(h * HV + (g0 + j * 2 * P)))
                    for j in range(2):
                        w = wout[:, :, j * 4 * P:(j + 1) * 4 * P]
                        chunk(h, 6 + j, [(first, w[:, bass.ds(h * E, E // 2), :]), (second, w[:, bass.ds(h * E + E // 2, E // 2), :])])
                    dst = head_of(out["new_state_prompt"][0, 0], h)
                    new = [head_of(out["new_state_sample"][0, b], h) for b in range(DEC_BATCH)]
                    sp.wait_ge(sem("r_ns"), 18 * h + 2)
                    sp.dma_start(dst, nsp[:, :, :]).then_inc(self.stored[0], 16)
                    for b in range(DEC_BATCH):
                        sp.wait_ge(sem("r_ns"), 18 * h + (2 + 2 * (b + 1)))
                        sp.dma_start(new[b], ns[:, b % 2, :, :]).then_inc(self.stored[b % 2], 16)
                        if b + ST_SLOTS < DEC_BATCH:
                            state(old[b + ST_SLOTS], b + ST_SLOTS)

            @property
            def x_done(self):
                return sem(f"x_ready{self.s + 1}")

            def sp_start(self, sp):
                sp.wait_ge(multiplied, self.c0)
                for i in range(2):
                    sp.dma_start(rtab[:, i, :], a["c_rtab"][:, i * T:(i + 1) * T]).then_inc(self.stored[i], 16)

            def sp_end(self, sp):
                for i in range(2):
                    sp.wait_ge(self.stored[i], self.STORES[i] * RET_HEADS + 16)

            def pe(self, pe):
                pe.wait_ge(sem("xl"), KD * (self.s + 1))
                norm_sum_pe(pe, self.s)
                with pe.Fori(0, RET_HEADS) as h:
                    self.pe_head(pe, h)

            def pe_head(self, pe, h):
                c = self.c0 + self.PER * h

                def slot(q):
                    return (self.c0 + q) % 2

                def columns(q, banks, free=None):
                    pe.wait_ge(lo_done, c + (q + 1))
                    if free:
                        pe.wait_ge(*free)
                    for part, ps in enumerate(banks):
                        for k in range(KD):
                            mm = product(pe, ps[:, 0:T], lambda W, k: W[:, slot(q), (part * KD + k) * P:(part * KD + k + 1) * P],
                                         k, XH[:, k, :], XL[:, k, :], k == 0, k == KD - 1)
                        mm.then_inc(multiplied if part else sem("r_part"), 1)

                def values(q, banks, free=None):
                    pe.wait_ge(lo_done, c + (q + 1))
                    if free:
                        pe.wait_ge(*free)
                    for t, ps in enumerate(banks):
                        for k in range(KD):
                            wh, wl = WH[:, slot(q), k * 2 * P:(k + 1) * 2 * P], WL[:, slot(q), k * 2 * P:(k + 1) * 2 * P]
                            xh, xl = XH[:, k, t * P:(t + 1) * P], XL[:, k, t * P:(t + 1) * P]
                            pe.matmul(ps[:, 0:2 * P], xh, wh, start=(k == 0), stop=False)
                            pe.matmul(ps[:, 0:2 * P], xh, wl, start=False, stop=False)
                            mm = pe.matmul(ps[:, 0:2 * P], xl, wh, start=False, stop=(k == KD - 1))
                        mm.then_inc(multiplied if t == TT - 1 else sem("r_part"), 1)

                pe.wait_ge(self.x_done, KD * h + 1)
                columns(0, (gate_ps[0], up_ps[0]))
                columns(1, (gate_ps[1], up_ps[1]))
                values(2, (down_ps[0], down_ps[1], norm_ps))
                values(3, (gate_ps[0], up_ps[0], misc_ps), (sem("r_rot"), 8 * h + 4))
                columns(4, (gate_ps[1], up_ps[1]), (sem("r_rot"), 8 * h + 8))
                columns(5, (down_ps[0], down_ps[1]), (sem("r_v"), 6 * h + 3))

                pe.wait_ge(sem("r_T"), 4 * h + 4)
                pe.wait_ge(sem("r_v"), 6 * h + 6)
                for t in range(TT):
                    ps = (norm_ps, norm_ps, misc_ps)[t]
                    for d in range(D):
                        at = (t % 2 * D + d) * P
                        mm = pe.transpose(ps[:, at:at + P], kT[:, d, t * P:(t + 1) * P], ident[:, :])
                mm.then_inc(sem("r_k_turned"), 1)
                for at, ks, qs in ((0, slice(0, P), slice(0, SEQ)), (2 * P, slice(P, SEQ), slice(P, SEQ)),
                                   (3 * P, slice(SEQ, T), slice(SEQ, T))):
                    n = qs.stop - qs.start
                    for d in range(D):
                        mm = pe.matmul(gate_ps[0][:, at:at + n], kT[:, d, ks], qT[:, d, qs], start=(d == 0), stop=(d == D - 1))
                mm.then_inc(sem("r_scores"), 1)
                pe.wait_ge(sem("r_at"), h + 1)
                pe.matmul(up_ps[0][:, :], at_[:, 0:P], vt[:, 0, :], start=True, stop=True)
                pe.wait_ge(sem("r_gt"), 4 * h + 4)
                pe.matmul(gate_ps[1][:, :], at_[:, P:2 * P], vt[:, 0, :], start=True, stop=False)
                pe.matmul(gate_ps[1][:, :], at_[:, 2 * P:3 * P], vt[:, 1, :], start=False, stop=True).then_inc(sem("r_o"), 1)
                ring = (norm_ps, misc_ps, down_ps[0])
                pe.wait_ge(sem("r_kz"), 4 * h + 4)
                for d in range(D):
                    for t in range(2):
                        mm = pe.matmul(ring[d][:, :], kz[:, t, d * P:(d + 1) * P], vt[:, t, :], start=(t == 0), stop=(t == 1))
                    mm.then_inc(sem("r_new"), 1)
                so = down_ps[1]
                pe.matmul(so[:, :], at_[:, 3 * P:4 * P], vt[:, 2, :], start=True, stop=False)
                pe.wait_ge(sem("r_qz"), 2 * h + 2)
                for b in range(DEC_BATCH):
                    pe.wait_ge(sem(f"r_st_in{b % ST_SLOTS}"), 16 * (DEC_BATCH // ST_SLOTS) * h + 16 * (b // ST_SLOTS + 1))
                    for d in range(D):
                        mm = pe.matmul(so[:, :], qz[:, d, b * P:(b + 1) * P], st[:, b % ST_SLOTS, d, :], start=False,
                                       stop=(b == DEC_BATCH - 1 and d == D - 1))
                    if b == DEC_BATCH - 1:
                        mm.then_inc(sem("r_o"), 1)
                    rows = slice(b // 2 * 2 * DEC_SEQ, (b // 2 + 1) * 2 * DEC_SEQ)
                    for d in range(D):
                        j = 2 + 2 * b + d
                        if j >= 3:
                            pe.wait_ge(sem("r_ns"), 18 * h + (j - 2))
                        pe.matmul(ring[j % 3][:, :], kz[rows, 2 + b % 2, d * P:(d + 1) * P], vt[rows, 2, :],
                                  start=True, stop=True).then_inc(sem("r_new"), 1)
                    if b == DEC_BATCH // 2:
                        self.pe_turn(pe, h, (0, 1))
                self.pe_turn(pe, h, (2,))

                for q in (6, 7):
                    pe.wait_ge(lo_done, c + (q + 1))
                    banks = (norm_ps, misc_ps, down_ps[0], down_ps[1]) if q == 6 else (gate_ps[0], up_ps[0], gate_ps[1], up_ps[1])
                    if q == 6:
                        pe.wait_ge(sem("r_ns"), 18 * h + 18)
                    for m, ps in enumerate(banks):
                        for k in range(E):
                            if q == 6 and m == 0:
                                pe.wait_ge(sem("r_zl"), E * h + (k + 1))
                            mm = product(pe, ps[:, 0:T], lambda W, k: W[:, slot(q), (4 * k + m) * P:(4 * k + m + 1) * P],
                                         k, zh[:, k, :], zl[:, k, :], k == 0, k == E - 1)
                        mm.then_inc(multiplied if m == 3 else sem("r_out"), 1)

            def pe_turn(self, pe, h, ts):
                pe.wait_ge(sem("r_on"), 3 * h + (ts[-1] + 1))
                for e, ps in enumerate((gate_ps[0], up_ps[0], gate_ps[1], up_ps[1])):
                    for t in ts:
                        mm = pe.transpose(ps[:, t * P:(t + 1) * P], on[:, t, e * P:(e + 1) * P], ident[:, :])
                    if ts[-1] == TT - 1:
                        mm.then_inc(sem("r_o_turned"), 1)

            def act(self, act):
                with act.Fori(0, RET_HEADS) as h:
                    self.act_head(act, h)
                for m in range(KD):
                    norm_tile_act(act, self.s + 1, m, gain(KD * (self.s + 1) + m), self.x_base)
                norm_root_act(act, self.s + 1)

            def act_head(self, act, h):
                c = self.c0 + self.PER * h
                self.look_act(act, h, 0)
                self.look_act(act, h, 1)
                for j in range(2):
                    for t, ps in enumerate((down_ps[0], down_ps[1], norm_ps) if j == 0 else (gate_ps[0], up_ps[0], misc_ps)):
                        if t < TT - 1:
                            act.wait_ge(sem("r_part"), 8 * h + (2 + 2 * j + t + 1))
                        else:
                            act.wait_ge(multiplied, c + (2 + j + 1))
                        act.activation(vt[:, t, j * 2 * P:(j + 1) * 2 * P], ps[:, 0:2 * P], ACT.Copy,
                                       scale=rsb[:, T + t:T + t + 1]).then_inc(sem("r_v"), 1)
                    self.look_act(act, h, 2 + j)
                for e in range(E):
                    act.wait_ge(sem("r_gt"), E * h + (e + 1))
                    act.activation(sg[:, e, :], gt[:, e % 2, :], ACT.Silu).then_inc(sem("r_sg"), 1)
                    if e % 2:
                        self.look_act(act, h, 4 + e // 2)
                act.wait_ge(sem("r_hc_in"), 16 * h + 16)
                act.wait_ge(sem("r_k_turned"), h + 1)
                for i, src in enumerate((norm_ps[:, 0:RET_DK], norm_ps[:, RET_DK:2 * RET_DK], misc_ps[:, 0:RET_DK], misc_ps[:, 0:RET_DK])):
                    act.activation(kz[:, i, :], src, ACT.Copy, scale=hc[:, ZETA + i:ZETA + i + 1]).then_inc(sem("r_kz"), 1)

                def normalise(ts, o, v):
                    banks = (up_ps[0], gate_ps[1], down_ps[1])
                    act.wait_ge(sem("r_o"), 2 * h + o)
                    for t in ts:
                        act.activation(on[:, t, :], banks[t][:, :], ACT.Square, accum_out=rst[:, 0, t:t + 1]).then_inc(sem("r_sq"), 1)
                    act.wait_ge(sem("r_var"), 4 * h + v)
                    act.activation(rst[:, 2, ts[0]:ts[-1] + 1], rst[:, 1, ts[0]:ts[-1] + 1], ACT.Sqrt).then_inc(sem("r_root"), 1)
                    act.wait_ge(sem("r_root"), 2 * h + o)
                    for t in ts:
                        act.activation(on[:, t, :], banks[t][:, :], ACT.Copy, scale=rst[:, 2, t:t + 1]).then_inc(sem("r_on"), 1)
                normalise((0, 1), 1, 2)
                normalise((2,), 2, 4)
                for e in range(E):
                    act.wait_ge(sem("r_z"), E * h + (e + 1))
                    act.activation(zh[:, e, :], zf[:, e % 2, :], ACT.Copy).then_inc(sem("r_zh"), 1)
                self.look_act(act, h, 6)
                self.look_act(act, h, 7)

            def dve(self, dve):
                dve.wait_ge(sem("rs"), self.s + 1)
                for i in range(2):
                    dve.wait_ge(self.stored[i], 16)
                    ins = dve.tensor_tensor(rturn[:, i, :], rtab[:, i, :], rsb[:, 0:T], ALU.mult)
                    ins.then_inc(sem("r_rturn"), 1)
                dve.wait_ge(sem("r_rturn"), 2)
                dve.tensor_copy(rst[:, 2, 3:4], ones[:, 0:1]).then_inc(self.x_done, 1)
                with dve.Fori(0, RET_HEADS) as h:
                    self.dve_head(dve, h)
                for m in range(KD):
                    norm_tile_dve(dve, self.s + 1, m, gain(KD * (self.s + 1) + m))
                norm_root_dve(dve, self.s + 1)

            def dve_head(self, dve, h):
                c = self.c0 + self.PER * h
                cos, sin = rturn[:, 0, :], rturn[:, 1, :]
                for i in range(2):
                    dve.wait_ge(sem("r_part"), 8 * h + (i + 1))
                    if i:
                        dve.wait_ge(sem("r_T"), 4 * h + 2)
                    dve.tensor_tensor(rot4[:, 0, :], gate_ps[i][:, 0:T], cos, ALU.mult).then_inc(sem("r_rot"), 1)
                    dve.tensor_tensor(rot4[:, 1, :], gate_ps[i][:, 0:T], sin, ALU.mult).then_inc(sem("r_rot"), 1)
                    dve.wait_ge(multiplied, c + (i + 1))
                    dve.tensor_tensor(rot4[:, 2, :], up_ps[i][:, 0:T], sin, ALU.mult).then_inc(sem("r_rot"), 1)
                    dve.tensor_tensor(rot4[:, 3, :], up_ps[i][:, 0:T], cos, ALU.mult).then_inc(sem("r_rot"), 1)
                    self.look_dve(dve, h, i)
                self.look_dve(dve, h, 2)
                self.look_dve(dve, h, 3)
                for e in range(E):
                    if e % 2:
                        dve.wait_ge(multiplied, c + (4 + e // 2 + 1))
                    else:
                        dve.wait_ge(sem("r_part"), 8 * h + (6 + e // 2 + 1))
                    if e >= 2:
                        dve.wait_ge(sem("r_sg"), E * h + (e - 1))
                    ps = (gate_ps[1], up_ps[1], down_ps[0], down_ps[1])[e]
                    dve.tensor_tensor(gt[:, e % 2, :], ps[:, 0:T], rsb[:, 0:T], ALU.mult).then_inc(sem("r_gt"), 1)
                    if e % 2:
                        self.look_dve(dve, h, 4 + e // 2)
                dve.wait_ge(sem("r_hc_in"), 16 * h + 16)
                dve.wait_ge(sem("r_scores"), h + 1)
                dve.tensor_tensor(at_[:, :], gate_ps[0][:, :], hc[:, DECAY], ALU.mult).then_inc(sem("r_at"), 1)

                def variance(t0, t1, v):
                    dve.wait_ge(sem("r_sq"), 3 * h + t1)
                    dve.tensor_scalar(rst[:, 1, t0:t1], rst[:, 0, t0:t1], 1.0 / HV, EPS, ALU.mult, ALU.add).then_inc(sem("r_var"), 1)
                    dve.wait_ge(sem("r_var"), 4 * h + v)
                    dve.reciprocal(rst[:, 1, t0:t1], rst[:, 1, t0:t1]).then_inc(sem("r_var"), 1)
                variance(0, 2, 1)
                ring = (norm_ps, misc_ps, down_ps[0])
                for j in range(18):
                    dve.wait_ge(sem("r_new"), 18 * h + (j + 1))
                    if j < 2:
                        if j == 0:
                            dve.wait_ge(self.stored[0], self.STORES[0] * h + 16)
                        dve.tensor_copy(nsp[:, j, :], ring[j][:, :]).then_inc(sem("r_ns"), 1)
                        continue
                    b, d = j // 2 - 1, j % 2
                    if b >= 1 and d == 0:
                        dve.wait_ge(self.stored[b % 2], self.STORES[b % 2] * h + 16 * (b // 2 + (2, 1)[b % 2]))
                    dve.scalar_tensor_tensor(ns[:, b % 2, d, :], st[:, b % ST_SLOTS, d, :], hc[:, G16:G16 + 1], ring[j % 3][:, :],
                                             ALU.mult, ALU.add).then_inc(sem("r_ns"), 1)
                variance(2, 3, 3)
                for e in range(E):
                    dve.wait_ge(sem("r_o_turned"), E * h + (e + 1))
                    if e >= 2:
                        dve.wait_ge(sem("r_zl"), E * h + (e - 1))
                    ps = (gate_ps[0], up_ps[0], gate_ps[1], up_ps[1])[e]
                    dve.scalar_tensor_tensor(zf[:, e % 2, :], ps[:, 0:T], gains[:, bass.ds(E * h + (RET_GAIN + e), 1)], sg[:, e, :],
                                             ALU.mult, ALU.mult).then_inc(sem("r_z"), 1)
                    if e >= 1:
                        self.dve_zl(dve, h, e - 1)
                self.dve_zl(dve, h, E - 1)
                for q in (6, 7):
                    banks = (norm_ps, misc_ps, down_ps[0], down_ps[1]) if q == 6 else (gate_ps[0], up_ps[0], gate_ps[1], up_ps[1])
                    for m, ps in enumerate(banks):
                        if m < 3:
                            dve.wait_ge(sem("r_out"), 6 * h + (3 * (q - 6) + m + 1))
                        else:
                            dve.wait_ge(multiplied, c + (q + 1))
                        mm = 4 * (q - 6) + m
                        dve.tensor_tensor(X[:, mm, :], X[:, mm, :], ps[:, 0:T], ALU.add).then_inc(self.x_done, 1)
                    self.look_dve(dve, h, q)

            def dve_zl(self, dve, h, e):
                dve.wait_ge(sem("r_zh"), E * h + (e + 1))
                dve.tensor_tensor(zl[:, e, :], zf[:, e % 2, :], zh[:, e, :].bitcast(F32), ALU.subtract).then_inc(sem("r_zl"), 1)

            def pool(self, pool):
                pool.wait_ge(multiplied, self.c0)
                pool.memset(qz[:, :, :], 0.0).then_inc(sem("r_zero"), 1)
                pool.wait_ge(sem("r_zero"), 1)
                with pool.Fori(0, RET_HEADS) as h:
                    for i, dst in enumerate((qT, kT)):
                        pool.wait_ge(sem("r_rot"), 8 * h + (4 * i + 4))
                        pool.tensor_tensor(dst[:, 0, :], rot4[:, 0, :], rot4[:, 2, :], ALU.subtract).then_inc(sem("r_T"), 1)
                        pool.tensor_tensor(dst[:, 1, :], rot4[:, 1, :], rot4[:, 3, :], ALU.add).then_inc(sem("r_T"), 1)
                        if i == 0:
                            pool.wait_ge(sem("r_hc_in"), 16 * h + 16)
                            pool.wait_ge(sem("r_T"), 4 * h + 2)
                            for d in range(D):
                                pool.tensor_tensor(qz[:, d, :].rearrange("p (b n) -> p b n", n=P + DEC_SEQ)[:, :, 0:DEC_SEQ],
                                                   qT[:, d, SEQ:T].rearrange("p (b n) -> p b n", n=DEC_SEQ),
                                                   hc[:, XI].rearrange("p (b n) -> p b n", n=DEC_SEQ), ALU.mult)\
                                    .then_inc(sem("r_qz"), 1)
                norm_sums_pool(pool, self.s + 1, self.x_base)

        C = 2 * KD + KF
        c_mla, c_ret = C, 3 * C + Mla.N_CHUNKS
        c_last = c_ret + Retention.PER * RET_HEADS
        whole, half = (SLOT, SLOT), (0, 0)
        phases = [Ffn(0, 0, 1, 0, 0, whole), Mla(1, c_mla, whole), Ffn(1, 0, 2, 2, c_mla + Mla.N_CHUNKS, whole),
                  Ffn(2, 1, 1, 3, c_mla + Mla.N_CHUNKS + C, whole), Retention(4, c_ret), Ffn(3, 1, 2, 5, c_last, half)]

        block = ctx.enter_context(nc.Block())

        @block.sync
        def _(sp):
            start_sp(sp)
            for ph in phases:
                if isinstance(ph, Retention):
                    ph.sp_start(sp)
                ph.sp(sp)
            end_sp(sp)
            for ph in phases:
                if isinstance(ph, Retention):
                    ph.sp_end(sp)
            sp.wait_ge(sem("stored"), 16 * STORES)

        @block.gpsimd
        def _(pool):
            start_pool(pool)
            norm_sums_pool(pool, 0)
            for ph in phases:
                ph.pool(pool)

        @block.scalar
        def _(act):
            start_act(act)
            for ph in phases:
                ph.act(act)
            end_act(act)

        @block.vector
        def _(dve):
            start_dve(dve)
            for ph in phases:
                ph.dve(dve)
            end_dve(dve)

        @block.tensor
        def _(pe):
            start_pe(pe)
            for ph in phases:
                ph.pe(pe)
            end_pe(pe)


def constants():
    f = np.float32
    pos = np.concatenate([np.arange(SEQ), np.tile(PAST_LEN + np.arange(DEC_SEQ), DEC_BATCH)]).astype(f)

    def angles(d):
        inv = f(1.0) / (f(ROPE_THETA) ** (np.arange(0, d, 2, dtype=f) / f(d)))
        ang = (inv[:, None] * pos[None, :]).astype(f).astype(np.float64)
        return np.cos(ang).astype(f), np.sin(ang).astype(f)

    turn, half = np.zeros((P, P), f), ROPE // 2
    for base in range(0, P, ROPE):
        for i in range(half):
            turn[base + half + i, base + i] = -1.0
            turn[base + i, base + half + i] = 1.0
    cos, sin = angles(ROPE)
    mla = np.concatenate([turn, np.tile(cos, (4, 1)), np.tile(sin, (4, 1))], axis=1)
    lg = np.log(f(1.0) - f(2.0) ** (-5.0 - np.arange(RET_HEADS, dtype=f))).astype(f).astype(np.float64)
    scale = RET_DK ** -0.5
    p, i = np.arange(P)[:, None], np.arange(SEQ)[None, :]
    s, j = p % DEC_SEQ, np.arange(P)[None, :]
    heads = []
    for g in lg:
        prompt = np.where(i >= p, np.exp(g * np.maximum(i - p, 0)), 0.0) * scale
        mine = (p // DEC_SEQ == j // DEC_SEQ) & (j % DEC_SEQ >= s)
        sample = np.where(mine, np.exp(g * np.maximum(j % DEC_SEQ - s, 0)), 0.0) * scale
        xi = np.broadcast_to(np.exp(g * (j % DEC_SEQ + 1)), (P, P))
        z = np.exp(g * (DEC_SEQ - 1 - s)) * scale
        even = p // DEC_SEQ % 2 == 0
        zeta = [np.exp(g * (SEQ - 1 - p)) * scale, np.exp(g * (SEQ - 1 - P - p)) * scale, z * even, z * ~even,
                np.full((P, 1), np.exp(g * DEC_SEQ)), np.zeros((P, 3))]
        heads.append(np.concatenate([prompt, prompt[:, 0:P], sample, xi] + zeta, axis=1))
    return {"c_ident": np.eye(P, dtype=f), "c_mla": mla, "c_rtab": np.concatenate(angles(RET_DK), axis=1),
            "c_ret": np.concatenate(heads, axis=1).astype(f)}


INPUTS = ["x_prompt", "x_sample", "cache_ckv", "cache_kpe", "state_ret", "norm_ffn1", "w_ffn1_gate", "w_ffn1_up",
          "w_ffn1_down", "norm_mix", "w_dq", "q_norm", "w_uq", "w_dkv", "kv_norm", "w_uk", "w_uv", "w_o_mla",
          "w_ret_in", "ret_gn", "w_ret_out", "norm_ffn2", "w_ffn2_gate", "w_ffn2_up", "w_ffn2_down", "norm_final"]
OUTPUTS = [("y_prompt", (1, SEQ, D_MODEL)), ("y_sample", (DEC_BATCH, DEC_SEQ, D_MODEL)),
           ("new_ckv_prompt", (1, 1, SEQ, KV_LORA)), ("new_kpe_prompt", (1, 1, SEQ, ROPE)),
           ("new_state_prompt", (1, 1, RET_HEADS, RET_DK, RET_DV)),
           ("new_ckv_sample", (1, DEC_BATCH, DEC_SEQ, KV_LORA)), ("new_kpe_sample", (1, DEC_BATCH, DEC_SEQ, ROPE)),
           ("new_state_sample", (1, DEC_BATCH, RET_HEADS, RET_DK, RET_DV))]


def kernel(**inputs):
    import concourse.bacc as bacc
    from concourse.bass_utils import run_bass_kernel_spmd

    nc = bacc.Bacc("TRN2", target_bir_lowering=False, num_devices=1)
    arrays = {f"{n}_dram": np.ascontiguousarray(inputs[n]) for n in INPUTS}
    arrays.update({f"{n}_dram": x for n, x in constants().items()})
    a = {n[:-5]: nc.dram_tensor(n, x.shape, mybir.dt.from_np(x.dtype), kind="ExternalInput").ap()
         for n, x in arrays.items()}
    out = {n: nc.dram_tensor(f"{n}_dram", shape, F32, kind="ExternalOutput").ap() for n, shape in OUTPUTS}
    stream_kernel(nc, a, out)
    r = run_bass_kernel_spmd(nc, [arrays], core_ids=[0]).results[0]
    return tuple(r[f"{n}_dram"] for n, _ in OUTPUTS)
```

```python
import math
from contextlib import ExitStack

import concourse.bass as bass
import numpy as np
from concourse import mybir
from concourse.alu_op_type import AluOpType as ALU

F32 = mybir.dt.float32
F32R = mybir.dt.float32r
ACT = mybir.ActivationFunctionType
AX = mybir.AxisListType
P = 128

D_MODEL, SEQ, DEPTH, DEC_BATCH, DEC_SEQ, PAST_LEN = 1024, 256, 2, 8, 16, 512
CHUNK, QBLK = 64, 128
MLA_HEADS, NOPE, ROPE, Q_LORA, KV_LORA = D_MODEL // 128, 128, 64, 3 * D_MODEL // 8, D_MODEL // 4
MLA_SCALE = (NOPE + ROPE) ** -0.5
RET_HEADS = 4
RET_DK, RET_DV = D_MODEL // RET_HEADS, 2 * D_MODEL // RET_HEADS
FFN_DIM = 256 * ((8 * D_MODEL // 3 + 255) // 256)
EPS = 1e-6
ROPE_THETA = 10000.0

T = SEQ + DEC_BATCH * DEC_SEQ
TT = T // P
KD = D_MODEL // P
KF = FFN_DIM // P
KQ = Q_LORA // P
KV = KV_LORA // P
SLOT = 2 * KD * P
UQ = 2 * (NOPE + ROPE)
HALF = KF // 2

GAINS = [("norm_ffn1", 0), ("norm_mix", 0), ("norm_ffn2", 0), ("norm_ffn1", 1), ("norm_mix", 1), ("norm_ffn2", 1),
         ("norm_final", None), ("q_norm", 0), ("kv_norm", 0), ("ret_gn", 0)]
FINAL_GAIN = 3 * DEPTH * KD
Q_GAIN = FINAL_GAIN + KD
KV_GAIN = Q_GAIN + KQ
RET_GAIN = KV_GAIN + KV
NG = RET_GAIN + RET_HEADS * RET_DV // P
N_NORMS = 3 * DEPTH + 1
STORES = 3 * TT


def stream_kernel(nc, a, out):
    ctx = ExitStack()
    with ctx:
        def sb(name, shape, dt=F32, where=ctx):
            return where.enter_context(nc.sbuf_tensor(name, shape, dt))

        def tile(t, i, n=T):
            flat = t[:, :, :].rearrange("p k n -> p (k n)")
            return flat[:, i * n:(i + 1) * n] if isinstance(i, int) else flat[:, bass.ds(i * n, n)]

        def gain(i):
            return gains[:, i:i + 1] if isinstance(i, int) else gains[:, bass.ds(i, 1)]

        sems = {}

        def sem(name):
            if name not in sems:
                sems[name] = ctx.enter_context(nc.semaphore(name))
            return sems[name]

        X = sb("X", [P, KD, T])
        XH = sb("XH", [P, KD, T], F32R)
        XL = sb("XL", [P, KD, T], F32R)
        RAW = sb("RAW", [P, 2, SLOT])
        WH = sb("WH", [P, 2, SLOT], F32R)
        WL = sb("WL", [P, 2, SLOT], F32R)
        gains = sb("gains", [P, NG])
        ident = sb("ident", [P, P])
        ones = sb("ones", [P, P])
        rsb = sb("rsb", [P, T + TT])
        var = sb("var", [P, T + TT])
        sq = sb("sq", [P, 1, T])
        acc = sb("acc", [P, T])
        upd = sb("upd", [P, T])
        bank = [ctx.enter_context(nc.psum_tensor(f"bank{i}", [P, 512], F32)) for i in range(8)]
        gate_ps, up_ps, down_ps, norm_ps, misc_ps = bank[0:2], bank[2:4], bank[4:6], bank[6], bank[7]

        with ExitStack() as r:
            AH = sb("AH", [P, KF, T], F32R, r)
            AL = sb("AL", [P, KF, T], F32R, r)
            gs = sb("gs", [P, 2, T], F32, r)
            si = sb("si", [P, 2, T], F32, r)
            au = sb("au", [P, 2, T], F32, r)
        with ExitStack() as r:
            xtok = sb("xtok", [P, TT, D_MODEL], F32, r)
            grow = sb("grow", [NG, P], F32, r)
        with ExitStack() as r:
            yf = sb("yf", [P, 2, T], F32, r)
            ytok = sb("ytok", [P, TT, D_MODEL], F32, r)

        raw_in = [sem("raw_in0"), sem("raw_in1")]
        hi_done, lo_done, multiplied = sem("hi_done"), sem("lo_done"), sem("multiplied")

        def load(sp, c, s, pieces):
            if not (isinstance(c, int) and c < 2):
                sp.wait_ge(lo_done, c - 1)
            for (lo, hi), src in pieces:
                dst = RAW[:, s, lo:hi].rearrange("p (k n) -> p k n", n=src.shape[2])
                sp.dma_start(dst, src).then_inc(raw_in[s], 16)

        def cuts(s, width):
            if width != KQ * UQ:
                return [(lambda W: W[:, s, 0:width], RAW[:, s, 0:width])]
            raw = RAW[:, s, 0:width].rearrange("p (c n) -> p c n", n=NOPE + ROPE)
            n = 2 * KQ * NOPE
            return [(lambda W: W[:, s, 0:n].rearrange("p (c n) -> p c n", n=NOPE), raw[:, :, 0:NOPE]),
                    (lambda W: W[:, s, n:width].rearrange("p (c n) -> p c n", n=ROPE), raw[:, :, NOPE:])]

        def split_hi(act, c, s, turn, width):
            act.wait_ge(raw_in[s], 32 * turn + 32)
            if not (isinstance(c, int) and c < 2):
                act.wait_ge(multiplied, c - 1)
            for dst, src in cuts(s, width):
                ins = act.activation(dst(WH), src, ACT.Copy)
            ins.then_inc(hi_done, 1)

        def split_lo(dve, c, s, width):
            dve.wait_ge(hi_done, c + 1)
            for dst, src in cuts(s, width):
                ins = dve.tensor_tensor(dst(WL), src, dst(WH).bitcast(F32), ALU.subtract)
            ins.then_inc(lo_done, 1)

        def product(pe, ps, w, k, xh, xl, first, last):
            wh, wl = w(WH, k), w(WL, k)
            pe.matmul(ps, wh, xh, start=first, stop=False)
            pe.matmul(ps, wh, xl, start=False, stop=False)
            return pe.matmul(ps, wl, xh, start=False, stop=last)

        def norm_tile_act(act, s, m, g, base=0):
            act.wait_ge(sem(f"x_ready{s}"), m + (base + 1))
            act.activation(tile(XH, m), tile(X, m), ACT.Copy, scale=g).then_inc(sem("xh"), 1)

        def norm_tile_dve(dve, s, m, g):
            dve.wait_ge(sem("xh"), m + (KD * s + 1))
            dve.scalar_tensor_tensor(tile(XL, m), tile(X, m), g, tile(XH, m).bitcast(F32),
                                     ALU.mult, ALU.subtract).then_inc(sem("xl"), 1)

        def norm_sums_pool(pool, s, base=0):
            pool.wait_ge(sem(f"x_ready{s}"), base + 1)
            pool.tensor_tensor(acc[:, :], X[:, 0, :], X[:, 0, :], ALU.mult).then_inc(sem("acc"), 1)
            with pool.Fori(1, KD) as m:
                pool.wait_ge(sem(f"x_ready{s}"), m + (base + 1))
                pool.wait_ge(sem("acc"), m + KD * s)
                pool.tensor_tensor(sq[:, 0, :], tile(X, m), tile(X, m), ALU.mult).then_inc(sem("sq"), 1)
                pool.wait_ge(sem("sq"), m + (KD - 1) * s)
                pool.tensor_tensor(acc[:, :], acc[:, :], sq[:, 0, :], ALU.add).then_inc(sem("acc"), 1)

        def norm_sum_pe(pe, s):
            pe.wait_ge(sem("acc"), KD * (s + 1))
            for t in range(TT):
                pe.matmul(norm_ps[:, T + t:T + t + 1], acc[:, t * P:(t + 1) * P], ones[:, 0:1], start=True, stop=True)
            pe.matmul(norm_ps[:, 0:T], ones[:, :], acc[:, :], start=True, stop=True).then_inc(sem("sum_done"), 1)

        def norm_root_dve(dve, s):
            dve.wait_ge(sem("sum_done"), s + 1)
            dve.tensor_scalar(var[:, :], norm_ps[:, 0:T + TT], 1.0 / D_MODEL, EPS, ALU.mult, ALU.add)\
               .then_inc(sem("var_done"), 1)
            dve.wait_ge(sem("var_done"), 2 * s + 1)
            dve.reciprocal(var[:, :], var[:, :]).then_inc(sem("var_done"), 1)

        def norm_root_act(act, s):
            act.wait_ge(sem("var_done"), 2 * s + 2)
            act.activation(rsb[:, :], var[:, :], ACT.Sqrt).then_inc(sem("rs"), 1)

        def start_sp(sp):
            for t in range(TT):
                src = a["x_prompt"][0, t * P:(t + 1) * P, :] if t < SEQ // P else \
                    a["x_sample"].rearrange("b s d -> (b s) d")
                sp.dma_start(xtok[:, t, :], src).then_inc(sem("xtok_in"), 16)
                if t == 0:
                    sp.dma_start(ident[:, :], a["c_ident"]).then_inc(sem("ident_in"), 16)
            row = 0
            for name, li in GAINS:
                src = a[name][li] if li is not None else a[name]
                src = src.rearrange("(k p) -> k p", p=P)
                sp.dma_start(grow[row:row + src.shape[0], :], src).then_inc(sem("gain_in"), 16)
                row += src.shape[0]

        def start_pool(pool):
            pool.memset(ones[:, :], 1.0).then_inc(sem("ones_set"), 1)

        def start_pe(pe):
            pe.wait_ge(sem("ident_in"), 16)
            pe.wait_ge(sem("gain_in"), 16 * len(GAINS))
            pe.transpose(misc_ps[:, 0:NG], grow[:, :], ident[0:NG, 0:NG]).then_inc(sem("gain_turned"), 1)
            pe.wait_ge(sem("xtok_in"), 16 * TT)
            for k in range(KD):
                if k >= 2:
                    pe.wait_ge(sem("x_ready0"), k - 1)
                for t in range(TT):
                    mm = pe.transpose(down_ps[k % 2][:, t * P:(t + 1) * P], xtok[:, t, k * P:(k + 1) * P],
                                      ident[:, :])
                mm.then_inc(sem("x_turned"), 1)

        def start_act(act):
            for c in (0, 1):
                split_hi(act, c, c, 0, SLOT)
            act.wait_ge(sem("gains_set"), 1)
            with act.Fori(0, KD) as m:
                norm_tile_act(act, 0, m, gain(m))
            norm_root_act(act, 0)

        def start_dve(dve):
            dve.wait_ge(sem("gain_turned"), 1)
            dve.tensor_copy(gains[:, :], misc_ps[:, 0:NG]).then_inc(sem("gains_set"), 1)
            for k in range(KD):
                dve.wait_ge(sem("x_turned"), k + 1)
                dve.tensor_copy(X[:, k, :], down_ps[k % 2][:, 0:T]).then_inc(sem("x_ready0"), 1)
            for c in (0, 1):
                split_lo(dve, c, c, SLOT)
            with dve.Fori(0, KD) as m:
                norm_tile_dve(dve, 0, m, gain(m))
            norm_root_dve(dve, 0)

        class Ffn:
            def __init__(self, f, li, which, s, c0, next_widths):
                self.f, self.s, self.c0, self.c1 = f, s, c0, c0 + KF
                self.wg = a[f"w_ffn{which}_gate"][li].rearrange("(k p) n -> p k n", p=P)
                self.wu = a[f"w_ffn{which}_up"][li].rearrange("(k p) n -> p k n", p=P)
                self.wd = a[f"w_ffn{which}_down"][li].rearrange("(k p) n -> p k n", p=P)
                self.next_widths = next_widths
                self.n0, self.m0 = f * KF, f * KD
                self.gate_done, self.scaled = sem("gate_done"), sem("gate_scaled")
                self.silu_done, self.act_done = sem("silu_done"), sem("act_done")
                self.ah_done, self.al_done, self.upd_done = sem("ah_done"), sem("al_done"), sem("upd_done")
                self.x_ready = sem(f"x_ready{s + 1}")

            def slot(self, c):
                return c % 2

            def sp(self, sp):
                def gate_pair(i):
                    for j in (0, 1):
                        c = self.c0 + j + 2 * i
                        cols = bass.ds((2 * i + j) * P, P)
                        load(sp, c, (self.c0 + j) % 2, [((0, KD * P), self.wg[:, :, cols]),
                                                        ((KD * P, 2 * KD * P), self.wu[:, :, cols])])
                first = 0
                if self.c0 == 0:
                    gate_pair(0)
                    first = 1
                with sp.Fori(first, KF // 2) as i:
                    gate_pair(i)
                with sp.Fori(0, KD) as m:
                    for j in (0, 1):
                        c = self.c1 + j + 2 * m
                        k0, k1 = j * HALF, j * HALF + HALF // 2
                        cols = bass.ds(m * P, P)
                        load(sp, c, (self.c1 + j) % 2,
                             [((0, HALF // 2 * P), self.wd[:, k0:k1, cols]),
                              ((HALF // 2 * P, HALF * P), self.wd[:, k1:k0 + HALF, cols])])

            def pe(self, pe):
                def gate_pair(i, first):
                    for j in (0, 1):
                        s = (self.c0 + j) % 2
                        pe.wait_ge(lo_done, self.c0 + j + 2 * i + 1)
                        for part, ps in ((0, gate_ps[j]), (1, up_ps[j])):
                            if not first:
                                pe.wait_ge(self.act_done if part else self.scaled, 2 * i + (self.n0 + j - 1))

                            def w(W, k):
                                at = (part * KD + k) * P
                                return W[:, s, at:at + P]
                            for k in range(KD):
                                if first and j == 0 and part == 0:
                                    pe.wait_ge(sem("xl"), KD * self.s + k + 1)
                                mm = product(pe, ps[:, 0:T], w, k, XH[:, k, :], XL[:, k, :], k == 0, k == KD - 1)
                            mm.then_inc(multiplied if part else self.gate_done, 1)
                            if first and j == 0 and part == 0:
                                norm_sum_pe(pe, self.s)
                gate_pair(0, True)
                with pe.Fori(1, KF // 2) as i:
                    gate_pair(i, False)

                def down_pair(i, first):
                    for mm_ in (0, 1):
                        for j in (0, 1):
                            s = (self.c1 + j) % 2
                            pe.wait_ge(lo_done, self.c1 + j + 2 * mm_ + 4 * i + 1)
                            if j == 0 and not first:
                                pe.wait_ge(self.upd_done, 2 * i + (self.m0 + mm_ - 1))

                            def w(W, k):
                                return W[:, s, k * P:(k + 1) * P]
                            for k in range(HALF):
                                kk = j * HALF + k
                                if first and mm_ == 0:
                                    pe.wait_ge(self.al_done, self.n0 + kk + 1)
                                mm = product(pe, down_ps[mm_][:, 0:T], w, k, AH[:, kk, :], AL[:, kk, :],
                                             kk == 0, kk == KF - 1)
                            mm.then_inc(multiplied, 1)
                down_pair(0, True)
                with pe.Fori(1, KD // 2) as i:
                    down_pair(i, False)

            def act(self, act):
                def gate_pair(i, widths):
                    for j in (0, 1):
                        n = 2 * i + j
                        act.wait_ge(self.scaled, n + (self.n0 + 1))
                        act.activation(si[:, j, :], gs[:, j, :], ACT.Silu).then_inc(self.silu_done, 1)
                        split_hi(act, self.c0 + 2 + j + 2 * i, (self.c0 + j) % 2, (self.c0 + j) // 2 + 1 + i, widths[j])
                        act.wait_ge(self.act_done, n + (self.n0 + 1))
                        act.activation(tile(AH, n), au[:, j, :], ACT.Copy).then_inc(self.ah_done, 1)
                with act.Fori(0, KF // 2 - 1) as i:
                    gate_pair(i, (SLOT, SLOT))
                gate_pair(KF // 2 - 1, (HALF * P, HALF * P))

                def down(m, widths):
                    for j in (0, 1):
                        if widths[j]:
                            split_hi(act, self.c1 + 2 + j + 2 * m, (self.c1 + j) % 2, (self.c1 + j) // 2 + 1 + m, widths[j])
                    if self.s + 1 < N_NORMS - 1:
                        norm_tile_act(act, self.s + 1, m, gain(m + KD * (self.s + 1)))
                with act.Fori(0, KD - 1) as m:
                    down(m, (HALF * P, HALF * P))
                down(KD - 1, self.next_widths)
                norm_root_act(act, self.s + 1)

            def dve(self, dve):
                def gate_pair(i, widths):
                    for j in (0, 1):
                        n, c = 2 * i + j, self.c0 + j + 2 * i
                        dve.wait_ge(self.gate_done, n + (self.n0 + 1))
                        if isinstance(i, int) and i == 0 and j == 0:
                            dve.wait_ge(sem("rs"), self.s + 1)
                        dve.tensor_tensor(gs[:, j, :], gate_ps[j][:, 0:T], rsb[:, 0:T], ALU.mult).then_inc(self.scaled, 1)
                        dve.wait_ge(self.silu_done, n + (self.n0 + 1))
                        dve.wait_ge(multiplied, c + 1)
                        dve.tensor_tensor(au[:, j, :], up_ps[j][:, 0:T], si[:, j, :], ALU.mult).then_inc(self.act_done, 1)
                        split_lo(dve, c + 2, (self.c0 + j) % 2, widths[j])
                        dve.wait_ge(self.ah_done, n + (self.n0 + 1))
                        dve.tensor_tensor(tile(AL, n), au[:, j, :], tile(AH, n).bitcast(F32), ALU.subtract).then_inc(self.al_done, 1)
                dve.wait_ge(sem("rs"), self.s + 1)
                with dve.Fori(0, KF // 2 - 1) as i:
                    gate_pair(i, (SLOT, SLOT))
                gate_pair(KF // 2 - 1, (HALF * P, HALF * P))

                def down(m, widths):
                    c = self.c1 + 2 * m
                    if widths[0]:
                        split_lo(dve, c + 2, self.c1 % 2, widths[0])
                    dve.wait_ge(multiplied, c + 2)
                    return c

                def down_pair(i, widths):
                    for q in (0, 1):
                        m = 2 * i + q
                        c = down(m, widths[q])
                        dve.scalar_tensor_tensor(upd[:, :], down_ps[q][:, 0:T], 0.5, rsb[:, 0:T], ALU.mult, ALU.mult)\
                           .then_inc(self.upd_done, 1)
                        dve.wait_ge(self.upd_done, m + (self.m0 + 1))
                        dve.tensor_tensor(tile(X, m), tile(X, m), upd[:, :], ALU.add).then_inc(self.x_ready, 1)
                        if widths[q][1]:
                            split_lo(dve, c + 3, (self.c1 + 1) % 2, widths[q][1])
                        if self.s + 1 < N_NORMS - 1:
                            norm_tile_dve(dve, self.s + 1, m, gain(m + KD * (self.s + 1)))
                w = (HALF * P, HALF * P)
                with dve.Fori(0, KD // 2 - 1) as i:
                    down_pair(i, (w, w))
                down_pair(KD // 2 - 1, (w, self.next_widths))
                norm_root_dve(dve, self.s + 1)

            def pool(self, pool):
                norm_sums_pool(pool, self.s + 1)

        def end_pe(pe):
            norm_sum_pe(pe, N_NORMS - 1)
            for k in range(KD):
                pe.wait_ge(sem("y_done"), k + 1)
                if k >= 2:
                    pe.wait_ge(sem("y_out"), k - 1)
                for t in range(TT):
                    mm = pe.transpose(gate_ps[k % 2][:, t * P:(t + 1) * P], yf[:, k % 2, t * P:(t + 1) * P], ident[:, :])
                mm.then_inc(sem("y_turned"), 1)

        def end_dve(dve):
            dve.wait_ge(sem("rs"), N_NORMS)
            for k in range(KD):
                if k >= 2:
                    dve.wait_ge(sem("y_turned"), k - 1)
                g = gain(FINAL_GAIN + k)
                dve.scalar_tensor_tensor(yf[:, k % 2, :], X[:, k, :], g, rsb[:, 0:T], ALU.mult, ALU.mult)\
                   .then_inc(sem("y_done"), 1)

        def end_act(act):
            for k in range(KD):
                act.wait_ge(sem("y_turned"), k + 1)
                act.activation(ytok[:, :, k * P:(k + 1) * P],
                               gate_ps[k % 2][:, 0:T].rearrange("p (t n) -> p t n", n=P), ACT.Copy)\
                   .then_inc(sem("y_out"), 1)

        def end_sp(sp):
            sp.wait_ge(sem("y_out"), KD)
            for t in range(TT):
                dst = out["y_prompt"][0, t * P:(t + 1) * P, :] if t < SEQ // P else \
                    out["y_sample"].rearrange("b s d -> (b s) d")
                sp.dma_start(dst, ytok[:, t, :]).then_inc(sem("stored"), 16)

        NP = SEQ // QBLK
        SC = NP * (NP + 1) // 2 * QBLK
        NC = PAST_LEN // P
        HQ = MLA_HEADS * DEC_SEQ
        PAST, NEW = slice(0, PAST_LEN), slice(PAST_LEN, PAST_LEN + P)
        LR = KV_LORA + ROPE
        with ExitStack() as r:
            mtab = sb("mtab", [P, P + 2 * T], F32, r)
            rot, mcos, msin = mtab[:, 0:P], mtab[:, P:P + T], mtab[:, P + T:P + 2 * T]
            mask_q = sb("mask_q", [1, P], F32, r)
            mask_k = sb("mask_k", [1, CHUNK], F32, r)
            qn = sb("qn", [P, MLA_HEADS, T], F32, r)
            qp = sb("qp", [ROPE, MLA_HEADS, T], F32, r)
            ckvT = sb("ckvT", [P, KV, T], F32, r)
            kpT = sb("kpT", [ROPE, T], F32, r)
            tok = sb("tok", [P, TT, LR], F32, r)
            wuk = sb("wuk", [P, KV, D_MODEL], F32, r)
            wuv = sb("wuv", [P, KV, D_MODEL], F32, r)
            wukT = sb("wukT", [P, MLA_HEADS, KV_LORA], F32, r)
            qps = sb("qps", [ROPE, DEC_BATCH, MLA_HEADS, DEC_SEQ], F32, r)
            lat = sb("lat", [P, KV, DEC_BATCH, MLA_HEADS, DEC_SEQ], F32, r)
            with ExitStack() as r1:
                cq = sb("cq", [P, KQ, T], F32, r1)
                cqh = sb("cqh", [P, KQ, T], F32R, r1)
                cql = sb("cql", [P, KQ, T], F32R, r1)
                ckv = sb("ckv", [P, KV, T], F32, r1)
                pe_raw = sb("pe_raw", [P, T], F32, r1)
                pe_cos = sb("pe_cos", [P, T], F32, r1)
                pe_sin = sb("pe_sin", [P, T], F32, r1)
                rq = sb("rq", [P, T], F32, r1)
                rkv = sb("rkv", [P, T], F32, r1)
                acc_q = sb("acc_q", [P, T], F32, r1)
                acc_kv = sb("acc_kv", [P, T], F32, r1)
            with ExitStack() as r2:
                NCB = 4
                cc = sb("cc", [P, NCB, NC, KV_LORA], F32, r2)
                cp = sb("cp", [P, NCB, NC, ROPE], F32, r2)
                stat = sb("stat", [P, 2, 8], F32, r2)
                with ExitStack() as r3:
                    val = sb("val", [P, NP, D_MODEL], F32, r3)
                    kn = sb("kn", [P, 2, SEQ], F32, r3)
                    pr = sb("pr", [P, 2, SC], F32, r3)
                    prT = sb("prT", [P, 2, SC], F32, r3)
                with ExitStack() as r3:
                    kt = sb("kt", [P, 2, KV + 1, PAST_LEN], F32, r3)
                    ps_ = sb("ps_", [P, 2, PAST_LEN + P], F32, r3)
                    psT = sb("psT", [P, 2, PAST_LEN + P], F32, r3)

        class Mla:
            N_CHUNKS = 7 + KD // 2

            def __init__(self, s, c0, next_widths):
                self.s, self.c0 = s, c0
                self.widths = [SLOT] * 3 + [KQ * UQ] * 4 + [SLOT] * (KD // 2) + list(next_widths)

            def look_act(self, act, q):
                c = self.c0 + q + 2
                if self.widths[q + 2]:
                    split_hi(act, c, c % 2, c // 2, self.widths[q + 2])

            def look_dve(self, dve, q):
                if self.widths[q + 2]:
                    split_lo(dve, self.c0 + q + 2, (self.c0 + q) % 2, self.widths[q + 2])

            def sp(self, sp):
                wdq = a["w_dq"][0].rearrange("(k p) n -> p k n", p=P)
                wdkv = a["w_dkv"][0].rearrange("(k p) n -> p k n", p=P)
                wuq = a["w_uq"][0].rearrange("(k p) n -> p k n", p=P)
                wo = a["w_o_mla"][0].rearrange("(k p) n -> p k n", p=P)
                first, second = (0, KD * P), (KD * P, 2 * KD * P)
                c = self.c0
                load(sp, c, c % 2, [(first, wdq[:, :, 0:P]), (second, wdq[:, :, P:2 * P])])
                load(sp, c + 1, (c + 1) % 2, [(first, wdq[:, :, 2 * P:3 * P]), (second, wdkv[:, :, 0:P])])
                sp.wait_ge(multiplied, c)
                sp.dma_start(mtab[:, :], a["c_mla"]).then_inc(sem("mtab_in"), 16)
                load(sp, c + 2, c % 2, [(first, wdkv[:, :, P:2 * P]), (second, wdkv[:, :, LR - P:LR])])
                sp.dma_start(wuk[:, :, :], a["w_uk"][0].rearrange("(k p) h n -> p k (h n)", p=P)).then_inc(sem("wuk_in"), 16)
                sp.dma_start(wuv[:, :, :], a["w_uv"][0].rearrange("(k p) h n -> p k (h n)", p=P)).then_inc(sem("wuv_in"), 16)
                for g in range(4):
                    load(sp, c + 3 + g, (c + 3 + g) % 2, [((0, 2 * UQ), wuq[:, 0:2, g * UQ:(g + 1) * UQ]),
                                                          ((2 * UQ, 3 * UQ), wuq[:, 2:3, g * UQ:(g + 1) * UQ])])
                for g in range(KD // 2):
                    load(sp, c + 7 + g, (c + 7 + g) % 2, [(first, wo[:, :, 2 * g * P:(2 * g + 1) * P]),
                                                          (second, wo[:, :, (2 * g + 1) * P:(2 * g + 2) * P])])
                    if g == 1:
                        self.sp_attention(sp)

            def sp_attention(self, sp):
                sp.wait_ge(multiplied, self.c0 + 7)
                sp.wait_ge(sem("m_rope"), 3 + 3 * 4)
                for b in range(DEC_BATCH):
                    if b == NCB:
                        for t in range(TT):
                            sp.wait_ge(sem("m_tok"), t + 1)
                            for o, n, lo, hi in (("ckv", KV_LORA, 0, KV_LORA), ("kpe", ROPE, KV_LORA, LR)):
                                if t < SEQ // P:
                                    dst = out[f"new_{o}_prompt"][0, 0, t * P:(t + 1) * P, :]
                                else:
                                    dst = out[f"new_{o}_sample"][0].rearrange("b s d -> (b s) d")
                                sp.dma_start(dst, tok[:, t, lo:hi]).then_inc(sem("stored"), 16)
                    if b >= NCB:
                        sp.wait_ge(sem("m_olat"), b - NCB + 1)
                    sp.dma_start(cc[:, b % NCB, :, :],
                                 a["cache_ckv"][0, b].rearrange("(p k) d -> p k d", k=NC)).then_inc(sem(f"cc_in{b % NCB}"), 16)
                    sp.dma_start(cp[:, b % NCB, :, :],
                                 a["cache_kpe"][0, b].rearrange("(p k) d -> p k d", k=NC)).then_inc(sem(f"cc_in{b % NCB}"), 16)

            def pe(self, pe):
                c0 = self.c0

                def projection(q, k_tiles, xh, xl, at, ready, before_last=None):
                    s = (c0 + q) % 2
                    pe.wait_ge(lo_done, c0 + q + 1)
                    banks = (gate_ps[q % 2], up_ps[q % 2])
                    for part, ps in enumerate(banks):
                        if part and before_last:
                            before_last()

                        def w(W, k):
                            return at(W[:, s, :], part, k)
                        for k in range(k_tiles):
                            if ready and part == 0:
                                pe.wait_ge(sem("xl"), KD * self.s + k + 1)
                            mm = product(pe, ps[:, 0:T], w, k, xh[:, k, :], xl[:, k, :], k == 0, k == k_tiles - 1)
                        mm.then_inc(multiplied if part else sem("m_part0"), 1)

                def two(W, part, k):
                    return W[:, (part * KD + k) * P:(part * KD + k + 1) * P]

                projection(0, KD, XH, XL, two, True, lambda: norm_sum_pe(pe, self.s))
                projection(1, KD, XH, XL, two, False)

                def q_sum():
                    pe.wait_ge(sem("m_acc_q"), KQ)
                    pe.matmul(norm_ps[:, 0:T], ones[:, :], acc_q[:, :], start=True, stop=True).then_inc(sem("m_ssq"), 1)
                pe.wait_ge(sem("m_proj"), 2)
                projection(2, KD, XH, XL, two, False, q_sum)

                def rotate(n):
                    pe.wait_ge(sem("m_proj"), 6 + 3 * n)
                    if n == 0:
                        pe.wait_ge(sem("mtab_in"), 16)
                    if n >= 1:
                        pe.wait_ge(sem("m_turn_read"), n)
                    pe.matmul(misc_ps[:, 0:T], rot, pe_raw[:, :], start=True, stop=True).then_inc(sem("m_turned"), 1)

                for g in range(4):
                    q, s = 3 + g, (c0 + 3 + g) % 2
                    pe.wait_ge(lo_done, c0 + q + 1)
                    for part in range(3):
                        ps = (gate_ps, up_ps, down_ps)[part][q % 2]

                        def w(Wt, k):
                            lo = (2 * k + part if part < 2 else 2 * KQ + k) * P
                            return Wt[:, s, lo:lo + P]
                        pe.wait_ge(sem("m_proj"), self.proj_before(g, part))
                        if part == 1:
                            rotate(g)
                        for k in range(KQ):
                            if g == 0 and part == 0:
                                pe.wait_ge(sem("m_cql"), k + 1)
                            mm = product(pe, ps[:, 0:T], w, k, cqh[:, k, :], cql[:, k, :], k == 0, k == KQ - 1)
                        mm.then_inc(multiplied if part == 2 else sem("m_part0"), 1)
                    if g == 0:
                        pe.wait_ge(sem("m_acc_kv"), KV)
                        pe.wait_ge(sem("m_var_q"), 1)
                        pe.matmul(norm_ps[:, 0:T], ones[:, :], acc_kv[:, :], start=True, stop=True).then_inc(sem("m_sskv"), 1)
                rotate(4)
                self.pe_prompt(pe)
                self.pe_sample(pe)

                for g in range(KD // 2):
                    q = 7 + g
                    pe.wait_ge(lo_done, c0 + q + 1)
                    s = (c0 + q) % 2
                    if g >= 2:
                        pe.wait_ge(sem(f"x_ready{self.s + 1}"), 2 * g - 2)
                    for part, ps in enumerate((gate_ps[g % 2], up_ps[g % 2])):
                        def w(W, k):
                            return two(W[:, s, :], part, k)
                        for k in range(KD):
                            if g == 0 and part == 0:
                                pe.wait_ge(sem("m_ol"), MLA_HEADS + k // 4 + 1)
                            mm = product(pe, ps[:, 0:T], w, k, XH[:, k, :], XL[:, k, :], k == 0, k == KD - 1)
                        mm.then_inc(multiplied if part else sem("m_o_part0"), 1)

            def proj_before(self, g, part):
                if g == 0:
                    return (3, 4, 1)[part]
                if g == 1:
                    return (5, 6, 1)[part]
                return 6 + 3 * (g - 2) + part + 1

            def pe_prompt(self, pe):
                pe.wait_ge(sem("wuk_in"), 16)
                pe.wait_ge(sem("wuv_in"), 16)
                pe.wait_ge(sem("m_proj"), 6 + 12)
                for i, ps in enumerate((gate_ps[0], gate_ps[1], up_ps[0], up_ps[1])):
                    for e in range(2):
                        for t in range(KV):
                            h = 2 * i + e
                            mm = pe.transpose(ps[:, (e * KV + t) * P:(e * KV + t + 1) * P],
                                              wuk[:, t, h * P:(h + 1) * P], ident[:, :])
                    mm.then_inc(sem("m_wukT"), 1)
                pe.wait_ge(sem("m_ckvT"), KV)
                pe.wait_ge(sem("m_rope"), 3 + 3 * 4)
                for i, ps in enumerate((down_ps[0], down_ps[1], norm_ps, misc_ps)):
                    kt_, half = i // 2, i % 2
                    for t in range(KV):
                        mm = pe.matmul(ps[:, 0:512], ckvT[:, t, kt_ * P:(kt_ + 1) * P],
                                       wuv[:, t, half * 512:(half + 1) * 512], start=(t == 0), stop=(t == KV - 1))
                    mm.then_inc(sem("m_val"), 1)
                for t in range(TT):
                    ps = down_ps[t % 2]
                    pe.wait_ge(sem("m_val_out"), t + 1 if t < 2 else 2)
                    if t == 2:
                        pe.wait_ge(sem("m_tok"), 1)
                    for k in range(KV):
                        pe.transpose(ps[:, k * P:(k + 1) * P], ckvT[:, k, t * P:(t + 1) * P], ident[:, :])
                    pe.transpose(ps[:, KV_LORA:LR], kpT[:, t * P:(t + 1) * P], ident[0:ROPE, 0:ROPE]).then_inc(sem("m_tok_turned"), 1)

                def keys(h):
                    if h == 0:
                        pe.wait_ge(sem("m_wukT_out"), 4)
                    if h >= 2:
                        pe.wait_ge(sem("m_kn"), h - 1)
                    for t in range(KV):
                        mm = pe.matmul(gate_ps[h % 2][:, 0:SEQ], wuk[:, t, h * P:(h + 1) * P], ckvT[:, t, 0:SEQ],
                                       start=(t == 0), stop=(t == KV - 1))
                    mm.then_inc(sem("m_keys"), 1)

                def scores(h):
                    pe.wait_ge(sem("m_kn"), h + 1)
                    if h == 0:
                        pe.wait_ge(sem("m_mask"), 3)
                    if h >= 2:
                        pe.wait_ge(sem("m_exp"), 2 * (h - 1))
                    ps = up_ps[h % 2]
                    at = 0
                    for blk in range(NP):
                        n, q0 = (blk + 1) * QBLK, blk * QBLK
                        pe.matmul(ps[:, at:at + n], qn[:, h, q0:q0 + QBLK], kn[:, h % 2, 0:n], start=True, stop=False)
                        pe.matmul(ps[:, at + n - CHUNK:at + n], mask_q[:, :], mask_k[:, :], start=False, stop=False,
                                  skip_group_check=True)
                        mm = pe.matmul(ps[:, at:at + n], qp[:, h, q0:q0 + QBLK], kpT[:, 0:n], start=False, stop=True)
                        at += n
                    mm.then_inc(sem("m_scores"), 1)

                def turn(h):
                    pe.wait_ge(sem("m_pr"), 2 * (h + 1))
                    if h < 2:
                        pe.wait_ge(sem("m_tok"), TT)
                    if h >= 2:
                        pe.wait_ge(sem("m_prT"), h - 1)
                    for i in range(SC // P):
                        mm = pe.transpose(down_ps[h % 2][:, i * P:(i + 1) * P], pr[:, h % 2, i * P:(i + 1) * P], ident[:, :])
                    mm.then_inc(sem("m_prTurned"), 1)

                def mix(h):
                    ps = (norm_ps, misc_ps)[h % 2]
                    pe.wait_ge(sem("m_prT"), h + 1)
                    if h < 2:
                        pe.wait_ge(sem("m_val_out"), 4)
                    if h >= 2:
                        pe.wait_ge(sem("m_ol"), h - 1)
                    at = 0
                    for blk in range(NP):
                        for k in range(blk + 1):
                            mm = pe.matmul(ps[:, blk * QBLK:(blk + 1) * QBLK], val[:, k, h * P:(h + 1) * P],
                                           prT[:, h % 2, at:at + P], start=(k == 0), stop=(k == blk))
                            at += P
                    mm.then_inc(sem("m_mixed"), 1)

                for i in range(MLA_HEADS + 3):
                    if i < MLA_HEADS:
                        keys(i)
                    if 0 <= i - 3:
                        mix(i - 3)
                    if 0 <= i - 1 < MLA_HEADS:
                        scores(i - 1)
                    if 0 <= i - 2 < MLA_HEADS:
                        turn(i - 2)

            def pe_sample(self, pe):
                for i in range(4):
                    ps = (gate_ps[0], gate_ps[1], up_ps[0], up_ps[1])[i]
                    pe.wait_ge(sem("m_exp"), 2 * MLA_HEADS)
                    for t in range(KV):
                        for e in range(2):
                            h = 2 * i + e
                            mm = pe.matmul(ps[:, (t * 2 + e) * P:(t * 2 + e + 1) * P], wukT[:, h, t * P:(t + 1) * P],
                                           qn[:, h, SEQ:T], start=True, stop=True)
                    mm.then_inc(sem("m_qlat"), 1)

                def turn_cache(b):
                    pe.wait_ge(sem(f"cc_in{b % NCB}"), 32 * (b // NCB + 1))
                    if b == 0:
                        pe.wait_ge(sem("m_lat"), 4 * KV)
                    if b >= 1:
                        pe.wait_ge(sem("m_kt_act"), 2 * b)
                        pe.wait_ge(sem("m_kt_dve"), b)
                    for t, ps in enumerate((gate_ps[0], gate_ps[1], up_ps[0])):
                        for k in range(NC):
                            if t < KV:
                                mm = pe.transpose(ps[:, k * P:(k + 1) * P], cc[:, b % NCB, k, t * P:(t + 1) * P], ident[:, :])
                            else:
                                mm = pe.transpose(ps[0:ROPE, k * P:(k + 1) * P], cp[:, b % NCB, k, :], ident[:, :])
                        mm.then_inc(sem("m_cturned"), 1)

                def scores(b):
                    pe.wait_ge(sem("m_kt_act"), 2 * (b + 1))
                    pe.wait_ge(sem("m_kt_dve"), b + 1)
                    if b == 0:
                        pe.wait_ge(sem("m_qps"), 1)
                        pe.wait_ge(sem("m_prT"), MLA_HEADS)
                    if b >= 1:
                        pe.wait_ge(sem("m_sexp"), 2 * b)
                    new = slice(SEQ + b * DEC_SEQ, SEQ + (b + 1) * DEC_SEQ)
                    for ps, n, ks in ((up_ps[1], PAST_LEN, [kt[:, b % 2, 0, :], kt[:, b % 2, 1, :], kt[0:ROPE, b % 2, 2, :]]),
                                      (down_ps[0], DEC_SEQ, [ckvT[:, 0, new], ckvT[:, 1, new], kpT[:, new]])):
                        qs = [x.rearrange("p h q -> p (h q)") for x in (lat[:, 0, b, :, :], lat[:, 1, b, :, :], qps[:, b, :, :])]
                        for i in range(3):
                            mm = pe.matmul(ps[:, 0:n], qs[i], ks[i], start=(i == 0), stop=(i == 2))
                    mm.then_inc(sem("m_sscores"), 1)

                def turn(b):
                    pe.wait_ge(sem("m_ps"), b + 1)
                    if b == 0:
                        pe.wait_ge(sem("m_ol"), MLA_HEADS)
                    if b >= 1:
                        pe.wait_ge(sem("m_psT"), 2 * b)
                    for k in range(NC + 1):
                        ps = down_ps[1][:, k * P:(k + 1) * P] if k < NC else norm_ps[:, 0:P]
                        mm = pe.transpose(ps, ps_[:, b % 2, k * P:(k + 1) * P], ident[:, :])
                    mm.then_inc(sem("m_psTurned"), 1)

                def mix(b):
                    pe.wait_ge(sem("m_psT"), 2 * (b + 1))
                    if b >= 1:
                        pe.wait_ge(sem("m_olat"), b)
                    for t in range(KV):
                        for k in range(NC + 1):
                            lhs = cc[:, b % NCB, k, t * P:(t + 1) * P] if k < NC else tok[:, TT - 1, t * P:(t + 1) * P]
                            mm = pe.matmul(misc_ps[:, t * P:(t + 1) * P], lhs, psT[:, b % 2, k * P:(k + 1) * P],
                                           start=(k == 0), stop=(k == NC))
                    mm.then_inc(sem("m_smixed"), 1)

                for i in range(DEC_BATCH + 3):
                    if i < DEC_BATCH:
                        turn_cache(i)
                    if 0 <= i - 3:
                        mix(i - 3)
                    if 0 <= i - 1 < DEC_BATCH:
                        scores(i - 1)
                    if 0 <= i - 2 < DEC_BATCH:
                        turn(i - 2)
                pe.wait_ge(sem("m_olat"), DEC_BATCH)
                for i, ps in enumerate(down_ps):
                    for e in range(4):
                        h = 4 * i + e
                        for t in range(KV):
                            mm = pe.matmul(ps[:, e * P:(e + 1) * P], wuv[:, t, h * P:(h + 1) * P], lat[:, t, :, h, :],
                                           start=(t == 0), stop=(t == KV - 1))
                    mm.then_inc(sem("m_vout"), 1)

            def act(self, act):
                for q in range(3):
                    self.look_act(act, q)
                    for t in ((0, 1), (2,), ())[q]:
                        act.wait_ge(sem("m_proj"), t + 1)
                        act.activation(cqh[:, t, :], cq[:, t, :], ACT.Copy, scale=gain(Q_GAIN + t)).then_inc(sem("m_cqh"), 1)
                act.wait_ge(sem("m_var_q"), 2)
                act.activation(rq[:, :], var[:, 0:T], ACT.Sqrt).then_inc(sem("m_rq"), 1)
                self.look_act(act, 3)
                act.wait_ge(sem("m_var_kv"), 2)
                act.activation(rkv[:, :], var[:, 0:T], ACT.Sqrt).then_inc(sem("m_rkv"), 1)
                for q in range(4, 7):
                    self.look_act(act, q)
                for i, ps in enumerate((gate_ps[0], gate_ps[1], up_ps[0], up_ps[1])):
                    act.wait_ge(sem("m_wukT"), i + 1)
                    act.activation(wukT[:, 2 * i:2 * i + 2, :].rearrange("p h n -> p (h n)"), ps[:, :], ACT.Copy).then_inc(sem("m_wukT_out"), 1)
                for i, ps in enumerate((down_ps[0], down_ps[1], norm_ps, misc_ps)):
                    act.wait_ge(sem("m_val"), i + 1)
                    act.activation(val[:, i // 2, (i % 2) * 512:(i % 2 + 1) * 512], ps[:, :], ACT.Copy).then_inc(sem("m_val_out"), 1)
                for t in range(TT):
                    act.wait_ge(sem("m_tok_turned"), t + 1)
                    act.activation(tok[:, t, :], down_ps[t % 2][:, 0:LR], ACT.Copy).then_inc(sem("m_tok"), 1)

                for i in range(MLA_HEADS + 3):
                    if i < MLA_HEADS:
                        act.wait_ge(sem("m_keys"), i + 1)
                        if i >= 2:
                            act.wait_ge(sem("m_scores"), i - 1)
                        act.activation(kn[:, i % 2, :], gate_ps[i % 2][:, 0:SEQ], ACT.Copy).then_inc(sem("m_kn"), 1)
                    h = i - 3
                    if h >= 0:
                        act.wait_ge(sem("m_mixed"), h + 1)
                        act.activation(XH[:, h, 0:SEQ], (norm_ps, misc_ps)[h % 2][:, 0:SEQ], ACT.Copy).then_inc(sem("m_oh"), 1)
                    h = i - 1
                    if 0 <= h < MLA_HEADS:
                        act.wait_ge(sem("m_negmax"), h + 1)
                        if h >= 2:
                            act.wait_ge(sem("m_prTurned"), h - 1)
                        at = 0
                        for blk in range(NP):
                            n = (blk + 1) * QBLK
                            act.activation(pr[:, h % 2, at:at + n], up_ps[h % 2][:, at:at + n], ACT.Exp,
                                           bias=stat[:, h % 2, 2 + blk:3 + blk], scale=MLA_SCALE,
                                           accum_out=stat[:, h % 2, 4 + blk:5 + blk]).then_inc(sem("m_exp"), 1)
                            at += n
                    h = i - 2
                    if 0 <= h < MLA_HEADS:
                        act.wait_ge(sem("m_prTurned"), h + 1)
                        if h >= 2:
                            act.wait_ge(sem("m_mixed"), h - 1)
                        act.activation(prT[:, h % 2, :], down_ps[h % 2][:, 0:SC], ACT.Copy).then_inc(sem("m_prT"), 1)

                for i, ps in enumerate((gate_ps[0], gate_ps[1], up_ps[0], up_ps[1])):
                    act.wait_ge(sem("m_qlat"), i + 1)
                    for t in range(KV):
                        act.activation(lat[:, t, :, 2 * i:2 * i + 2, :].rearrange("p b e q -> p e b q"),
                                       ps[:, t * 2 * P:(t + 1) * 2 * P].rearrange("p (e b q) -> p e b q", e=2, b=DEC_BATCH),
                                       ACT.Copy).then_inc(sem("m_lat"), 1)
                for i in range(DEC_BATCH + 3):
                    b = i
                    if b < DEC_BATCH:
                        for t in range(KV):
                            act.wait_ge(sem("m_cturned"), 3 * b + t + 1)
                            if b >= 2:
                                act.wait_ge(sem("m_sscores"), b - 1)
                            act.activation(kt[:, b % 2, t, :], gate_ps[t][:, :], ACT.Copy).then_inc(sem("m_kt_act"), 1)
                    b = i - 1
                    if 0 <= b < DEC_BATCH:
                        act.wait_ge(sem("m_snegmax"), b + 1)
                        act.wait_ge(sem("m_zero"), b + 1)
                        act.activation(ps_[:, b % 2, PAST], up_ps[1][:, :], ACT.Exp, bias=stat[:, b % 2, 2:3], scale=MLA_SCALE,
                                       accum_out=stat[:, b % 2, 4:5]).then_inc(sem("m_sexp"), 1)
                        at = PAST_LEN + b * DEC_SEQ
                        act.activation(ps_[:, b % 2, at:at + DEC_SEQ], down_ps[0][:, 0:DEC_SEQ], ACT.Exp,
                                       bias=stat[:, b % 2, 2:3], scale=MLA_SCALE,
                                       accum_out=stat[:, b % 2, 5:6]).then_inc(sem("m_sexp"), 1)
                    b = i - 2
                    if 0 <= b < DEC_BATCH:
                        act.wait_ge(sem("m_psTurned"), b + 1)
                        if b >= 2:
                            act.wait_ge(sem("m_smixed"), b - 1)
                        act.activation(psT[:, b % 2, PAST], down_ps[1][:, :], ACT.Copy).then_inc(sem("m_psT"), 1)
                        act.activation(psT[:, b % 2, NEW], norm_ps[:, 0:P], ACT.Copy).then_inc(sem("m_psT"), 1)
                for i in range(2):
                    act.wait_ge(sem("m_vout"), i + 1)
                    act.activation(XH[:, 4 * i:4 * i + 4, SEQ:T], down_ps[i][:, :].rearrange("p (h n) -> p h n", h=4),
                                   ACT.Copy).then_inc(sem("m_oh"), 1)
                for q in range(7, 7 + KD // 2):
                    self.look_act(act, q)
                act.wait_ge(sem("stored"), 16 * 2 * TT)
                act.wait_ge(multiplied, self.c0 + self.N_CHUNKS)
                for m in range(KD):
                    norm_tile_act(act, self.s + 1, m, gain(KD * (self.s + 1) + m))
                norm_root_act(act, self.s + 1)

            def dve(self, dve):
                c0 = self.c0
                dve.wait_ge(sem("rs"), self.s + 1)
                targets = [cq[:, 0, :], cq[:, 1, :], cq[:, 2, :], ckv[:, 0, :], ckv[:, 1, :], pe_raw[:, :]]
                for q in range(3):
                    for part in range(2):
                        t = 2 * q + part
                        dve.wait_ge(*((multiplied, c0 + q + 1) if part else (sem("m_part0"), q + 1)))
                        dve.tensor_tensor(targets[t], (gate_ps, up_ps)[part][q % 2][:, 0:T], rsb[:, 0:T], ALU.mult)\
                           .then_inc(sem("m_proj"), 1)
                    self.look_dve(dve, q)
                    for t in ((0, 1), (2,), ())[q]:
                        dve.wait_ge(sem("m_cqh"), t + 1)
                        dve.scalar_tensor_tensor(cql[:, t, :], cq[:, t, :], gain(Q_GAIN + t), cqh[:, t, :].bitcast(F32),
                                                 ALU.mult, ALU.subtract).then_inc(sem("m_cql"), 1)

                def root(ss, name, n):
                    dve.wait_ge(sem(ss), 1)
                    dve.tensor_scalar(var[:, 0:T], norm_ps[:, 0:T], 1.0 / n, EPS, ALU.mult, ALU.add).then_inc(sem(name), 1)
                    dve.wait_ge(sem(name), 1)
                    dve.reciprocal(var[:, 0:T], var[:, 0:T]).then_inc(sem(name), 1)

                def rope(n, outs):
                    if n == 0:
                        dve.wait_ge(sem("mtab_in"), 16)
                    dve.wait_ge(sem("m_proj"), 6 + 3 * n)
                    dve.wait_ge(sem("m_turned"), n + 1)
                    dve.tensor_tensor(pe_sin[:, :], misc_ps[:, 0:T], msin, ALU.mult).then_inc(sem("m_turn_read"), 1)
                    dve.tensor_tensor(pe_cos[:, :], pe_raw[:, :], mcos, ALU.mult).then_inc(sem("m_rope"), 1)
                    dve.wait_ge(sem("m_turn_read"), n + 1)
                    dve.wait_ge(sem("m_rope"), 3 * n + 1)
                    for lo, dst in outs:
                        ins = dve.tensor_tensor(dst, pe_cos[lo:lo + ROPE, :], pe_sin[lo:lo + ROPE, :], ALU.add)
                        ins.then_inc(sem("m_rope"), 1 if len(outs) == 2 else 2)
                root("m_ssq", "m_var_q", Q_LORA)
                rope(0, [(ROPE, kpT[:, :])])
                dve.wait_ge(sem("m_rq"), 1)
                for g in range(4):
                    q = 3 + g
                    for part in range(3):
                        dve.wait_ge(*((multiplied, c0 + q + 1) if part == 2 else (sem("m_part0"), 3 + 2 * g + part + 1)))
                        dst = qn[:, 2 * g + part, :] if part < 2 else pe_raw[:, :]
                        dve.tensor_tensor(dst, (gate_ps, up_ps, down_ps)[part][q % 2][:, 0:T], rq[:, :], ALU.mult)\
                           .then_inc(sem("m_proj"), 1)
                    self.look_dve(dve, q)
                    if g == 0:
                        root("m_sskv", "m_var_kv", KV_LORA)
                        dve.wait_ge(sem("m_rkv"), 1)
                        for t in range(KV):
                            dve.scalar_tensor_tensor(ckvT[:, t, :], ckv[:, t, :], gain(KV_GAIN + t), rkv[:, :],
                                                     ALU.mult, ALU.mult).then_inc(sem("m_ckvT"), 1)
                    rope(g + 1, [(0, qp[:, 2 * g, :]), (ROPE, qp[:, 2 * g + 1, :])])

                for i in range(MLA_HEADS + 3):
                    h = i - 3
                    if h >= 0:
                        dve.wait_ge(sem("m_oh"), h + 1)
                        dve.tensor_tensor(XL[:, h, 0:SEQ], (norm_ps, misc_ps)[h % 2][:, 0:SEQ], XH[:, h, 0:SEQ].bitcast(F32),
                                          ALU.subtract).then_inc(sem("m_ol"), 1)
                    h = i - 1
                    if 0 <= h < MLA_HEADS:
                        dve.wait_ge(sem("m_scores"), h + 1)
                        at = 0
                        for blk in range(NP):
                            n = (blk + 1) * QBLK
                            dve.tensor_reduce(stat[:, h % 2, blk:blk + 1], up_ps[h % 2][:, at:at + n], AX.X, ALU.max)\
                               .then_inc(sem("m_max"), 1)
                            at += n
                        dve.wait_ge(sem("m_max"), 2 * (h + 1))
                        dve.tensor_scalar(stat[:, h % 2, 2:4], stat[:, h % 2, 0:2], -MLA_SCALE, None, ALU.mult)\
                           .then_inc(sem("m_negmax"), 1)
                        dve.wait_ge(sem("m_exp"), 2 * (h + 1))
                        dve.reciprocal(stat[:, h % 2, 6:8], stat[:, h % 2, 4:6]).then_inc(sem("m_inv"), 1)
                        dve.wait_ge(sem("m_inv"), h + 1)
                        at = 0
                        for blk in range(NP):
                            n = (blk + 1) * QBLK
                            dve.tensor_scalar(pr[:, h % 2, at:at + n], pr[:, h % 2, at:at + n], stat[:, h % 2, 6 + blk:7 + blk],
                                              None, ALU.mult).then_inc(sem("m_pr"), 1)
                            at += n

                for i in range(DEC_BATCH + 3):
                    b = i
                    if b < DEC_BATCH:
                        dve.wait_ge(sem("m_cturned"), 3 * b + 3)
                        if b >= 2:
                            dve.wait_ge(sem("m_sscores"), b - 1)
                        dve.tensor_copy(kt[0:ROPE, b % 2, KV, :], up_ps[0][0:ROPE, :]).then_inc(sem("m_kt_dve"), 1)
                    b = i - 3
                    if b >= 0:
                        dve.wait_ge(sem("m_smixed"), b + 1)
                        dve.tensor_copy(lat[:, :, b, :, :].rearrange("p t h q -> p t (h q)"),
                                        misc_ps[:, 0:KV * P].rearrange("p (t n) -> p t n", t=KV))\
                           .then_inc(sem("m_olat"), 1)
                    b = i - 1
                    if 0 <= b < DEC_BATCH:
                        st = stat[:, b % 2, :]
                        dve.wait_ge(sem("m_sscores"), b + 1)
                        dve.tensor_reduce(st[:, 0:1], up_ps[1][:, :], AX.X, ALU.max).then_inc(sem("m_smax"), 1)
                        dve.tensor_reduce(st[:, 1:2], down_ps[0][:, 0:DEC_SEQ], AX.X, ALU.max).then_inc(sem("m_smax"), 1)
                        dve.wait_ge(sem("m_smax"), 3 * b + 2)
                        dve.tensor_tensor(st[:, 3:4], st[:, 0:1], st[:, 1:2], ALU.max).then_inc(sem("m_smax"), 1)
                        dve.wait_ge(sem("m_smax"), 3 * b + 3)
                        dve.tensor_scalar(st[:, 2:3], st[:, 3:4], -MLA_SCALE, None, ALU.mult).then_inc(sem("m_snegmax"), 1)
                        dve.wait_ge(sem("m_sexp"), 2 * (b + 1))
                        dve.tensor_tensor(st[:, 6:7], st[:, 4:5], st[:, 5:6], ALU.add).then_inc(sem("m_sinv"), 1)
                        dve.wait_ge(sem("m_sinv"), 2 * b + 1)
                        dve.reciprocal(st[:, 7:8], st[:, 6:7]).then_inc(sem("m_sinv"), 1)
                        dve.wait_ge(sem("m_sinv"), 2 * b + 2)
                        dve.tensor_scalar(ps_[:, b % 2, :], ps_[:, b % 2, :], st[:, 7:8], None, ALU.mult).then_inc(sem("m_ps"), 1)
                for i in range(2):
                    dve.wait_ge(sem("m_oh"), MLA_HEADS + i + 1)
                    dve.tensor_tensor(XL[:, 4 * i:4 * i + 4, SEQ:T], down_ps[i][:, :].rearrange("p (h n) -> p h n", h=4),
                                      XH[:, 4 * i:4 * i + 4, SEQ:T].bitcast(F32), ALU.subtract).then_inc(sem("m_ol"), 1)

                for g in range(KD // 2):
                    for part in range(2):
                        m = 2 * g + part
                        dve.wait_ge(*((multiplied, c0 + 7 + g + 1) if part else (sem("m_o_part0"), g + 1)))
                        dve.tensor_tensor(X[:, m, :], X[:, m, :], (gate_ps, up_ps)[part][g % 2][:, 0:T], ALU.add)\
                           .then_inc(sem(f"x_ready{self.s + 1}"), 1)
                    self.look_dve(dve, 7 + g)
                dve.wait_ge(sem("stored"), 16 * 2 * TT)
                for m in range(KD):
                    norm_tile_dve(dve, self.s + 1, m, gain(KD * (self.s + 1) + m))
                norm_root_dve(dve, self.s + 1)

            def pool(self, pool):
                pool.wait_ge(multiplied, self.c0)
                pool.memset(mask_q[:, :], 0.0).then_inc(sem("m_mask"), 1)
                pool.memset(mask_k[:, :], -1e30).then_inc(sem("m_mask"), 1)
                pool.wait_ge(sem("m_mask"), 2)
                pool.memset(mask_q[:, 0:CHUNK], 1.0).then_inc(sem("m_mask"), 1)
                for name, src, n, total, ready in (("q", cq, KQ, acc_q, 0), ("kv", ckv, KV, acc_kv, KQ)):
                    for t in range(n):
                        pool.wait_ge(sem("m_proj"), ready + t + 1)
                        if t:
                            pool.wait_ge(sem(f"m_acc_{name}"), t)
                        dst = sq[:, 0, :] if t else total[:, :]
                        pool.tensor_tensor(dst, src[:, t, :], src[:, t, :], ALU.mult)\
                            .then_inc(sem(f"m_sq_{name}" if t else f"m_acc_{name}"), 1)
                        if t:
                            pool.wait_ge(sem(f"m_sq_{name}"), t)
                            pool.tensor_tensor(total[:, :], total[:, :], sq[:, 0, :], ALU.add).then_inc(sem(f"m_acc_{name}"), 1)
                pool.wait_ge(sem("m_rope"), 3 + 3 * 4)
                pool.tensor_copy(qps[:, :, :, :], qp[:, :, SEQ:T].rearrange("p h (b q) -> p b h q", b=DEC_BATCH))\
                    .then_inc(sem("m_qps"), 1)
                for b in range(DEC_BATCH):
                    if b == 0:
                        pool.wait_ge(sem("m_prT"), MLA_HEADS)
                        pool.wait_ge(sem("m_ol"), MLA_HEADS)
                    if b >= 2:
                        pool.wait_ge(sem("m_psTurned"), b - 1)
                    pool.memset(ps_[:, b % 2, NEW], 0.0).then_inc(sem("m_zero"), 1)
                norm_sums_pool(pool, self.s + 1)

        HV, E, D = RET_DV, RET_DV // P, RET_DK // P
        PAIR = 2 * DEC_SEQ
        PAIRS = DEC_BATCH // 2
        N_NEW = D * (DEC_BATCH + 1)
        HC = 4 * P + P + 8
        DECAY, XI, ZETA = slice(0, 4 * P), slice(4 * P, 5 * P), 5 * P
        G16 = ZETA + 4
        with ExitStack() as r:
            rtab = sb("rtab", [P, 2, T], F32, r)
            rturn = sb("rturn", [P, 2, T], F32, r)
            hc = sb("hc", [P, HC], F32, r)
            rot4 = sb("rot4", [P, 4, T], F32, r)
            qT = sb("qT", [P, D, T], F32, r)
            kT = sb("kT", [P, D, T], F32, r)
            kz = sb("kz", [P, 4, RET_DK], F32, r)
            vt = sb("vt", [P, TT, HV], F32, r)
            gt = sb("gt", [P, 2, T], F32, r)
            sg = sb("sg", [P, E, T], F32, r)
            at_ = sb("at_", [P, 4 * P], F32, r)
            qz = sb("qz", [P, D, DEC_BATCH * PAIR], F32, r)
            st = sb("st", [P, DEC_BATCH, D, HV], F32, r)
            mark = sb("mark", [P, 5], F32, r)
            nsp = sb("nsp", [P, D, HV], F32, r)
            on = sb("on", [P, TT, HV], F32, r)
            rst = sb("rst", [P, 3, 4], F32, r)
            zf = sb("zf", [P, 2, T], F32, r)
            zh = sb("zh", [P, E, T], F32R, r)
            zl = sb("zl", [P, E, T], F32R, r)

        class Retention:
            PER = 8
            STORES = (16 * PAIRS, 16 * (PAIRS + 1))

            def __init__(self, s, c0):
                self.s, self.c0 = s, c0
                self.stored = (sem("r_stored0"), sem("r_stored1"))
                self.st_in = (sem("r_st_in0"), sem("r_st_in1"))
                self.x_base = 1 + KD * (RET_HEADS - 1)

            Q_BANKS, K_BANKS = (bank[1], bank[7]), (bank[2], bank[3])
            V_BANKS = ((bank[0], bank[4], bank[5]), (bank[6], bank[1], bank[7]))
            TURNED_K, SCORES = (bank[2], bank[2], bank[3]), bank[4]
            O_BANKS = (bank[5], bank[6], bank[7])
            G_BANKS = (bank[0], bank[1], bank[0], bank[1])
            NEW_BANKS = (bank[2:6] * 3) + [bank[2], bank[3], bank[4], bank[6], bank[7], bank[1]]
            TURNED_O = (bank[6], bank[7], bank[0], bank[5])
            OUT_BANKS = (bank[0], bank[5], bank[2], bank[3], bank[4], bank[6], bank[0], bank[5])

            def look_act(self, act, h, q):
                c, s = self.c0 + q + 2, (self.c0 + q) % 2
                split_hi(act, c + self.PER * h, s, c // 2 + self.PER // 2 * h, SLOT)

            def look_dve(self, dve, h, q):
                split_lo(dve, self.c0 + q + 2 + self.PER * h, (self.c0 + q) % 2, SLOT)

            def sp(self, sp):
                win = a["w_ret_in"][0].rearrange("(k p) n -> p k n", p=P)
                wout = a["w_ret_out"][0].rearrange("(k p) n -> p k n", p=P)
                first, second = (0, KD * P), (KD * P, 2 * KD * P)
                k0, v0 = RET_HEADS * RET_DK, 2 * RET_HEADS * RET_DK
                g0 = v0 + RET_HEADS * HV

                def chunk(h, q, pieces):
                    load(sp, self.c0 + q + self.PER * h, (self.c0 + q) % 2, pieces)

                def tiles(col):
                    return [(first, win[:, :, bass.ds(col, P)]), (second, win[:, :, bass.ds(col + P, P)])]

                with sp.Fori(0, RET_HEADS) as h:
                    chunk(h, 0, tiles(h * RET_DK))
                    chunk(h, 1, tiles(h * RET_DK + k0))
                    for j in range(2):
                        w = win[:, :, bass.ds(h * HV + (v0 + j * 2 * P), 2 * P)]
                        chunk(h, 2 + j, [(first, w[:, 0:KD // 2, :]), (second, w[:, KD // 2:KD, :])])
                    for j in range(2):
                        chunk(h, 4 + j, tiles(h * HV + (g0 + j * 2 * P)))
                    for j in range(2):
                        w = wout[:, :, j * 4 * P:(j + 1) * 4 * P]
                        chunk(h, 6 + j, [(first, w[:, bass.ds(h * E, E // 2), :]), (second, w[:, bass.ds(h * E + E // 2, E // 2), :])])

            @property
            def x_done(self):
                return sem(f"x_ready{self.s + 1}")

            def sp_end(self, sp):
                for i in range(2):
                    sp.wait_ge(self.stored[i], self.STORES[i] * RET_HEADS + 16)

            def pe(self, pe):
                pe.wait_ge(sem("xl"), KD * (self.s + 1))
                norm_sum_pe(pe, self.s)
                with pe.Fori(0, RET_HEADS) as h:
                    self.pe_head(pe, h)

            def pe_head(self, pe, h):
                c = self.c0 + self.PER * h

                def slot(q):
                    return (self.c0 + q) % 2

                def columns(q, banks, free=None):
                    pe.wait_ge(lo_done, c + (q + 1))
                    if free:
                        pe.wait_ge(*free)
                    for part, ps in enumerate(banks):
                        for k in range(KD):
                            mm = product(pe, ps[:, 0:T], lambda W, k: W[:, slot(q), (part * KD + k) * P:(part * KD + k + 1) * P],
                                         k, XH[:, k, :], XL[:, k, :], k == 0, k == KD - 1)
                        mm.then_inc(multiplied if part else sem("r_part"), 1)

                def values(q, banks, free=None):
                    pe.wait_ge(lo_done, c + (q + 1))
                    if free:
                        pe.wait_ge(*free)
                    for t, ps in enumerate(banks):
                        for k in range(KD):
                            wh, wl = WH[:, slot(q), k * 2 * P:(k + 1) * 2 * P], WL[:, slot(q), k * 2 * P:(k + 1) * 2 * P]
                            xh, xl = XH[:, k, t * P:(t + 1) * P], XL[:, k, t * P:(t + 1) * P]
                            pe.matmul(ps[:, 0:2 * P], xh, wh, start=(k == 0), stop=False)
                            pe.matmul(ps[:, 0:2 * P], xh, wl, start=False, stop=False)
                            mm = pe.matmul(ps[:, 0:2 * P], xl, wh, start=False, stop=(k == KD - 1))
                        mm.then_inc(multiplied if t == TT - 1 else sem("r_part"), 1)

                columns(0, self.Q_BANKS)
                pe.wait_ge(self.x_done, KD * h + 1)
                columns(1, self.K_BANKS)
                values(2, self.V_BANKS[0])
                values(3, self.V_BANKS[1], (sem("r_rot"), 8 * h + 4))

                pe.wait_ge(sem("r_T"), 4 * h + 4)
                for t, ps in enumerate(self.TURNED_K):
                    for d in range(D):
                        at = (t % 2 * D + d) * P
                        mm = pe.transpose(ps[:, at:at + P], kT[:, d, t * P:(t + 1) * P], ident[:, :])
                mm.then_inc(sem("r_k_turned"), 1)
                pe.wait_ge(sem("r_v"), 6 * h + 2)
                for at, ks, qs in ((0, slice(0, P), slice(0, SEQ)), (2 * P, slice(P, SEQ), slice(P, SEQ)),
                                   (3 * P, slice(SEQ, T), slice(SEQ, T))):
                    n = qs.stop - qs.start
                    for d in range(D):
                        mm = pe.matmul(self.SCORES[:, at:at + n], kT[:, d, ks], qT[:, d, qs], start=(d == 0), stop=(d == D - 1))
                mm.then_inc(sem("r_scores"), 1)
                o0, o1, os = self.O_BANKS
                pe.wait_ge(sem("r_v"), 6 * h + 6)
                pe.wait_ge(sem("r_qz"), D * h + D)
                for odd in range(2):
                    pe.wait_ge(self.st_in[odd], 16 * PAIRS * h + 16 * PAIRS)
                    for d in range(D):
                        for j in range(PAIRS):
                            b = 2 * j + odd
                            pe.matmul(os[j * PAIR:(j + 1) * PAIR, :], qz[:, d, b * PAIR:(b + 1) * PAIR], st[:, b, d, :],
                                      start=(odd == 0 and d == 0), stop=False)
                pe.wait_ge(sem("r_at"), h + 1)
                pe.matmul(os[:, :], at_[:, 3 * P:4 * P], vt[:, 2, :], start=False, stop=True)
                pe.matmul(o0[:, :], at_[:, 0:P], vt[:, 0, :], start=True, stop=True)
                pe.matmul(o1[:, :], at_[:, P:2 * P], vt[:, 0, :], start=True, stop=False)
                pe.matmul(o1[:, :], at_[:, 2 * P:3 * P], vt[:, 1, :], start=False, stop=True).then_inc(sem("r_o"), 1)

                def new_states(part):
                    odd, d = part // D, part % D
                    if part == 0:
                        pe.wait_ge(sem("r_kz"), 4 * h + 4)
                        pe.wait_ge(sem("r_on"), TT * h + 1)
                    for j in range(PAIRS):
                        n = PAIRS * part + j
                        if part:
                            pe.wait_ge(sem("r_ns"), N_NEW * h + (n - PAIRS + 1))
                        if part == 3 and j == 3:
                            pe.wait_ge(sem("r_z"), E * h + 1)
                        rows = slice(j * PAIR, (j + 1) * PAIR)
                        pe.matmul(self.NEW_BANKS[n][:, :], kz[rows, 2 + odd, d * P:(d + 1) * P], vt[rows, 2, :],
                                  start=True, stop=True).then_inc(sem("r_new"), 1)

                def gate(n):
                    q, part = 4 + n // 2, n % 2
                    if part == 0:
                        pe.wait_ge(lo_done, c + (q + 1))
                    if n >= 2:
                        pe.wait_ge(sem("r_gt"), E * h + (n - 1))
                    for k in range(KD):
                        mm = product(pe, self.G_BANKS[n][:, 0:T], lambda W, k: W[:, slot(q), (part * KD + k) * P:(part * KD + k + 1) * P],
                                     k, XH[:, k, :], XL[:, k, :], k == 0, k == KD - 1)
                    mm.then_inc(multiplied if part else sem("r_part"), 1)

                def turn(e):
                    for t in range(TT):
                        mm = pe.transpose(self.TURNED_O[e][:, t * P:(t + 1) * P], on[:, t, e * P:(e + 1) * P], ident[:, :])
                    mm.then_inc(sem("r_o_turned"), 1)

                for n in range(3):
                    gate(n)
                    new_states(n)
                pe.wait_ge(sem("r_on"), TT * h + TT)
                turn(0)
                turn(1)
                gate(3)
                pe.wait_ge(sem("r_gt"), E * h + 3)
                turn(2)
                pe.wait_ge(sem("r_ns"), N_NEW * h + 3 * PAIRS)
                turn(3)
                new_states(3)
                for d in range(D):
                    if d == 0:
                        pe.wait_ge(sem("r_z"), E * h + 2)
                    else:
                        pe.wait_ge(sem("r_gt"), E * h + E)
                    for t in range(2):
                        mm = pe.matmul(self.NEW_BANKS[4 * PAIRS + d][:, :], kz[:, t, d * P:(d + 1) * P], vt[:, t, :],
                                       start=(t == 0), stop=(t == 1))
                    mm.then_inc(sem("r_new"), 1)

                for m, ps in enumerate(self.OUT_BANKS):
                    q = 6 + m // 4
                    if m % 4 == 0:
                        pe.wait_ge(lo_done, c + (q + 1))
                    if m == 0:
                        pe.wait_ge(sem("r_z"), E * h + 3)
                    if m == 2:
                        pe.wait_ge(sem("r_ns"), N_NEW * h + N_NEW)
                    if m >= 6:
                        pe.wait_ge(self.x_done, KD * h + (m - 6 + 2))
                    for k in range(E):
                        if m == 0:
                            pe.wait_ge(sem("r_zl"), E * h + (k + 1))
                        mm = product(pe, ps[:, 0:T], lambda W, k: W[:, slot(q), (4 * k + m % 4) * P:(4 * k + m % 4 + 1) * P],
                                     k, zh[:, k, :], zl[:, k, :], k == 0, k == E - 1)
                    mm.then_inc(multiplied if m % 4 == 3 else sem("r_out"), 1)

            def act(self, act):
                with act.Fori(0, RET_HEADS) as h:
                    self.act_head(act, h)
                for m in range(KD):
                    norm_tile_act(act, self.s + 1, m, gain(KD * (self.s + 1) + m), self.x_base)
                for i in range(2):
                    act.wait_ge(self.stored[i], self.STORES[i] * RET_HEADS + 16)
                norm_root_act(act, self.s + 1)

            def act_head(self, act, h):
                c = self.c0 + self.PER * h
                self.look_act(act, h, 0)
                self.look_act(act, h, 1)
                def value_tiles(j):
                    for t, ps in enumerate(self.V_BANKS[j]):
                        if t < TT - 1:
                            act.wait_ge(sem("r_part"), 8 * h + (2 + 2 * j + t + 1))
                        else:
                            act.wait_ge(multiplied, c + (2 + j + 1))
                        act.activation(vt[:, t, j * 2 * P:(j + 1) * 2 * P], ps[:, 0:2 * P], ACT.Copy,
                                       scale=rsb[:, T + t:T + t + 1]).then_inc(sem("r_v"), 1)

                def silu(e):
                    act.wait_ge(sem("r_gt"), E * h + (e + 1))
                    act.activation(sg[:, e, :], gt[:, e % 2, :], ACT.Silu).then_inc(sem("r_sg"), 1)

                def z_hi(e):
                    act.wait_ge(sem("r_z"), E * h + (e + 1))
                    act.activation(zh[:, e, :], zf[:, e % 2, :], ACT.Copy).then_inc(sem("r_zh"), 1)

                value_tiles(0)
                self.look_act(act, h, 2)
                value_tiles(1)
                act.wait_ge(sem("r_hc_in"), 16 * h + 16)
                act.wait_ge(sem("r_k_turned"), h + 1)
                t0, t1, ts = (ps[:, at:at + RET_DK] for ps, at in zip(self.TURNED_K, (0, RET_DK, 0)))
                for i, src in enumerate((t0, t1, ts, ts)):
                    act.activation(kz[:, i, :], src, ACT.Copy, scale=hc[:, ZETA + i:ZETA + i + 1]).then_inc(sem("r_kz"), 1)
                self.look_act(act, h, 3)
                act.wait_ge(sem("r_o"), h + 1)
                for t in range(TT):
                    act.activation(on[:, t, :], self.O_BANKS[t][:, :], ACT.Square, accum_out=rst[:, 0, t:t + 1]).then_inc(sem("r_sq"), 1)
                act.wait_ge(sem("r_var"), 2 * h + 2)
                act.activation(rst[:, 2, 0:TT], rst[:, 1, 0:TT], ACT.Sqrt).then_inc(sem("r_root"), 1)
                act.wait_ge(sem("r_root"), h + 1)
                for t in range(TT):
                    act.activation(on[:, t, :], self.O_BANKS[t][:, :], ACT.Copy, scale=rst[:, 2, t:t + 1]).then_inc(sem("r_on"), 1)
                silu(0)
                silu(1)
                self.look_act(act, h, 4)
                silu(2)
                z_hi(0)
                z_hi(1)
                silu(3)
                z_hi(2)
                z_hi(3)
                for q in (5, 6, 7):
                    self.look_act(act, h, q)

            def dve(self, dve):
                dve.wait_ge(sem("rs"), self.s + 1)
                for i in range(2):
                    dve.wait_ge(self.stored[i], 16)
                    ins = dve.tensor_tensor(rturn[:, i, :], rtab[:, i, :], rsb[:, 0:T], ALU.mult)
                    ins.then_inc(sem("r_rturn"), 1)
                dve.wait_ge(sem("r_rturn"), 2)
                dve.tensor_copy(rst[:, 2, 3:4], ones[:, 0:1]).then_inc(self.x_done, 1)
                with dve.Fori(0, RET_HEADS) as h:
                    self.dve_head(dve, h)
                for m in range(KD):
                    norm_tile_dve(dve, self.s + 1, m, gain(KD * (self.s + 1) + m))
                for i in range(2):
                    dve.wait_ge(self.stored[i], self.STORES[i] * RET_HEADS + 16)
                norm_root_dve(dve, self.s + 1)

            def dve_head(self, dve, h):
                c = self.c0 + self.PER * h
                cos, sin = rturn[:, 0, :], rturn[:, 1, :]
                for i in range(2):
                    dve.wait_ge(sem("r_part"), 8 * h + (i + 1))
                    if i:
                        dve.wait_ge(sem("r_T"), 4 * h + 2)
                    x1, x2 = (self.Q_BANKS, self.K_BANKS)[i]
                    dve.tensor_tensor(rot4[:, 0, :], x1[:, 0:T], cos, ALU.mult).then_inc(sem("r_rot"), 1)
                    dve.tensor_tensor(rot4[:, 1, :], x1[:, 0:T], sin, ALU.mult).then_inc(sem("r_rot"), 1)
                    dve.wait_ge(multiplied, c + (i + 1))
                    dve.tensor_tensor(rot4[:, 2, :], x2[:, 0:T], sin, ALU.mult).then_inc(sem("r_rot"), 1)
                    dve.tensor_tensor(rot4[:, 3, :], x2[:, 0:T], cos, ALU.mult).then_inc(sem("r_rot"), 1)
                    self.look_dve(dve, h, i)
                self.look_dve(dve, h, 2)
                dve.wait_ge(sem("r_hc_in"), 16 * h + 16)
                dve.wait_ge(sem("r_scores"), h + 1)
                dve.tensor_tensor(at_[:, :], self.SCORES[:, :], hc[:, DECAY], ALU.mult).then_inc(sem("r_at"), 1)
                self.look_dve(dve, h, 3)
                dve.wait_ge(sem("r_sq"), TT * h + TT)
                dve.tensor_scalar(rst[:, 1, 0:TT], rst[:, 0, 0:TT], 1.0 / HV, EPS, ALU.mult, ALU.add).then_inc(sem("r_var"), 1)
                dve.wait_ge(sem("r_var"), 2 * h + 1)
                dve.reciprocal(rst[:, 1, 0:TT], rst[:, 1, 0:TT]).then_inc(sem("r_var"), 1)

                def gate(e):
                    if e % 2:
                        dve.wait_ge(multiplied, c + (4 + e // 2 + 1))
                    else:
                        dve.wait_ge(sem("r_part"), 8 * h + (6 + e // 2 + 1))
                    if e >= 2:
                        dve.wait_ge(sem("r_sg"), E * h + (e - 1))
                    dve.tensor_tensor(gt[:, e % 2, :], self.G_BANKS[e][:, 0:T], rsb[:, 0:T], ALU.mult).then_inc(sem("r_gt"), 1)

                def new_states(part):
                    odd, d = part // D, part % D
                    for j in range(PAIRS):
                        n = PAIRS * part + j
                        dve.wait_ge(sem("r_new"), N_NEW * h + (n + 1))
                        old = st[:, 2 * j + odd, d, :]
                        dve.scalar_tensor_tensor(old, old, hc[:, G16:G16 + 1], self.NEW_BANKS[n][:, :],
                                                 ALU.mult, ALU.add).then_inc(sem("r_ns"), 1)

                def z(e):
                    dve.wait_ge(sem("r_o_turned"), E * h + (e + 1))
                    dve.wait_ge(sem("r_sg"), E * h + (e + 1))
                    if e >= 2:
                        dve.wait_ge(sem("r_zl"), E * h + (e - 1))
                    dve.scalar_tensor_tensor(zf[:, e % 2, :], self.TURNED_O[e][:, 0:T], gains[:, bass.ds(E * h + (RET_GAIN + e), 1)],
                                             sg[:, e, :], ALU.mult, ALU.mult).then_inc(sem("r_z"), 1)

                for e in range(2):
                    gate(e)
                    new_states(e)
                self.look_dve(dve, h, 4)
                gate(2)
                new_states(2)
                z(0)
                z(1)
                self.dve_zl(dve, h, 0)
                self.dve_zl(dve, h, 1)
                gate(3)
                z(2)
                z(3)
                self.dve_zl(dve, h, 2)
                self.dve_zl(dve, h, 3)
                new_states(3)
                dve.wait_ge(self.stored[1], self.STORES[1] * h + 16)
                for d in range(D):
                    n = 4 * PAIRS + d
                    dve.wait_ge(sem("r_new"), N_NEW * h + (n + 1))
                    dve.tensor_copy(nsp[:, d, :], self.NEW_BANKS[n][:, :]).then_inc(sem("r_ns"), 1)
                self.look_dve(dve, h, 5)
                for m, ps in enumerate(self.OUT_BANKS):
                    if m % 4 < 3:
                        dve.wait_ge(sem("r_out"), 6 * h + (3 * (m // 4) + m % 4 + 1))
                    else:
                        dve.wait_ge(multiplied, c + (6 + m // 4 + 1))
                    dve.tensor_tensor(X[:, m, :], X[:, m, :], ps[:, 0:T], ALU.add).then_inc(self.x_done, 1)
                    if m % 4 == 3:
                        self.look_dve(dve, h, 6 + m // 4)

            def dve_zl(self, dve, h, e):
                dve.wait_ge(sem("r_zh"), E * h + (e + 1))
                dve.tensor_tensor(zl[:, e, :], zf[:, e % 2, :], zh[:, e, :].bitcast(F32), ALU.subtract).then_inc(sem("r_zl"), 1)

            def pool(self, pool):
                pool.wait_ge(multiplied, self.c0)
                for i in range(2):
                    pool.dma_start(rtab[:, i, :], a["c_rtab"][:, i * T:(i + 1) * T]).then_inc(self.stored[i], 16)
                pool.memset(qz[:, :, :], 0.0).then_inc(sem("r_zero"), 1)
                pool.wait_ge(sem("r_zero"), 1)

                def head_of(x, h):
                    return x.rearrange("h (d p) e -> p (h d) e", p=P)[:, bass.ds(h * D, D), :]

                def wait_at_mark(i, count, value):
                    pool.wait_ge(count, value)
                    pool.tensor_tensor(mark[:, i:i + 1], ones[:, 0:1], ones[:, 0:1], ALU.mult).then_inc(sem("r_mark"), 1)

                with pool.Fori(0, RET_HEADS) as h:
                    pool.dma_start(hc[:, :], a["c_ret"][:, bass.ds(h * HC, HC)]).then_inc(sem("r_hc_in"), 16)
                    for odd in range(2):
                        wait_at_mark(odd, self.stored[odd], self.STORES[odd] * h + 16)
                        for b in range(odd, DEC_BATCH, 2):
                            pool.dma_start(st[:, b, :, :], head_of(a["state_ret"][0, b], h)).then_inc(self.st_in[odd], 16)
                    for i, dst in enumerate((qT, kT)):
                        pool.wait_ge(sem("r_rot"), 8 * h + (4 * i + 4))
                        pool.tensor_tensor(dst[:, 0, :], rot4[:, 0, :], rot4[:, 2, :], ALU.subtract).then_inc(sem("r_T"), 1)
                        pool.tensor_tensor(dst[:, 1, :], rot4[:, 1, :], rot4[:, 3, :], ALU.add).then_inc(sem("r_T"), 1)
                        if i == 0:
                            pool.wait_ge(sem("r_hc_in"), 16 * h + 16)
                            pool.wait_ge(sem("r_T"), 4 * h + 2)
                            for d in range(D):
                                def runs(x, n):
                                    return x.rearrange("p (j e n) -> p j e n", e=n, n=DEC_SEQ)
                                pool.tensor_tensor(runs(qz[:, d, :], 4)[:, :, 0:4:3, :], runs(qT[:, d, SEQ:T], 2),
                                                   runs(hc[:, XI], 2), ALU.mult).then_inc(sem("r_qz"), 1)
                    for odd in range(2):
                        wait_at_mark(2 + odd, sem("r_ns"), N_NEW * h + 2 * PAIRS * (odd + 1))
                        for b in range(odd, DEC_BATCH, 2):
                            pool.dma_start(head_of(out["new_state_sample"][0, b], h), st[:, b, :, :])\
                                .then_inc(self.stored[odd], 16)
                    wait_at_mark(4, sem("r_ns"), N_NEW * h + N_NEW)
                    pool.dma_start(head_of(out["new_state_prompt"][0, 0], h), nsp[:, :, :]).then_inc(self.stored[1], 16)
                norm_sums_pool(pool, self.s + 1, self.x_base)

        C = 2 * KD + KF
        c_mla, c_ret = C, 3 * C + Mla.N_CHUNKS
        c_last = c_ret + Retention.PER * RET_HEADS
        whole, half = (SLOT, SLOT), (0, 0)
        phases = [Ffn(0, 0, 1, 0, 0, whole), Mla(1, c_mla, whole), Ffn(1, 0, 2, 2, c_mla + Mla.N_CHUNKS, whole),
                  Ffn(2, 1, 1, 3, c_mla + Mla.N_CHUNKS + C, whole), Retention(4, c_ret), Ffn(3, 1, 2, 5, c_last, half)]

        block = ctx.enter_context(nc.Block())

        @block.sync
        def _(sp):
            start_sp(sp)
            for ph in phases:
                ph.sp(sp)
            end_sp(sp)
            for ph in phases:
                if isinstance(ph, Retention):
                    ph.sp_end(sp)
            sp.wait_ge(sem("stored"), 16 * STORES)

        @block.gpsimd
        def _(pool):
            start_pool(pool)
            norm_sums_pool(pool, 0)
            for ph in phases:
                ph.pool(pool)

        @block.scalar
        def _(act):
            start_act(act)
            for ph in phases:
                ph.act(act)
            end_act(act)

        @block.vector
        def _(dve):
            start_dve(dve)
            for ph in phases:
                ph.dve(dve)
            end_dve(dve)

        @block.tensor
        def _(pe):
            start_pe(pe)
            for ph in phases:
                ph.pe(pe)
            end_pe(pe)


def constants():
    f = np.float32
    pos = np.concatenate([np.arange(SEQ), np.tile(PAST_LEN + np.arange(DEC_SEQ), DEC_BATCH)]).astype(f)

    def angles(d):
        inv = f(1.0) / (f(ROPE_THETA) ** (np.arange(0, d, 2, dtype=f) / f(d)))
        ang = (inv[:, None] * pos[None, :]).astype(f).astype(np.float64)
        return np.cos(ang).astype(f), np.sin(ang).astype(f)

    turn, half = np.zeros((P, P), f), ROPE // 2
    for base in range(0, P, ROPE):
        for i in range(half):
            turn[base + half + i, base + i] = -1.0
            turn[base + i, base + half + i] = 1.0
    cos, sin = angles(ROPE)
    mla = np.concatenate([turn, np.tile(cos, (4, 1)), np.tile(sin, (4, 1))], axis=1)
    lg = np.log(f(1.0) - f(2.0) ** (-5.0 - np.arange(RET_HEADS, dtype=f))).astype(f).astype(np.float64)
    scale = RET_DK ** -0.5
    p, i = np.arange(P)[:, None], np.arange(SEQ)[None, :]
    s, j = p % DEC_SEQ, np.arange(P)[None, :]
    heads = []
    for g in lg:
        prompt = np.where(i >= p, np.exp(g * np.maximum(i - p, 0)), 0.0) * scale
        mine = (p // DEC_SEQ == j // DEC_SEQ) & (j % DEC_SEQ >= s)
        sample = np.where(mine, np.exp(g * np.maximum(j % DEC_SEQ - s, 0)), 0.0) * scale
        xi = np.broadcast_to(np.exp(g * (j % DEC_SEQ + 1)), (P, P))
        z = np.exp(g * (DEC_SEQ - 1 - s)) * scale
        even = p // DEC_SEQ % 2 == 0
        zeta = [np.exp(g * (SEQ - 1 - p)) * scale, np.exp(g * (SEQ - 1 - P - p)) * scale, z * even, z * ~even,
                np.full((P, 1), np.exp(g * DEC_SEQ)), np.zeros((P, 3))]
        heads.append(np.concatenate([prompt, prompt[:, 0:P], sample, xi] + zeta, axis=1))
    return {"c_ident": np.eye(P, dtype=f), "c_mla": mla, "c_rtab": np.concatenate(angles(RET_DK), axis=1),
            "c_ret": np.concatenate(heads, axis=1).astype(f)}


INPUTS = ["x_prompt", "x_sample", "cache_ckv", "cache_kpe", "state_ret", "norm_ffn1", "w_ffn1_gate", "w_ffn1_up",
          "w_ffn1_down", "norm_mix", "w_dq", "q_norm", "w_uq", "w_dkv", "kv_norm", "w_uk", "w_uv", "w_o_mla",
          "w_ret_in", "ret_gn", "w_ret_out", "norm_ffn2", "w_ffn2_gate", "w_ffn2_up", "w_ffn2_down", "norm_final"]
OUTPUTS = [("y_prompt", (1, SEQ, D_MODEL)), ("y_sample", (DEC_BATCH, DEC_SEQ, D_MODEL)),
           ("new_ckv_prompt", (1, 1, SEQ, KV_LORA)), ("new_kpe_prompt", (1, 1, SEQ, ROPE)),
           ("new_state_prompt", (1, 1, RET_HEADS, RET_DK, RET_DV)),
           ("new_ckv_sample", (1, DEC_BATCH, DEC_SEQ, KV_LORA)), ("new_kpe_sample", (1, DEC_BATCH, DEC_SEQ, ROPE)),
           ("new_state_sample", (1, DEC_BATCH, RET_HEADS, RET_DK, RET_DV))]


def kernel(**inputs):
    import concourse.bacc as bacc
    from concourse.bass_utils import run_bass_kernel_spmd

    nc = bacc.Bacc("TRN2", target_bir_lowering=False, num_devices=1)
    arrays = {f"{n}_dram": np.ascontiguousarray(inputs[n]) for n in INPUTS}
    arrays.update({f"{n}_dram": x for n, x in constants().items()})
    a = {n[:-5]: nc.dram_tensor(n, x.shape, mybir.dt.from_np(x.dtype), kind="ExternalInput").ap()
         for n, x in arrays.items()}
    out = {n: nc.dram_tensor(f"{n}_dram", shape, F32, kind="ExternalOutput").ap() for n, shape in OUTPUTS}
    stream_kernel(nc, a, out)
    r = run_bass_kernel_spmd(nc, [arrays], core_ids=[0]).results[0]
    return tuple(r[f"{n}_dram"] for n, _ in OUTPUTS)
```

```python
from contextlib import ExitStack

import concourse.bass as bass
import numpy as np
from concourse import mybir
from concourse.alu_op_type import AluOpType as ALU

F32 = mybir.dt.float32
F32R = mybir.dt.float32r
ACT = mybir.ActivationFunctionType
AX = mybir.AxisListType
P = 128

D_MODEL, SEQ, DEPTH, DEC_BATCH, DEC_SEQ, PAST_LEN = 1024, 256, 2, 8, 16, 512
CHUNK, QBLK = 64, 128
MLA_HEADS, NOPE, ROPE, Q_LORA, KV_LORA = D_MODEL // 128, 128, 64, 3 * D_MODEL // 8, D_MODEL // 4
MLA_SCALE = (NOPE + ROPE) ** -0.5
RET_HEADS = 4
RET_DK, RET_DV = D_MODEL // RET_HEADS, 2 * D_MODEL // RET_HEADS
FFN_DIM = 256 * ((8 * D_MODEL // 3 + 255) // 256)
EPS = 1e-6
ROPE_THETA = 10000.0

T = SEQ + DEC_BATCH * DEC_SEQ
TT = T // P
KD = D_MODEL // P
KF = FFN_DIM // P
KQ = Q_LORA // P
KV = KV_LORA // P
SLOT = 2 * KD * P
UQ = 2 * (NOPE + ROPE)
HALF = KF // 2

GAINS = [("norm_ffn1", 0), ("norm_mix", 0), ("norm_ffn2", 0), ("norm_ffn1", 1), ("norm_mix", 1), ("norm_ffn2", 1),
         ("norm_final", None), ("q_norm", 0), ("kv_norm", 0), ("ret_gn", 0)]
FINAL_GAIN = 3 * DEPTH * KD
Q_GAIN = FINAL_GAIN + KD
KV_GAIN = Q_GAIN + KQ
RET_GAIN = KV_GAIN + KV
NG = RET_GAIN + RET_HEADS * RET_DV // P
N_NORMS = 3 * DEPTH + 1
STORES = 3 * TT


def stream_kernel(nc, a, out):
    ctx = ExitStack()
    with ctx:
        def sb(name, shape, dt=F32, where=ctx):
            return where.enter_context(nc.sbuf_tensor(name, shape, dt))

        def tile(t, i, n=T):
            flat = t[:, :, :].rearrange("p k n -> p (k n)")
            return flat[:, i * n:(i + 1) * n] if isinstance(i, int) else flat[:, bass.ds(i * n, n)]

        def gain(i):
            return gains[:, i:i + 1] if isinstance(i, int) else gains[:, bass.ds(i, 1)]

        sems = {}

        def sem(name):
            if name not in sems:
                sems[name] = ctx.enter_context(nc.semaphore(name))
            return sems[name]

        X = sb("X", [P, KD, T])
        XH = sb("XH", [P, KD, T], F32R)
        XL = sb("XL", [P, KD, T], F32R)
        RAW = sb("RAW", [P, 2, SLOT])
        WH = sb("WH", [P, 2, SLOT], F32R)
        WL = sb("WL", [P, 2, SLOT], F32R)
        gains = sb("gains", [P, NG])
        ident = sb("ident", [P, P])
        ones = sb("ones", [P, P])
        rsb = sb("rsb", [P, T + TT])
        var = sb("var", [P, T + TT])
        sq = sb("sq", [P, 2, T])
        acc = sb("acc", [P, T])
        bank = [ctx.enter_context(nc.psum_tensor(f"bank{i}", [P, 512], F32)) for i in range(8)]
        gate_ps, up_ps, down_ps, norm_ps, misc_ps = bank[0:2], bank[2:4], bank[4:6], bank[6], bank[7]

        with ExitStack() as r:
            AH = sb("AH", [P, KF, T], F32R, r)
            AL = sb("AL", [P, KF, T], F32R, r)
            gs = sb("gs", [P, 2, T], F32, r)
            si = sb("si", [P, 2, T], F32, r)
            au = sb("au", [P, 2, T], F32, r)
            ytok = sb("ytok", [P, TT, D_MODEL], F32, r)
        with ExitStack() as r:
            xtok = sb("xtok", [P, TT, D_MODEL], F32, r)
            grow0 = sb("grow0", [KD, P], F32, r)
            grow = sb("grow", [NG - KD, P], F32, r)

        raw_in = [sem("raw_in0"), sem("raw_in1")]
        hi_done, lo_done, multiplied = sem("hi_done"), sem("lo_done"), sem("multiplied")

        def load(sp, c, s, pieces):
            if not (isinstance(c, int) and c < 2):
                sp.wait_ge(lo_done, c - 1)
            for (lo, hi), src in pieces:
                dst = RAW[:, s, lo:hi].rearrange("p (k n) -> p k n", n=src.shape[2])
                sp.dma_start(dst, src).then_inc(raw_in[s], 16)

        def cuts(s, width):
            if width != KQ * UQ:
                return [(lambda W: W[:, s, 0:width], RAW[:, s, 0:width])]
            raw = RAW[:, s, 0:width].rearrange("p (c n) -> p c n", n=NOPE + ROPE)
            n = 2 * KQ * NOPE
            return [(lambda W: W[:, s, 0:n].rearrange("p (c n) -> p c n", n=NOPE), raw[:, :, 0:NOPE]),
                    (lambda W: W[:, s, n:width].rearrange("p (c n) -> p c n", n=ROPE), raw[:, :, NOPE:])]

        def split_hi(act, c, s, turn, width):
            act.wait_ge(raw_in[s], 32 * turn + 32)
            if not (isinstance(c, int) and c < 2):
                act.wait_ge(multiplied, c - 1)
            for dst, src in cuts(s, width):
                ins = act.activation(dst(WH), src, ACT.Copy)
            ins.then_inc(hi_done, 1)

        def split_lo(dve, c, s, width):
            dve.wait_ge(hi_done, c + 1)
            for dst, src in cuts(s, width):
                ins = dve.tensor_tensor(dst(WL), src, dst(WH).bitcast(F32), ALU.subtract)
            ins.then_inc(lo_done, 1)

        def product(pe, ps, w, k, xh, xl, first, last):
            wh, wl = w(WH, k), w(WL, k)
            pe.matmul(ps, wh, xh, start=first, stop=False)
            pe.matmul(ps, wh, xl, start=False, stop=False)
            return pe.matmul(ps, wl, xh, start=False, stop=last)

        def norm_tile_act(act, s, m, g, base=0):
            act.wait_ge(sem(f"x_ready{s}"), m + (base + 1))
            act.activation(tile(XH, m), tile(X, m), ACT.Copy, scale=g).then_inc(sem("xh"), 1)

        def norm_tile_dve(dve, s, m, g):
            dve.wait_ge(sem("xh"), m + (KD * s + 1))
            dve.scalar_tensor_tensor(tile(XL, m), tile(X, m), g, tile(XH, m).bitcast(F32),
                                     ALU.mult, ALU.subtract).then_inc(sem("xl"), 1)

        def norm_sums_pool(pool, s, base=0):
            pool.wait_ge(sem(f"x_ready{s}"), base + 1)
            pool.tensor_tensor(acc[:, :], X[:, 0, :], X[:, 0, :], ALU.mult).then_inc(sem("acc"), 1)
            with pool.Fori(1, KD) as m:
                pool.wait_ge(sem(f"x_ready{s}"), m + (base + 1))
                pool.wait_ge(sem("acc"), m + KD * s)
                pool.tensor_tensor(sq[:, 0, :], tile(X, m), tile(X, m), ALU.mult).then_inc(sem("sq"), 1)
                pool.wait_ge(sem("sq"), m + (KD - 1) * s)
                pool.tensor_tensor(acc[:, :], acc[:, :], sq[:, 0, :], ALU.add).then_inc(sem("acc"), 1)

        def norm_sum_pe(pe, s, columns=slice(0, T + TT)):
            pe.wait_ge(sem("acc"), KD * (s + 1))
            for t in range(TT):
                mm = pe.matmul(norm_ps[:, T + t:T + t + 1], acc[:, t * P:(t + 1) * P], ones[:, 0:1], start=True, stop=True)
            if columns.start < T:
                mm = pe.matmul(norm_ps[:, 0:T], ones[:, :], acc[:, :], start=True, stop=True)
            mm.then_inc(sem("sum_done"), 1)

        def norm_root_dve(dve, s, columns=slice(0, T + TT)):
            dve.wait_ge(sem("sum_done"), s + 1)
            dve.tensor_scalar(var[:, columns], norm_ps[:, columns], 1.0 / D_MODEL, EPS, ALU.mult, ALU.add)\
               .then_inc(sem("var_done"), 1)
            dve.wait_ge(sem("var_done"), 2 * s + 1)
            dve.reciprocal(var[:, columns], var[:, columns]).then_inc(sem("var_done"), 1)

        def norm_root_act(act, s, columns=slice(0, T + TT)):
            act.wait_ge(sem("var_done"), 2 * s + 2)
            act.activation(rsb[:, columns], var[:, columns], ACT.Sqrt).then_inc(sem("rs"), 1)

        X_HALF = KD // 2

        def gain_rows(name, li):
            src = a[name][li] if li is not None else a[name]
            return src.rearrange("(k p) -> k p", p=P)

        def start_sp(sp, ffn):
            ffn.load_gate(sp, 0, 0)
            sp.dma_start(ident[:, :], a["c_ident"]).then_inc(sem("ident_in"), 16)
            sp.dma_start(grow0[:, :], gain_rows(*GAINS[0])).then_inc(sem("gain0_in"), 16)
            x_tiles = [a["x_prompt"][0, t * P:(t + 1) * P, :] for t in range(SEQ // P)] + [a["x_sample"].rearrange("b s d -> (b s) d")]
            for half in range(2):
                cols = slice(half * D_MODEL // 2, (half + 1) * D_MODEL // 2)
                for t, src in enumerate(x_tiles):
                    sp.dma_start(xtok[:, t, cols], src[:, cols]).then_inc(sem(f"xtok_in{half}"), 16)
            ffn.load_gate(sp, 0, 1)
            row = 0
            for name, li in GAINS[1:]:
                src = gain_rows(name, li)
                sp.dma_start(grow[row:row + src.shape[0], :], src).then_inc(sem("gain_in"), 16)
                row += src.shape[0]

        def start_pe(pe):
            pe.wait_ge(sem("ident_in"), 16)
            pe.wait_ge(sem("gain0_in"), 16)
            pe.transpose(misc_ps[:, 0:KD], grow0[:, :], ident[0:KD, 0:KD]).then_inc(sem("gain_turned"), 1)
            for k in range(KD):
                if k % X_HALF == 0:
                    pe.wait_ge(sem(f"xtok_in{k // X_HALF}"), 16 * TT)
                if k >= 2:
                    pe.wait_ge(sem("x_ready0"), k - 1)
                for t in range(TT):
                    mm = pe.transpose(down_ps[k % 2][:, t * P:(t + 1) * P], xtok[:, t, k * P:(k + 1) * P],
                                      ident[:, :])
                mm.then_inc(sem("x_turned"), 1)
            pe.wait_ge(sem("gain_in"), 16 * len(GAINS[1:]))
            pe.wait_ge(sem("gains_set"), 1)
            pe.transpose(misc_ps[:, 0:NG - KD], grow[:, :], ident[0:NG - KD, 0:NG - KD]).then_inc(sem("gain_turned"), 1)

        def start_act(act):
            split_hi(act, 0, 0, 0, SLOT)
            act.wait_ge(sem("gains_set"), 1)
            for k in range(KD):
                norm_tile_act(act, 0, k, gain(k))
                if k >= 3:
                    act.wait_ge(sem("acc"), k - 1)
                act.activation(sq[:, k % 2, :] if k else acc[:, :], X[:, k, :], ACT.Square)\
                    .then_inc(sem("sq" if k else "acc"), 1)
            split_hi(act, 1, 1, 0, SLOT)
            norm_root_act(act, 0)

        def start_pool(pool):
            pool.memset(ones[:, :], 1.0).then_inc(sem("ones_set"), 1)
            for k in range(1, KD):
                pool.wait_ge(sem("sq"), k)
                pool.wait_ge(sem("acc"), k)
                pool.tensor_tensor(acc[:, :], acc[:, :], sq[:, k % 2, :], ALU.add).then_inc(sem("acc"), 1)

        def start_dve(dve):
            split_lo(dve, 0, 0, SLOT)
            dve.wait_ge(sem("gain_turned"), 1)
            dve.tensor_copy(gains[:, 0:KD], misc_ps[:, 0:KD]).then_inc(sem("gains_set"), 1)
            for k in range(KD + 1):
                if k < KD:
                    dve.wait_ge(sem("x_turned"), k + 1)
                    dve.tensor_copy(X[:, k, :], down_ps[k % 2][:, 0:T]).then_inc(sem("x_ready0"), 1)
                if k >= 1:
                    norm_tile_dve(dve, 0, k - 1, gain(k - 1))
            split_lo(dve, 1, 1, SLOT)
            dve.wait_ge(sem("gain_turned"), 2)
            dve.tensor_copy(gains[:, KD:NG], misc_ps[:, 0:NG - KD]).then_inc(sem("gains_set"), 1)
            norm_root_dve(dve, 0)

        class Ffn:
            def __init__(self, f, li, which, s, c0, next_widths):
                self.f, self.s, self.c0, self.c1 = f, s, c0, c0 + KF
                self.last = s + 1 == N_NORMS - 1
                self.wg = a[f"w_ffn{which}_gate"][li].rearrange("(k p) n -> p k n", p=P)
                self.wu = a[f"w_ffn{which}_up"][li].rearrange("(k p) n -> p k n", p=P)
                self.wd = a[f"w_ffn{which}_down"][li].rearrange("(k p) n -> p k n", p=P)
                self.next_widths = next_widths
                self.n0 = f * KF
                self.gate_done, self.scaled = sem("gate_done"), sem("gate_scaled")
                self.silu_done, self.act_done = sem("silu_done"), sem("act_done")
                self.ah_done, self.al_done, self.silu_scaled = sem("ah_done"), sem("al_done"), sem("silu_scaled")
                self.x_ready = sem(f"x_ready{s + 1}")

            def slot(self, c):
                return c % 2

            def load_gate(self, sp, i, j):
                cols = bass.ds((2 * i + j) * P, P)
                load(sp, self.c0 + j + 2 * i, (self.c0 + j) % 2, [((0, KD * P), self.wg[:, :, cols]),
                                                                  ((KD * P, 2 * KD * P), self.wu[:, :, cols])])

            def sp(self, sp):
                first = 1 if self.c0 == 0 else 0
                with sp.Fori(first, KF // 2) as i:
                    self.load_gate(sp, i, 0)
                    self.load_gate(sp, i, 1)
                with sp.Fori(0, KD) as m:
                    for j in (0, 1):
                        c = self.c1 + j + 2 * m
                        k0, k1 = j * HALF, j * HALF + HALF // 2
                        cols = bass.ds(m * P, P)
                        load(sp, c, (self.c1 + j) % 2,
                             [((0, HALF // 2 * P), self.wd[:, k0:k1, cols]),
                              ((HALF // 2 * P, HALF * P), self.wd[:, k1:k0 + HALF, cols])])

            def pe(self, pe):
                def gate_pair(i, first):
                    for j in (0, 1):
                        s = (self.c0 + j) % 2
                        pe.wait_ge(lo_done, self.c0 + j + 2 * i + 1)
                        for part, ps in ((0, gate_ps[j]), (1, up_ps[j])):
                            if not first:
                                pe.wait_ge(self.act_done if part else self.scaled, 2 * i + (self.n0 + j - 1))

                            def w(W, k):
                                at = (part * KD + k) * P
                                return W[:, s, at:at + P]
                            for k in range(KD):
                                if first and j == 0 and part == 0:
                                    pe.wait_ge(sem("xl"), KD * self.s + k + 1)
                                mm = product(pe, ps[:, 0:T], w, k, XH[:, k, :], XL[:, k, :], k == 0, k == KD - 1)
                            mm.then_inc(multiplied if part else self.gate_done, 1)
                            if first and j == 0 and part == 0:
                                norm_sum_pe(pe, self.s)
                gate_pair(0, True)
                with pe.Fori(1, KF // 2) as i:
                    gate_pair(i, False)

                def down_pair(i, first):
                    for mm_ in (0, 1):
                        for j in (0, 1):
                            s = (self.c1 + j) % 2
                            pe.wait_ge(lo_done, self.c1 + j + 2 * mm_ + 4 * i + 1)
                            if j == 0 and not first:
                                pe.wait_ge(self.x_ready, 2 * i + (mm_ - 1))

                            def w(W, k):
                                return W[:, s, k * P:(k + 1) * P]
                            for k in range(HALF):
                                kk = j * HALF + k
                                if first and mm_ == 0:
                                    pe.wait_ge(self.al_done, self.n0 + kk + 1)
                                mm = product(pe, down_ps[mm_][:, 0:T], w, k, AH[:, kk, :], AL[:, kk, :],
                                             kk == 0, kk == KF - 1)
                            mm.then_inc(multiplied, 1)
                        if self.last and not (first and mm_ == 0):
                            turn_y(pe, 2 * i + mm_ - 1, 1 - mm_)
                down_pair(0, True)
                with pe.Fori(1, KD // 2) as i:
                    down_pair(i, False)

            def act(self, act):
                def gate_pair(i, widths):
                    for j in (0, 1):
                        n = 2 * i + j
                        act.wait_ge(self.scaled, n + (self.n0 + 1))
                        act.activation(si[:, j, :], gs[:, j, :], ACT.Silu).then_inc(self.silu_done, 1)
                        split_hi(act, self.c0 + 2 + j + 2 * i, (self.c0 + j) % 2, (self.c0 + j) // 2 + 1 + i, widths[j])
                        act.wait_ge(self.act_done, n + (self.n0 + 1))
                        act.activation(tile(AH, n), au[:, j, :], ACT.Copy).then_inc(self.ah_done, 1)
                with act.Fori(0, KF // 2 - 1) as i:
                    gate_pair(i, (SLOT, SLOT))
                gate_pair(KF // 2 - 1, (HALF * P, HALF * P))

                def split(m, j, width):
                    if width:
                        split_hi(act, self.c1 + 2 + j + 2 * m, (self.c1 + j) % 2, (self.c1 + j) // 2 + 1 + m, width)

                def normalise(m):
                    norm_tile_act(act, self.s + 1, m, gain(m + KD * (self.s + 1)))

                if self.last:
                    for m in range(KD):
                        if m < KD - 1:
                            split(m, 0, HALF * P)
                            split(m, 1, HALF * P)
                        gain_y(act, m)
                        if m >= 1:
                            take_y(act, m - 1)
                    return
                with act.Fori(0, KD - 1) as m:
                    split(m, 0, HALF * P)
                    split(m, 1, HALF * P)
                    normalise(m)
                split(KD - 1, 0, self.next_widths[0])
                normalise(KD - 1)
                split(KD - 1, 1, self.next_widths[1])
                norm_root_act(act, self.s + 1)

            def dve(self, dve):
                def gate_pair(i, widths):
                    for j in (0, 1):
                        n, c = 2 * i + j, self.c0 + j + 2 * i
                        dve.wait_ge(self.gate_done, n + (self.n0 + 1))
                        if isinstance(i, int) and i == 0 and j == 0:
                            dve.wait_ge(sem("rs"), self.s + 1)
                        dve.tensor_tensor(gs[:, j, :], gate_ps[j][:, 0:T], rsb[:, 0:T], ALU.mult).then_inc(self.scaled, 1)
                        dve.wait_ge(self.silu_scaled, n + (self.n0 + 1))
                        dve.wait_ge(multiplied, c + 1)
                        dve.tensor_tensor(au[:, j, :], up_ps[j][:, 0:T], si[:, j, :], ALU.mult).then_inc(self.act_done, 1)
                        split_lo(dve, c + 2, (self.c0 + j) % 2, widths[j])
                        dve.wait_ge(self.ah_done, n + (self.n0 + 1))
                        dve.tensor_tensor(tile(AL, n), au[:, j, :], tile(AH, n).bitcast(F32), ALU.subtract).then_inc(self.al_done, 1)
                dve.wait_ge(sem("rs"), self.s + 1)
                with dve.Fori(0, KF // 2 - 1) as i:
                    gate_pair(i, (SLOT, SLOT))
                gate_pair(KF // 2 - 1, (HALF * P, HALF * P))

                def down(m, widths):
                    c = self.c1 + 2 * m
                    if widths[0]:
                        split_lo(dve, c + 2, self.c1 % 2, widths[0])
                    dve.wait_ge(multiplied, c + 2)
                    return c

                def down_pair(i, widths):
                    for q in (0, 1):
                        m = 2 * i + q
                        c = down(m, widths[q])
                        dve.scalar_tensor_tensor(tile(X, m), down_ps[q][:, 0:T], 0.5, tile(X, m), ALU.mult, ALU.add)\
                           .then_inc(self.x_ready, 1)
                        last = isinstance(m, int) and m == KD - 1
                        if not last:
                            split_lo(dve, c + 3, (self.c1 + 1) % 2, widths[q][1])
                        if not self.last:
                            norm_tile_dve(dve, self.s + 1, m, gain(m + KD * (self.s + 1)))
                        if last and widths[q][1]:
                            split_lo(dve, c + 3, (self.c1 + 1) % 2, widths[q][1])
                w = (HALF * P, HALF * P)
                with dve.Fori(0, KD // 2 - 1) as i:
                    down_pair(i, (w, w))
                down_pair(KD // 2 - 1, (w, self.next_widths))
                if not self.last:
                    norm_root_dve(dve, self.s + 1)

            def pool(self, pool):
                pool.wait_ge(sem("rs"), self.s + 1)
                with pool.Fori(0, KF // 2) as i:
                    for j in (0, 1):
                        pool.wait_ge(self.silu_done, 2 * i + (self.n0 + j + 1))
                        pool.tensor_tensor(si[:, j, :], si[:, j, :], rsb[:, 0:T], ALU.mult).then_inc(self.silu_scaled, 1)
                norm_sums_pool(pool, self.s + 1)

        TOKEN_COLUMNS = slice(T, T + TT)

        def gain_y(act, m):
            act.wait_ge(sem(f"x_ready{N_NORMS - 1}"), m + 1)
            act.activation(gs[:, m % 2, :], X[:, m, :], ACT.Copy, scale=gain(FINAL_GAIN + m)).then_inc(sem("y_gained"), 1)

        def turn_y(pe, m, slot):
            pe.wait_ge(sem("y_gained"), m + 1)
            if not isinstance(m, int) or m >= 2:
                pe.wait_ge(sem("y_taken"), m - 1)
            for t in range(TT):
                mm = pe.transpose(gate_ps[slot][:, t * P:(t + 1) * P], gs[:, slot, t * P:(t + 1) * P], ident[:, :])
            mm.then_inc(sem("y_turned"), 1)

        def take_y(act, m):
            act.wait_ge(sem("y_turned"), m + 1)
            act.activation(ytok[:, :, m * P:(m + 1) * P],
                           gate_ps[m % 2][:, 0:T].rearrange("p (t n) -> p t n", n=P), ACT.Copy).then_inc(sem("y_taken"), 1)

        def end_pe(pe):
            turn_y(pe, KD - 1, (KD - 1) % 2)
            norm_sum_pe(pe, N_NORMS - 1, TOKEN_COLUMNS)

        def end_act(act):
            take_y(act, KD - 1)
            norm_root_act(act, N_NORMS - 1, TOKEN_COLUMNS)
            act.wait_ge(sem("rs"), N_NORMS)
            act.activation(ytok[:, 1, :], ytok[:, 1, :], ACT.Copy, scale=rsb[:, T + 1:T + 2]).then_inc(sem("y_done1"), 1)

        def end_dve(dve):
            norm_root_dve(dve, N_NORMS - 1, TOKEN_COLUMNS)
            dve.wait_ge(sem("y_taken"), KD)
            dve.wait_ge(sem("rs"), N_NORMS)
            for t in (0, 2):
                dve.tensor_scalar(ytok[:, t, :], ytok[:, t, :], rsb[:, T + t:T + t + 1], None, ALU.mult).then_inc(sem("y_done0"), 1)

        def end_sp(sp):
            for t in range(TT):
                sp.wait_ge(sem(f"y_done{t % 2}"), t // 2 + 1)
                dst = out["y_prompt"][0, t * P:(t + 1) * P, :] if t < SEQ // P else \
                    out["y_sample"].rearrange("b s d -> (b s) d")
                sp.dma_start(dst, ytok[:, t, :]).then_inc(sem("stored"), 16)

        NP = SEQ // QBLK
        SC = NP * (NP + 1) // 2 * QBLK
        NC = PAST_LEN // P
        HQ = MLA_HEADS * DEC_SEQ
        PAST, NEW = slice(0, PAST_LEN), slice(PAST_LEN, PAST_LEN + P)
        LR = KV_LORA + ROPE
        with ExitStack() as r:
            mtab = sb("mtab", [P, P + 2 * T], F32, r)
            rot, mcos, msin = mtab[:, 0:P], mtab[:, P:P + T], mtab[:, P + T:P + 2 * T]
            mask_q = sb("mask_q", [1, P], F32, r)
            mask_k = sb("mask_k", [1, CHUNK], F32, r)
            qn = sb("qn", [P, MLA_HEADS, T], F32, r)
            qp = sb("qp", [ROPE, MLA_HEADS, T], F32, r)
            ckvT = sb("ckvT", [P, KV, T], F32, r)
            kpT = sb("kpT", [ROPE, T], F32, r)
            tok = sb("tok", [P, TT, LR], F32, r)
            wuk = sb("wuk", [P, KV, D_MODEL], F32, r)
            wuv = sb("wuv", [P, KV, D_MODEL], F32, r)
            wukT = sb("wukT", [P, MLA_HEADS, KV_LORA], F32, r)
            qps = sb("qps", [ROPE, DEC_BATCH, MLA_HEADS, DEC_SEQ], F32, r)
            lat = sb("lat", [P, KV, DEC_BATCH, MLA_HEADS, DEC_SEQ], F32, r)
            with ExitStack() as r1:
                cq = sb("cq", [P, KQ, T], F32, r1)
                cqh = sb("cqh", [P, KQ, T], F32R, r1)
                cql = sb("cql", [P, KQ, T], F32R, r1)
                ckv = sb("ckv", [P, KV, T], F32, r1)
                pe_raw = sb("pe_raw", [P, T], F32, r1)
                pe_cos = sb("pe_cos", [P, T], F32, r1)
                pe_sin = sb("pe_sin", [P, T], F32, r1)
                rq = sb("rq", [P, T], F32, r1)
                rkv = sb("rkv", [P, T], F32, r1)
                acc_q = sb("acc_q", [P, T], F32, r1)
                acc_kv = sb("acc_kv", [P, T], F32, r1)
            with ExitStack() as r2:
                NCB = 4
                cc = sb("cc", [P, NCB, NC, KV_LORA], F32, r2)
                cp = sb("cp", [P, NCB, NC, ROPE], F32, r2)
                stat = sb("stat", [P, 2, 8], F32, r2)
                with ExitStack() as r3:
                    val = sb("val", [P, NP, D_MODEL], F32, r3)
                    kn = sb("kn", [P, 2, SEQ], F32, r3)
                    pr = sb("pr", [P, 2, SC], F32, r3)
                    prT = sb("prT", [P, 2, SC], F32, r3)
                with ExitStack() as r3:
                    kt = sb("kt", [P, 2, KV + 1, PAST_LEN], F32, r3)
                    ps_ = sb("ps_", [P, 2, PAST_LEN + P], F32, r3)
                    psT = sb("psT", [P, 2, PAST_LEN + P], F32, r3)

        class Mla:
            N_CHUNKS = 7 + KD // 2

            def __init__(self, s, c0, next_widths):
                self.s, self.c0 = s, c0
                self.widths = [SLOT] * 3 + [KQ * UQ] * 4 + [SLOT] * (KD // 2) + list(next_widths)

            def look_act(self, act, q):
                c = self.c0 + q + 2
                if self.widths[q + 2]:
                    split_hi(act, c, c % 2, c // 2, self.widths[q + 2])

            def look_dve(self, dve, q):
                if self.widths[q + 2]:
                    split_lo(dve, self.c0 + q + 2, (self.c0 + q) % 2, self.widths[q + 2])

            def sp(self, sp):
                wdq = a["w_dq"][0].rearrange("(k p) n -> p k n", p=P)
                wdkv = a["w_dkv"][0].rearrange("(k p) n -> p k n", p=P)
                wuq = a["w_uq"][0].rearrange("(k p) n -> p k n", p=P)
                wo = a["w_o_mla"][0].rearrange("(k p) n -> p k n", p=P)
                first, second = (0, KD * P), (KD * P, 2 * KD * P)
                c = self.c0
                load(sp, c, c % 2, [(first, wdq[:, :, 0:P]), (second, wdq[:, :, P:2 * P])])
                load(sp, c + 1, (c + 1) % 2, [(first, wdq[:, :, 2 * P:3 * P]), (second, wdkv[:, :, 0:P])])
                sp.wait_ge(multiplied, c)
                sp.dma_start(mtab[:, :], a["c_mla"]).then_inc(sem("mtab_in"), 16)
                load(sp, c + 2, c % 2, [(first, wdkv[:, :, P:2 * P]), (second, wdkv[:, :, LR - P:LR])])
                for g in range(4):
                    load(sp, c + 3 + g, (c + 3 + g) % 2, [((0, 2 * UQ), wuq[:, 0:2, g * UQ:(g + 1) * UQ]),
                                                          ((2 * UQ, 3 * UQ), wuq[:, 2:3, g * UQ:(g + 1) * UQ])])
                sp.dma_start(wuk[:, :, :], a["w_uk"][0].rearrange("(k p) h n -> p k (h n)", p=P)).then_inc(sem("wuk_in"), 16)
                sp.dma_start(wuv[:, :, :], a["w_uv"][0].rearrange("(k p) h n -> p k (h n)", p=P)).then_inc(sem("wuv_in"), 16)
                for g in range(KD // 2):
                    load(sp, c + 7 + g, (c + 7 + g) % 2, [(first, wo[:, :, 2 * g * P:(2 * g + 1) * P]),
                                                          (second, wo[:, :, (2 * g + 1) * P:(2 * g + 2) * P])])
                self.sp_attention(sp)

            def sp_attention(self, sp):
                sp.wait_ge(multiplied, self.c0 + 7)
                sp.wait_ge(sem("m_rope"), 3 + 3 * 4)
                for b in range(DEC_BATCH):
                    if b == NCB:
                        for t in range(TT):
                            sp.wait_ge(sem("m_tok"), t + 1)
                            for o, n, lo, hi in (("ckv", KV_LORA, 0, KV_LORA), ("kpe", ROPE, KV_LORA, LR)):
                                if t < SEQ // P:
                                    dst = out[f"new_{o}_prompt"][0, 0, t * P:(t + 1) * P, :]
                                else:
                                    dst = out[f"new_{o}_sample"][0].rearrange("b s d -> (b s) d")
                                sp.dma_start(dst, tok[:, t, lo:hi]).then_inc(sem("stored"), 16)
                    if b >= NCB:
                        sp.wait_ge(sem("m_olat"), b - NCB + 1)
                    sp.dma_start(cc[:, b % NCB, :, :],
                                 a["cache_ckv"][0, b].rearrange("(p k) d -> p k d", k=NC)).then_inc(sem(f"cc_in{b % NCB}"), 16)
                    sp.dma_start(cp[:, b % NCB, :, :],
                                 a["cache_kpe"][0, b].rearrange("(p k) d -> p k d", k=NC)).then_inc(sem(f"cc_in{b % NCB}"), 16)

            def pe(self, pe):
                c0 = self.c0

                def projection(q, k_tiles, xh, xl, at, ready, before_last=None):
                    s = (c0 + q) % 2
                    pe.wait_ge(lo_done, c0 + q + 1)
                    banks = (gate_ps[q % 2], up_ps[q % 2])
                    for part, ps in enumerate(banks):
                        if part and before_last:
                            before_last()

                        def w(W, k):
                            return at(W[:, s, :], part, k)
                        for k in range(k_tiles):
                            if ready and part == 0:
                                pe.wait_ge(sem("xl"), KD * self.s + k + 1)
                            mm = product(pe, ps[:, 0:T], w, k, xh[:, k, :], xl[:, k, :], k == 0, k == k_tiles - 1)
                        mm.then_inc(multiplied if part else sem("m_part0"), 1)

                def two(W, part, k):
                    return W[:, (part * KD + k) * P:(part * KD + k + 1) * P]

                projection(0, KD, XH, XL, two, True, lambda: norm_sum_pe(pe, self.s))
                projection(1, KD, XH, XL, two, False)

                def q_sum():
                    pe.wait_ge(sem("m_acc_q"), KQ)
                    pe.matmul(norm_ps[:, 0:T], ones[:, :], acc_q[:, :], start=True, stop=True).then_inc(sem("m_ssq"), 1)
                pe.wait_ge(sem("m_proj"), 2)
                projection(2, KD, XH, XL, two, False, q_sum)

                def rotate(n):
                    pe.wait_ge(sem("m_proj"), 6 + 3 * n)
                    if n == 0:
                        pe.wait_ge(sem("mtab_in"), 16)
                    if n >= 1:
                        pe.wait_ge(sem("m_turn_read"), n)
                    pe.matmul(misc_ps[:, 0:T], rot, pe_raw[:, :], start=True, stop=True).then_inc(sem("m_turned"), 1)

                for g in range(4):
                    q, s = 3 + g, (c0 + 3 + g) % 2
                    pe.wait_ge(lo_done, c0 + q + 1)
                    for part in range(3):
                        ps = (gate_ps, up_ps, down_ps)[part][q % 2]

                        def w(Wt, k):
                            lo = (2 * k + part if part < 2 else 2 * KQ + k) * P
                            return Wt[:, s, lo:lo + P]
                        pe.wait_ge(sem("m_proj"), self.proj_before(g, part))
                        if part == 1:
                            rotate(g)
                        if part == 1 and g == 0:
                            pe.wait_ge(sem("m_acc_kv"), KV)
                            pe.wait_ge(sem("m_var_q"), 1)
                            pe.matmul(norm_ps[:, 0:T], ones[:, :], acc_kv[:, :], start=True, stop=True).then_inc(sem("m_sskv"), 1)
                        for k in range(KQ):
                            if g == 0 and part == 0:
                                pe.wait_ge(sem("m_cql"), k + 1)
                            mm = product(pe, ps[:, 0:T], w, k, cqh[:, k, :], cql[:, k, :], k == 0, k == KQ - 1)
                        mm.then_inc(multiplied if part == 2 else sem("m_part0"), 1)
                rotate(4)
                self.pe_prompt(pe)
                self.pe_sample(pe)

                for g in range(KD // 2):
                    q = 7 + g
                    pe.wait_ge(lo_done, c0 + q + 1)
                    s = (c0 + q) % 2
                    if g >= 2:
                        pe.wait_ge(sem(f"x_ready{self.s + 1}"), 2 * g - 2)
                    for part, ps in enumerate((gate_ps[g % 2], up_ps[g % 2])):
                        def w(W, k):
                            return two(W[:, s, :], part, k)
                        for k in range(KD):
                            if g == 0 and part == 0:
                                pe.wait_ge(sem("m_ol"), MLA_HEADS + k // 4 + 1)
                            mm = product(pe, ps[:, 0:T], w, k, XH[:, k, :], XL[:, k, :], k == 0, k == KD - 1)
                        mm.then_inc(multiplied if part else sem("m_o_part0"), 1)

            def proj_before(self, g, part):
                if g == 0:
                    return (3, 4, 1)[part]
                if g == 1:
                    return (5, 6, 1)[part]
                return 6 + 3 * (g - 2) + part + 1

            def pe_prompt(self, pe):
                pe.wait_ge(sem("wuk_in"), 16)
                pe.wait_ge(sem("wuv_in"), 16)
                pe.wait_ge(sem("m_proj"), 6 + 12)
                for i, ps in enumerate((gate_ps[0], gate_ps[1], up_ps[0], up_ps[1])):
                    for e in range(2):
                        for t in range(KV):
                            h = 2 * i + e
                            mm = pe.transpose(ps[:, (e * KV + t) * P:(e * KV + t + 1) * P],
                                              wuk[:, t, h * P:(h + 1) * P], ident[:, :])
                    mm.then_inc(sem("m_wukT"), 1)
                pe.wait_ge(sem("m_ckvT"), KV)
                pe.wait_ge(sem("m_rope"), 3)
                for i, ps in enumerate((down_ps[0], down_ps[1], norm_ps, misc_ps)):
                    kt_, half = i // 2, i % 2
                    if i == 3:
                        pe.wait_ge(sem("m_turn_read"), 5)
                    for t in range(KV):
                        mm = pe.matmul(ps[:, 0:512], ckvT[:, t, kt_ * P:(kt_ + 1) * P],
                                       wuv[:, t, half * 512:(half + 1) * 512], start=(t == 0), stop=(t == KV - 1))
                    mm.then_inc(sem("m_val"), 1)
                for t in range(TT):
                    ps = down_ps[t % 2]
                    pe.wait_ge(sem("m_val_out"), t + 1 if t < 2 else 2)
                    if t == 2:
                        pe.wait_ge(sem("m_tok"), 1)
                    for k in range(KV):
                        pe.transpose(ps[:, k * P:(k + 1) * P], ckvT[:, k, t * P:(t + 1) * P], ident[:, :])
                    pe.transpose(ps[:, KV_LORA:LR], kpT[:, t * P:(t + 1) * P], ident[0:ROPE, 0:ROPE]).then_inc(sem("m_tok_turned"), 1)

                def keys(h):
                    if h == 0:
                        pe.wait_ge(sem("m_wukT_out"), 4)
                    if h >= 2:
                        pe.wait_ge(sem("m_kn"), h - 1)
                    for t in range(KV):
                        mm = pe.matmul(gate_ps[h % 2][:, 0:SEQ], wuk[:, t, h * P:(h + 1) * P], ckvT[:, t, 0:SEQ],
                                       start=(t == 0), stop=(t == KV - 1))
                    mm.then_inc(sem("m_keys"), 1)

                def scores(h):
                    pe.wait_ge(sem("m_kn"), h + 1)
                    if h == 0:
                        pe.wait_ge(sem("m_mask"), 3)
                        pe.wait_ge(sem("m_rope"), 3 + 3 * 4)
                    if h >= 2:
                        pe.wait_ge(sem("m_exp"), 2 * (h - 1))
                    ps = up_ps[h % 2]
                    at = 0
                    for blk in range(NP):
                        n, q0 = (blk + 1) * QBLK, blk * QBLK
                        pe.matmul(ps[:, at:at + n], qn[:, h, q0:q0 + QBLK], kn[:, h % 2, 0:n], start=True, stop=False)
                        pe.matmul(ps[:, at + n - CHUNK:at + n], mask_q[:, :], mask_k[:, :], start=False, stop=False,
                                  skip_group_check=True)
                        mm = pe.matmul(ps[:, at:at + n], qp[:, h, q0:q0 + QBLK], kpT[:, 0:n], start=False, stop=True)
                        at += n
                    mm.then_inc(sem("m_scores"), 1)

                def turn(h):
                    pe.wait_ge(sem("m_pr"), 2 * (h + 1))
                    if h < 2:
                        pe.wait_ge(sem("m_tok"), TT)
                    if h >= 2:
                        pe.wait_ge(sem("m_prT"), h - 1)
                    for i in range(SC // P):
                        mm = pe.transpose(down_ps[h % 2][:, i * P:(i + 1) * P], pr[:, h % 2, i * P:(i + 1) * P], ident[:, :])
                    mm.then_inc(sem("m_prTurned"), 1)

                def mix(h):
                    ps = (norm_ps, misc_ps)[h % 2]
                    pe.wait_ge(sem("m_prT"), h + 1)
                    if h < 2:
                        pe.wait_ge(sem("m_val_out"), 4)
                    if h >= 2:
                        pe.wait_ge(sem("m_ol"), h - 1)
                    at = 0
                    for blk in range(NP):
                        for k in range(blk + 1):
                            mm = pe.matmul(ps[:, blk * QBLK:(blk + 1) * QBLK], val[:, k, h * P:(h + 1) * P],
                                           prT[:, h % 2, at:at + P], start=(k == 0), stop=(k == blk))
                            at += P
                    mm.then_inc(sem("m_mixed"), 1)

                def sample_queries(i):
                    ps = (gate_ps[0], gate_ps[1], up_ps[0], up_ps[1])[i]
                    if i == 0:
                        pe.wait_ge(sem("m_kn"), MLA_HEADS)
                    if i == 2:
                        pe.wait_ge(sem("m_exp"), 2 * MLA_HEADS)
                    for t in range(KV):
                        for e in range(2):
                            h = 2 * i + e
                            mm = pe.matmul(ps[:, (t * 2 + e) * P:(t * 2 + e + 1) * P], wukT[:, h, t * P:(t + 1) * P],
                                           qn[:, h, SEQ:T], start=True, stop=True)
                    mm.then_inc(sem("m_qlat"), 1)

                for i in range(MLA_HEADS + 3):
                    if i < MLA_HEADS:
                        keys(i)
                    elif i > MLA_HEADS:
                        sample_queries(2 * (i - MLA_HEADS - 1))
                        sample_queries(2 * (i - MLA_HEADS - 1) + 1)
                    if 0 <= i - 3:
                        mix(i - 3)
                    if 0 <= i - 1 < MLA_HEADS:
                        scores(i - 1)
                    if 0 <= i - 2 < MLA_HEADS:
                        turn(i - 2)

            def pe_sample(self, pe):
                def turn_cache(b):
                    pe.wait_ge(sem(f"cc_in{b % NCB}"), 32 * (b // NCB + 1))
                    if b == 0:
                        pe.wait_ge(sem("m_lat"), 4 * KV)
                    if b >= 1:
                        pe.wait_ge(sem("m_kt_act"), 2 * b)
                        pe.wait_ge(sem("m_kt_dve"), b)
                    for t, ps in enumerate((gate_ps[0], gate_ps[1], up_ps[0])):
                        for k in range(NC):
                            if t < KV:
                                mm = pe.transpose(ps[:, k * P:(k + 1) * P], cc[:, b % NCB, k, t * P:(t + 1) * P], ident[:, :])
                            else:
                                mm = pe.transpose(ps[0:ROPE, k * P:(k + 1) * P], cp[:, b % NCB, k, :], ident[:, :])
                        mm.then_inc(sem("m_cturned"), 1)

                def scores(b):
                    pe.wait_ge(sem("m_kt_act"), 2 * (b + 1))
                    pe.wait_ge(sem("m_kt_dve"), b + 1)
                    if b == 0:
                        pe.wait_ge(sem("m_qps"), 1)
                        pe.wait_ge(sem("m_prT"), MLA_HEADS)
                    if b >= 1:
                        pe.wait_ge(sem("m_sexp"), 2 * b)
                    new = slice(SEQ + b * DEC_SEQ, SEQ + (b + 1) * DEC_SEQ)
                    for ps, n, ks in ((up_ps[1], PAST_LEN, [kt[:, b % 2, 0, :], kt[:, b % 2, 1, :], kt[0:ROPE, b % 2, 2, :]]),
                                      (down_ps[0], DEC_SEQ, [ckvT[:, 0, new], ckvT[:, 1, new], kpT[:, new]])):
                        qs = [x.rearrange("p h q -> p (h q)") for x in (lat[:, 0, b, :, :], lat[:, 1, b, :, :], qps[:, b, :, :])]
                        for i in range(3):
                            mm = pe.matmul(ps[:, 0:n], qs[i], ks[i], start=(i == 0), stop=(i == 2))
                    mm.then_inc(sem("m_sscores"), 1)

                def turn(b):
                    pe.wait_ge(sem("m_ps"), b + 1)
                    if b == 0:
                        pe.wait_ge(sem("m_ol"), MLA_HEADS)
                    if b >= 1:
                        pe.wait_ge(sem("m_psT"), 2 * b)
                    for k in range(NC + 1):
                        ps = down_ps[1][:, k * P:(k + 1) * P] if k < NC else norm_ps[:, 0:P]
                        mm = pe.transpose(ps, ps_[:, b % 2, k * P:(k + 1) * P], ident[:, :])
                    mm.then_inc(sem("m_psTurned"), 1)

                def mix(b):
                    pe.wait_ge(sem("m_psT"), 2 * (b + 1))
                    if b >= 1:
                        pe.wait_ge(sem("m_olat"), b)
                    for t in range(KV):
                        for k in range(NC + 1):
                            lhs = cc[:, b % NCB, k, t * P:(t + 1) * P] if k < NC else tok[:, TT - 1, t * P:(t + 1) * P]
                            mm = pe.matmul(misc_ps[:, t * P:(t + 1) * P], lhs, psT[:, b % 2, k * P:(k + 1) * P],
                                           start=(k == 0), stop=(k == NC))
                    mm.then_inc(sem("m_smixed"), 1)

                for i in range(DEC_BATCH + 2):
                    if i >= 2:
                        turn(i - 2)
                    if 0 <= i - 1 < DEC_BATCH:
                        scores(i - 1)
                    if i < DEC_BATCH:
                        turn_cache(i)
                    if i >= 2:
                        mix(i - 2)
                pe.wait_ge(sem("m_olat"), DEC_BATCH)
                for i, ps in enumerate(down_ps):
                    for e in range(4):
                        h = 4 * i + e
                        for t in range(KV):
                            mm = pe.matmul(ps[:, e * P:(e + 1) * P], wuv[:, t, h * P:(h + 1) * P], lat[:, t, :, h, :],
                                           start=(t == 0), stop=(t == KV - 1))
                    mm.then_inc(sem("m_vout"), 1)

            def act(self, act):
                for q in range(3):
                    if q == 2:
                        act.wait_ge(sem("m_var_q"), 2)
                        act.activation(rq[:, :], var[:, 0:T], ACT.Sqrt).then_inc(sem("m_rq"), 1)
                    self.look_act(act, q)
                    for t in ((0, 1), (2,), ())[q]:
                        act.wait_ge(sem("m_proj"), t + 1)
                        act.activation(cqh[:, t, :], cq[:, t, :], ACT.Copy, scale=gain(Q_GAIN + t)).then_inc(sem("m_cqh"), 1)
                for q in range(3, 7):
                    self.look_act(act, q)
                    if q == 3:
                        act.wait_ge(sem("m_var_kv"), 2)
                        act.activation(rkv[:, :], var[:, 0:T], ACT.Sqrt).then_inc(sem("m_rkv"), 1)
                for i, ps in enumerate((gate_ps[0], gate_ps[1], up_ps[0], up_ps[1])):
                    act.wait_ge(sem("m_wukT"), i + 1)
                    act.activation(wukT[:, 2 * i:2 * i + 2, :].rearrange("p h n -> p (h n)"), ps[:, :], ACT.Copy).then_inc(sem("m_wukT_out"), 1)
                act.wait_ge(sem("m_rope"), 3 + 3 * 4)
                for i, ps in enumerate((down_ps[0], down_ps[1], norm_ps, misc_ps)):
                    act.wait_ge(sem("m_val"), i + 1)
                    act.activation(val[:, i // 2, (i % 2) * 512:(i % 2 + 1) * 512], ps[:, :], ACT.Copy).then_inc(sem("m_val_out"), 1)
                for t in range(TT):
                    act.wait_ge(sem("m_tok_turned"), t + 1)
                    act.activation(tok[:, t, :], down_ps[t % 2][:, 0:LR], ACT.Copy).then_inc(sem("m_tok"), 1)

                def sample_queries(i):
                    act.wait_ge(sem("m_qlat"), i + 1)
                    ps = (gate_ps[0], gate_ps[1], up_ps[0], up_ps[1])[i]
                    for t in range(KV):
                        act.activation(lat[:, t, :, 2 * i:2 * i + 2, :].rearrange("p b e q -> p e b q"),
                                       ps[:, t * 2 * P:(t + 1) * 2 * P].rearrange("p (e b q) -> p e b q", e=2, b=DEC_BATCH),
                                       ACT.Copy).then_inc(sem("m_lat"), 1)

                for i in range(MLA_HEADS + 3):
                    if i == MLA_HEADS + 2:
                        for j in range(4):
                            sample_queries(j)
                    if i < MLA_HEADS:
                        act.wait_ge(sem("m_keys"), i + 1)
                        if i >= 2:
                            act.wait_ge(sem("m_scores"), i - 1)
                        act.activation(kn[:, i % 2, :], gate_ps[i % 2][:, 0:SEQ], ACT.Copy).then_inc(sem("m_kn"), 1)
                    h = i - 3
                    if h >= 0:
                        act.wait_ge(sem("m_mixed"), h + 1)
                        act.activation(XH[:, h, 0:SEQ], (norm_ps, misc_ps)[h % 2][:, 0:SEQ], ACT.Copy).then_inc(sem("m_oh"), 1)
                    h = i - 2
                    if 0 <= h < MLA_HEADS:
                        act.wait_ge(sem("m_prTurned"), h + 1)
                        if h >= 2:
                            act.wait_ge(sem("m_mixed"), h - 1)
                        act.activation(prT[:, h % 2, :], down_ps[h % 2][:, 0:SC], ACT.Copy).then_inc(sem("m_prT"), 1)
                    h = i - 1
                    if 0 <= h < MLA_HEADS:
                        act.wait_ge(sem("m_negmax"), h + 1)
                        if h >= 2:
                            act.wait_ge(sem("m_prTurned"), h - 1)
                        at = 0
                        for blk in range(NP):
                            n = (blk + 1) * QBLK
                            act.activation(pr[:, h % 2, at:at + n], up_ps[h % 2][:, at:at + n], ACT.Exp,
                                           bias=stat[:, h % 2, 2 + blk:3 + blk], scale=MLA_SCALE,
                                           accum_out=stat[:, h % 2, 4 + blk:5 + blk]).then_inc(sem("m_exp"), 1)
                            at += n

                for i in range(DEC_BATCH + 2):
                    b = i - 2
                    if 0 <= b < DEC_BATCH:
                        act.wait_ge(sem("m_psTurned"), b + 1)
                        if b >= 2:
                            act.wait_ge(sem("m_smixed"), b - 1)
                        act.activation(psT[:, b % 2, PAST], down_ps[1][:, :], ACT.Copy).then_inc(sem("m_psT"), 1)
                        act.activation(psT[:, b % 2, NEW], norm_ps[:, 0:P], ACT.Copy).then_inc(sem("m_psT"), 1)
                    b = i - 1
                    if 0 <= b < DEC_BATCH:
                        act.wait_ge(sem("m_snegmax"), b + 1)
                        act.wait_ge(sem("m_zero"), b + 1)
                        act.activation(ps_[:, b % 2, PAST], up_ps[1][:, :], ACT.Exp, bias=stat[:, b % 2, 2:3], scale=MLA_SCALE,
                                       accum_out=stat[:, b % 2, 4:5]).then_inc(sem("m_sexp"), 1)
                        at = PAST_LEN + b * DEC_SEQ
                        act.activation(ps_[:, b % 2, at:at + DEC_SEQ], down_ps[0][:, 0:DEC_SEQ], ACT.Exp,
                                       bias=stat[:, b % 2, 2:3], scale=MLA_SCALE,
                                       accum_out=stat[:, b % 2, 5:6]).then_inc(sem("m_sexp"), 1)
                    b = i
                    if b < DEC_BATCH:
                        for t in range(KV):
                            act.wait_ge(sem("m_cturned"), 3 * b + t + 1)
                            if b >= 2:
                                act.wait_ge(sem("m_sscores"), b - 1)
                            act.activation(kt[:, b % 2, t, :], gate_ps[t][:, :], ACT.Copy).then_inc(sem("m_kt_act"), 1)
                for i in range(2):
                    act.wait_ge(sem("m_vout"), i + 1)
                    act.activation(XH[:, 4 * i:4 * i + 4, SEQ:T], down_ps[i][:, :].rearrange("p (h n) -> p h n", h=4),
                                   ACT.Copy).then_inc(sem("m_oh"), 1)
                for q in range(7, 6 + KD // 2):
                    self.look_act(act, q)
                act.wait_ge(sem("stored"), 16 * 2 * TT)
                act.wait_ge(multiplied, self.c0 + self.N_CHUNKS)
                for m in range(KD):
                    norm_tile_act(act, self.s + 1, m, gain(KD * (self.s + 1) + m))
                self.look_act(act, 6 + KD // 2)
                norm_root_act(act, self.s + 1)

            def dve(self, dve):
                c0 = self.c0
                dve.wait_ge(sem("rs"), self.s + 1)
                targets = [cq[:, 0, :], cq[:, 1, :], cq[:, 2, :], ckv[:, 0, :], ckv[:, 1, :], pe_raw[:, :]]
                def root(ss, name, n):
                    dve.wait_ge(sem(ss), 1)
                    dve.tensor_scalar(var[:, 0:T], norm_ps[:, 0:T], 1.0 / n, EPS, ALU.mult, ALU.add).then_inc(sem(name), 1)
                    dve.wait_ge(sem(name), 1)
                    dve.reciprocal(var[:, 0:T], var[:, 0:T]).then_inc(sem(name), 1)

                for q in range(3):
                    for part in range(2):
                        t = 2 * q + part
                        if t == 5:
                            root("m_ssq", "m_var_q", Q_LORA)
                        dve.wait_ge(*((multiplied, c0 + q + 1) if part else (sem("m_part0"), q + 1)))
                        dve.tensor_tensor(targets[t], (gate_ps, up_ps)[part][q % 2][:, 0:T], rsb[:, 0:T], ALU.mult)\
                           .then_inc(sem("m_proj"), 1)
                    self.look_dve(dve, q)
                    for t in ((0, 1), (2,), ())[q]:
                        dve.wait_ge(sem("m_cqh"), t + 1)
                        dve.scalar_tensor_tensor(cql[:, t, :], cq[:, t, :], gain(Q_GAIN + t), cqh[:, t, :].bitcast(F32),
                                                 ALU.mult, ALU.subtract).then_inc(sem("m_cql"), 1)

                def turned_by_sin(n):
                    if n == 0:
                        dve.wait_ge(sem("mtab_in"), 16)
                    else:
                        dve.wait_ge(sem("m_rope"), 3 * n)
                    dve.wait_ge(sem("m_turned"), n + 1)
                    dve.tensor_tensor(pe_sin[:, :], misc_ps[:, 0:T], msin, ALU.mult).then_inc(sem("m_turn_read"), 1)

                turned_by_sin(0)
                dve.wait_ge(sem("m_rq"), 1)
                for g in range(4):
                    q = 3 + g
                    for part in range(3):
                        dve.wait_ge(*((multiplied, c0 + q + 1) if part == 2 else (sem("m_part0"), 3 + 2 * g + part + 1)))
                        if part == 2:
                            dve.wait_ge(sem("m_rope"), 3 * g + 1)
                        dst = qn[:, 2 * g + part, :] if part < 2 else pe_raw[:, :]
                        dve.tensor_tensor(dst, (gate_ps, up_ps, down_ps)[part][q % 2][:, 0:T], rq[:, :], ALU.mult)\
                           .then_inc(sem("m_proj"), 1)
                    if g < 2:
                        self.look_dve(dve, q)
                    if g == 0:
                        root("m_sskv", "m_var_kv", KV_LORA)
                    turned_by_sin(g + 1)
                    if g >= 2:
                        self.look_dve(dve, q)
                    if g == 1:
                        dve.wait_ge(sem("m_rkv"), 1)
                        for t in range(KV):
                            dve.scalar_tensor_tensor(ckvT[:, t, :], ckv[:, t, :], gain(KV_GAIN + t), rkv[:, :],
                                                     ALU.mult, ALU.mult).then_inc(sem("m_ckvT"), 1)

                for i in range(MLA_HEADS + 3):
                    h = i - 3
                    if h >= 0:
                        dve.wait_ge(sem("m_oh"), h + 1)
                        dve.tensor_tensor(XL[:, h, 0:SEQ], (norm_ps, misc_ps)[h % 2][:, 0:SEQ], XH[:, h, 0:SEQ].bitcast(F32),
                                          ALU.subtract).then_inc(sem("m_ol"), 1)
                    h = i - 1
                    if 0 <= h < MLA_HEADS:
                        dve.wait_ge(sem("m_scores"), h + 1)
                        at = 0
                        for blk in range(NP):
                            n = (blk + 1) * QBLK
                            dve.tensor_reduce(stat[:, h % 2, blk:blk + 1], up_ps[h % 2][:, at:at + n], AX.X, ALU.max)\
                               .then_inc(sem("m_max"), 1)
                            at += n
                        dve.wait_ge(sem("m_max"), 2 * (h + 1))
                        dve.tensor_scalar(stat[:, h % 2, 2:4], stat[:, h % 2, 0:2], -MLA_SCALE, None, ALU.mult)\
                           .then_inc(sem("m_negmax"), 1)
                        dve.wait_ge(sem("m_exp"), 2 * (h + 1))
                        dve.reciprocal(stat[:, h % 2, 6:8], stat[:, h % 2, 4:6]).then_inc(sem("m_inv"), 1)
                        dve.wait_ge(sem("m_inv"), h + 1)
                        at = 0
                        for blk in range(NP):
                            n = (blk + 1) * QBLK
                            dve.tensor_scalar(pr[:, h % 2, at:at + n], pr[:, h % 2, at:at + n], stat[:, h % 2, 6 + blk:7 + blk],
                                              None, ALU.mult).then_inc(sem("m_pr"), 1)
                            at += n

                for i in range(DEC_BATCH + 2):
                    b = i - 1
                    if 0 <= b < DEC_BATCH:
                        st = stat[:, b % 2, :]
                        dve.wait_ge(sem("m_sscores"), b + 1)
                        dve.tensor_reduce(st[:, 0:1], up_ps[1][:, :], AX.X, ALU.max).then_inc(sem("m_smax"), 1)
                        dve.tensor_reduce(st[:, 1:2], down_ps[0][:, 0:DEC_SEQ], AX.X, ALU.max).then_inc(sem("m_smax"), 1)
                        dve.wait_ge(sem("m_smax"), 3 * b + 2)
                        dve.tensor_tensor(st[:, 3:4], st[:, 0:1], st[:, 1:2], ALU.max).then_inc(sem("m_smax"), 1)
                        dve.wait_ge(sem("m_smax"), 3 * b + 3)
                        dve.tensor_scalar(st[:, 2:3], st[:, 3:4], -MLA_SCALE, None, ALU.mult).then_inc(sem("m_snegmax"), 1)
                        dve.wait_ge(sem("m_sexp"), 2 * (b + 1))
                        dve.tensor_tensor(st[:, 6:7], st[:, 4:5], st[:, 5:6], ALU.add).then_inc(sem("m_sinv"), 1)
                        dve.wait_ge(sem("m_sinv"), 2 * b + 1)
                        dve.reciprocal(st[:, 7:8], st[:, 6:7]).then_inc(sem("m_sinv"), 1)
                        dve.wait_ge(sem("m_sinv"), 2 * b + 2)
                        dve.tensor_scalar(ps_[:, b % 2, :], ps_[:, b % 2, :], st[:, 7:8], None, ALU.mult).then_inc(sem("m_ps"), 1)
                    b = i
                    if b < DEC_BATCH:
                        dve.wait_ge(sem("m_cturned"), 3 * b + 3)
                        if b >= 2:
                            dve.wait_ge(sem("m_sscores"), b - 1)
                        dve.tensor_copy(kt[0:ROPE, b % 2, KV, :], up_ps[0][0:ROPE, :]).then_inc(sem("m_kt_dve"), 1)
                    b = i - 2
                    if b >= 0:
                        dve.wait_ge(sem("m_smixed"), b + 1)
                        dve.tensor_copy(lat[:, :, b, :, :].rearrange("p t h q -> p t (h q)"),
                                        misc_ps[:, 0:KV * P].rearrange("p (t n) -> p t n", t=KV))\
                           .then_inc(sem("m_olat"), 1)
                for i in range(2):
                    dve.wait_ge(sem("m_oh"), MLA_HEADS + i + 1)
                    dve.tensor_tensor(XL[:, 4 * i:4 * i + 4, SEQ:T], down_ps[i][:, :].rearrange("p (h n) -> p h n", h=4),
                                      XH[:, 4 * i:4 * i + 4, SEQ:T].bitcast(F32), ALU.subtract).then_inc(sem("m_ol"), 1)

                for g in range(KD // 2):
                    for part in range(2):
                        m = 2 * g + part
                        dve.wait_ge(*((multiplied, c0 + 7 + g + 1) if part else (sem("m_o_part0"), g + 1)))
                        dve.tensor_tensor(X[:, m, :], X[:, m, :], (gate_ps, up_ps)[part][g % 2][:, 0:T], ALU.add)\
                           .then_inc(sem(f"x_ready{self.s + 1}"), 1)
                    if g < KD // 2 - 1:
                        self.look_dve(dve, 7 + g)
                dve.wait_ge(sem("stored"), 16 * 2 * TT)
                for m in range(KD):
                    norm_tile_dve(dve, self.s + 1, m, gain(KD * (self.s + 1) + m))
                self.look_dve(dve, 6 + KD // 2)
                norm_root_dve(dve, self.s + 1)

            def pool(self, pool):
                pool.wait_ge(multiplied, self.c0)
                pool.memset(mask_q[:, :], 0.0).then_inc(sem("m_mask"), 1)
                pool.memset(mask_k[:, :], -1e30).then_inc(sem("m_mask"), 1)
                pool.wait_ge(sem("m_mask"), 2)
                pool.memset(mask_q[:, 0:CHUNK], 1.0).then_inc(sem("m_mask"), 1)
                for name, src, n, total, ready in (("q", cq, KQ, acc_q, 0), ("kv", ckv, KV, acc_kv, KQ)):
                    for t in range(n):
                        pool.wait_ge(sem("m_proj"), ready + t + 1)
                        if t:
                            pool.wait_ge(sem(f"m_acc_{name}"), t)
                        dst = sq[:, 0, :] if t else total[:, :]
                        pool.tensor_tensor(dst, src[:, t, :], src[:, t, :], ALU.mult)\
                            .then_inc(sem(f"m_sq_{name}" if t else f"m_acc_{name}"), 1)
                        if t:
                            pool.wait_ge(sem(f"m_sq_{name}"), t)
                            pool.tensor_tensor(total[:, :], total[:, :], sq[:, 0, :], ALU.add).then_inc(sem(f"m_acc_{name}"), 1)
                for n in range(5):
                    outs = [(0, qp[:, 2 * n - 2, :]), (ROPE, qp[:, 2 * n - 1, :])] if n else [(ROPE, kpT[:, :])]
                    if n == 0:
                        pool.wait_ge(sem("mtab_in"), 16)
                    else:
                        pool.wait_ge(sem("m_rope"), 3 * n)
                    pool.wait_ge(sem("m_proj"), 6 + 3 * n)
                    pool.tensor_tensor(pe_cos[:, :], pe_raw[:, :], mcos, ALU.mult).then_inc(sem("m_rope"), 1)
                    pool.wait_ge(sem("m_rope"), 3 * n + 1)
                    pool.wait_ge(sem("m_turn_read"), n + 1)
                    for lo, dst in outs:
                        pool.tensor_tensor(dst, pe_cos[lo:lo + ROPE, :], pe_sin[lo:lo + ROPE, :], ALU.add)\
                            .then_inc(sem("m_rope"), 1 if len(outs) == 2 else 2)
                pool.wait_ge(sem("m_rope"), 3 + 3 * 4)
                pool.tensor_copy(qps[:, :, :, :], qp[:, :, SEQ:T].rearrange("p h (b q) -> p b h q", b=DEC_BATCH))\
                    .then_inc(sem("m_qps"), 1)
                for b in range(DEC_BATCH):
                    if b == 0:
                        pool.wait_ge(sem("m_prT"), MLA_HEADS)
                        pool.wait_ge(sem("m_ol"), MLA_HEADS)
                    if b >= 2:
                        pool.wait_ge(sem("m_psTurned"), b - 1)
                    pool.memset(ps_[:, b % 2, NEW], 0.0).then_inc(sem("m_zero"), 1)
                norm_sums_pool(pool, self.s + 1)

        HV, E, D = RET_DV, RET_DV // P, RET_DK // P
        PAIR = 2 * DEC_SEQ
        PAIRS = DEC_BATCH // 2
        N_NEW = D * (DEC_BATCH + 1)
        HC = 4 * P + P + 8
        DECAY, XI, ZETA = slice(0, 4 * P), slice(4 * P, 5 * P), 5 * P
        G16 = ZETA + 4
        with ExitStack() as r:
            rturn = sb("rturn", [P, 2, T], F32, r)
            hc = sb("hc", [P, HC], F32, r)
            rot4 = sb("rot4", [P, 4, T], F32, r)
            qT = sb("qT", [P, D, T], F32, r)
            kT = sb("kT", [P, D, T], F32, r)
            kh = sb("kh", [P, 4, RET_DK], F32R, r)
            kl = sb("kl", [P, 4, RET_DK], F32R, r)
            vh = sb("vh", [P, TT, HV], F32R, r)
            vl = sb("vl", [P, TT, HV], F32R, r)
            gt = sb("gt", [P, 2, T], F32, r)
            sg = sb("sg", [P, E, T], F32, r)
            at_ = gt[:, :, :].rearrange("p e n -> p (e n)")[:, 0:4 * P]
            ah = sb("ah", [P, 4 * P], F32R, r)
            al = sb("al", [P, 4 * P], F32R, r)
            qz = sb("qz", [P, D, DEC_BATCH * PAIR], F32, r)
            st = sb("st", [P, DEC_BATCH, D, HV], F32, r)
            mark = sb("mark", [P, 5], F32, r)
            nsp = sb("nsp", [P, D, HV], F32, r)
            on = sb("on", [P, TT, HV], F32, r)
            rst = sb("rst", [P, 3, 4], F32, r)
            zf = sb("zf", [P, 2, T], F32, r)
            zh = sb("zh", [P, E, T], F32R, r)
            zl = sb("zl", [P, E, T], F32R, r)

        class Retention:
            PER = 8
            STORES = (16 * PAIRS, 16 * (PAIRS + 1))

            def __init__(self, s, c0):
                self.s, self.c0 = s, c0
                self.stored = (sem("r_stored0"), sem("r_stored1"))
                self.st_in = (sem("r_st_in0"), sem("r_st_in1"))
                self.x_base = 1 + KD * (RET_HEADS - 1)

            Q_BANKS, K_BANKS = (bank[1], bank[7]), (bank[2], bank[3])
            V_BANKS = ((bank[0], bank[4], bank[5]), (bank[6], bank[1], bank[7]))
            TURNED_K, SCORES = (bank[2], bank[2], bank[3]), bank[4]
            O_BANKS = (bank[5], bank[6], bank[7])
            G_BANKS = (bank[0], bank[1], bank[0], bank[1])
            NEW_BANKS = (bank[2:6] * 3) + [bank[2], bank[3], bank[4], bank[6], bank[7], bank[1]]
            TURNED_O = (bank[6], bank[7], bank[0], bank[5])
            OUT_BANKS = (bank[0], bank[5], bank[2], bank[3], bank[4], bank[6], bank[0], bank[5])

            def look_act(self, act, h, q):
                c, s = self.c0 + q + 2, (self.c0 + q) % 2
                split_hi(act, c + self.PER * h, s, c // 2 + self.PER // 2 * h, SLOT)

            def look_dve(self, dve, h, q):
                split_lo(dve, self.c0 + q + 2 + self.PER * h, (self.c0 + q) % 2, SLOT)

            def sp(self, sp):
                win = a["w_ret_in"][0].rearrange("(k p) n -> p k n", p=P)
                wout = a["w_ret_out"][0].rearrange("(k p) n -> p k n", p=P)
                first, second = (0, KD * P), (KD * P, 2 * KD * P)
                k0, v0 = RET_HEADS * RET_DK, 2 * RET_HEADS * RET_DK
                g0 = v0 + RET_HEADS * HV

                def chunk(h, q, pieces):
                    load(sp, self.c0 + q + self.PER * h, (self.c0 + q) % 2, pieces)

                def tiles(col):
                    return [(first, win[:, :, bass.ds(col, P)]), (second, win[:, :, bass.ds(col + P, P)])]

                with sp.Fori(0, RET_HEADS) as h:
                    chunk(h, 0, tiles(h * RET_DK))
                    chunk(h, 1, tiles(h * RET_DK + k0))
                    for j in range(2):
                        w = win[:, :, bass.ds(h * HV + (v0 + j * 2 * P), 2 * P)]
                        chunk(h, 2 + j, [(first, w[:, 0:KD // 2, :]), (second, w[:, KD // 2:KD, :])])
                    for j in range(2):
                        chunk(h, 4 + j, tiles(h * HV + (g0 + j * 2 * P)))
                    for j in range(2):
                        w = wout[:, :, j * 4 * P:(j + 1) * 4 * P]
                        chunk(h, 6 + j, [(first, w[:, bass.ds(h * E, E // 2), :]), (second, w[:, bass.ds(h * E + E // 2, E // 2), :])])

            @property
            def x_done(self):
                return sem(f"x_ready{self.s + 1}")

            def sp_end(self, sp):
                for i in range(2):
                    sp.wait_ge(self.stored[i], self.STORES[i] * RET_HEADS + 16)

            def turned_keys(self):
                t0, t1, ts = (ps[:, at:at + RET_DK] for ps, at in zip(self.TURNED_K, (0, RET_DK, 0)))
                return t0, t1, ts, ts

            def pe(self, pe):
                self.pe_columns(pe, 0, 0, self.Q_BANKS, wait_x=True)
                norm_sum_pe(pe, self.s)
                with pe.Fori(0, RET_HEADS - 1) as h:
                    self.pe_head(pe, h)
                    self.pe_columns(pe, h + 1, 0, self.Q_BANKS)
                self.pe_head(pe, RET_HEADS - 1)

            def pe_columns(self, pe, h, q, banks, wait_x=False):
                s = (self.c0 + q) % 2
                pe.wait_ge(lo_done, self.PER * h + (self.c0 + q + 1))
                for part, ps in enumerate(banks):
                    for k in range(KD):
                        if wait_x and part == 0:
                            pe.wait_ge(sem("xl"), KD * self.s + k + 1)
                        mm = product(pe, ps[:, 0:T], lambda W, k: W[:, s, (part * KD + k) * P:(part * KD + k + 1) * P],
                                     k, XH[:, k, :], XL[:, k, :], k == 0, k == KD - 1)
                    mm.then_inc(multiplied if part else sem("r_part"), 1)

            def pe_head(self, pe, h):
                c = self.c0 + self.PER * h

                def slot(q):
                    return (self.c0 + q) % 2

                def values(q, banks, free=None):
                    pe.wait_ge(lo_done, c + (q + 1))
                    if free:
                        pe.wait_ge(*free)
                    for t, ps in enumerate(banks):
                        for k in range(KD):
                            wh, wl = WH[:, slot(q), k * 2 * P:(k + 1) * 2 * P], WL[:, slot(q), k * 2 * P:(k + 1) * 2 * P]
                            xh, xl = XH[:, k, t * P:(t + 1) * P], XL[:, k, t * P:(t + 1) * P]
                            pe.matmul(ps[:, 0:2 * P], xh, wh, start=(k == 0), stop=False)
                            pe.matmul(ps[:, 0:2 * P], xh, wl, start=False, stop=False)
                            mm = pe.matmul(ps[:, 0:2 * P], xl, wh, start=False, stop=(k == KD - 1))
                        mm.then_inc(multiplied if t == TT - 1 else sem("r_part"), 1)

                pe.wait_ge(self.x_done, KD * h + 1)
                self.pe_columns(pe, h, 1, self.K_BANKS)
                values(2, self.V_BANKS[0])
                values(3, self.V_BANKS[1], (sem("r_rot"), 8 * h + 4))

                pe.wait_ge(sem("r_T"), 4 * h + 4)
                for t, ps in enumerate(self.TURNED_K):
                    for d in range(D):
                        at = (t % 2 * D + d) * P
                        mm = pe.transpose(ps[:, at:at + P], kT[:, d, t * P:(t + 1) * P], ident[:, :])
                mm.then_inc(sem("r_k_turned"), 1)
                pe.wait_ge(sem("r_vl"), 6 * h + 2)
                for at, ks, qs in ((0, slice(0, P), slice(0, SEQ)), (2 * P, slice(P, SEQ), slice(P, SEQ)),
                                   (3 * P, slice(SEQ, T), slice(SEQ, T))):
                    n = qs.stop - qs.start
                    for d in range(D):
                        mm = pe.matmul(self.SCORES[:, at:at + n], kT[:, d, ks], qT[:, d, qs], start=(d == 0), stop=(d == D - 1))
                mm.then_inc(sem("r_scores"), 1)
                o0, o1, os = self.O_BANKS
                pe.wait_ge(sem("r_vl"), 6 * h + 6)
                pe.wait_ge(sem("r_qz"), D * h + D)
                for odd in range(2):
                    pe.wait_ge(self.st_in[odd], 16 * PAIRS * h + 16 * PAIRS)
                    for d in range(D):
                        for j in range(PAIRS):
                            b = 2 * j + odd
                            pe.matmul(os[j * PAIR:(j + 1) * PAIR, :], qz[:, d, b * PAIR:(b + 1) * PAIR], st[:, b, d, :],
                                      start=(odd == 0 and d == 0), stop=False)
                pe.wait_ge(sem("r_al"), h + 1)

                def weighted(o, block, t, first, last):
                    a = slice(block * P, (block + 1) * P)
                    pe.matmul(o[:, :], ah[:, a], vh[:, t, :], start=first, stop=False)
                    pe.matmul(o[:, :], ah[:, a], vl[:, t, :], start=False, stop=False)
                    return pe.matmul(o[:, :], al[:, a], vh[:, t, :], start=False, stop=last)
                weighted(os, 3, 2, False, True)
                weighted(o0, 0, 0, True, True)
                weighted(o1, 1, 0, True, False)
                weighted(o1, 2, 1, False, True).then_inc(sem("r_o"), 1)

                def new_states(part):
                    odd, d = part // D, part % D
                    if part:
                        pe.wait_ge(sem("r_ns"), N_NEW * h + PAIRS * part)
                    if part == 3:
                        pe.wait_ge(sem("r_z"), E * h + 1)
                    if part == 0:
                        pe.wait_ge(sem("r_kl"), 4 * h + 4)
                        pe.wait_ge(sem("r_on"), TT * h + 1)
                    for n, (k, v) in enumerate(((kh, vh), (kh, vl), (kl, vh))):
                        for j in range(PAIRS):
                            rows = slice(j * PAIR, (j + 1) * PAIR)
                            mm = pe.matmul(self.NEW_BANKS[PAIRS * part + j][:, :], k[rows, 2 + odd, d * P:(d + 1) * P],
                                           v[rows, 2, :], start=(n == 0), stop=(n == 2))
                    mm.then_inc(sem("r_new"), 1)

                def gate(n):
                    q, part = 4 + n // 2, n % 2
                    if part == 0:
                        pe.wait_ge(lo_done, c + (q + 1))
                    if n >= 2:
                        pe.wait_ge(sem("r_gt"), E * h + (n - 1))
                    for k in range(KD):
                        mm = product(pe, self.G_BANKS[n][:, 0:T], lambda W, k: W[:, slot(q), (part * KD + k) * P:(part * KD + k + 1) * P],
                                     k, XH[:, k, :], XL[:, k, :], k == 0, k == KD - 1)
                    mm.then_inc(multiplied if part else sem("r_part"), 1)

                def turn(e):
                    for t in range(TT):
                        mm = pe.transpose(self.TURNED_O[e][:, t * P:(t + 1) * P], on[:, t, e * P:(e + 1) * P], ident[:, :])
                    mm.then_inc(sem("r_o_turned"), 1)

                for n in range(3):
                    gate(n)
                    new_states(n)
                pe.wait_ge(sem("r_on"), TT * h + TT)
                turn(0)
                turn(1)
                gate(3)
                pe.wait_ge(sem("r_gt"), E * h + 3)
                turn(2)
                pe.wait_ge(sem("r_ns"), N_NEW * h + 3 * PAIRS)
                turn(3)
                new_states(3)
                for d in range(D):
                    if d == 0:
                        pe.wait_ge(sem("r_z"), E * h + 2)
                    else:
                        pe.wait_ge(sem("r_gt"), E * h + E)
                    for t in range(2):
                        for k, v in ((kh, vh), (kh, vl), (kl, vh)):
                            mm = pe.matmul(self.NEW_BANKS[4 * PAIRS + d][:, :], k[:, t, d * P:(d + 1) * P], v[:, t, :],
                                           start=(t == 0 and k is kh and v is vh), stop=(t == 1 and k is kl))
                    mm.then_inc(sem("r_new"), 1)

                for m, ps in enumerate(self.OUT_BANKS):
                    q = 6 + m // 4
                    if m % 4 == 0:
                        pe.wait_ge(lo_done, c + (q + 1))
                    if m == 0:
                        pe.wait_ge(sem("r_z"), E * h + 3)
                    if m == 2:
                        pe.wait_ge(sem("r_ns"), N_NEW * h + N_NEW)
                    if m >= 6:
                        pe.wait_ge(self.x_done, KD * h + (m - 6 + 2))
                    for k in range(E):
                        if m == 0:
                            pe.wait_ge(sem("r_zl"), E * h + (k + 1))
                        mm = product(pe, ps[:, 0:T], lambda W, k: W[:, slot(q), (4 * k + m % 4) * P:(4 * k + m % 4 + 1) * P],
                                     k, zh[:, k, :], zl[:, k, :], k == 0, k == E - 1)
                    mm.then_inc(multiplied if m % 4 == 3 else sem("r_out"), 1)

            def act(self, act):
                with act.Fori(0, RET_HEADS - 1) as h:
                    self.act_head(act, h)
                    self.look_act(act, h, self.PER - 1)
                self.act_head(act, RET_HEADS - 1)
                for m in range(KD):
                    norm_tile_act(act, self.s + 1, m, gain(KD * (self.s + 1) + m), self.x_base)
                self.look_act(act, RET_HEADS - 1, self.PER - 1)
                for i in range(2):
                    act.wait_ge(self.stored[i], self.STORES[i] * RET_HEADS + 16)
                norm_root_act(act, self.s + 1)

            def act_head(self, act, h):
                c = self.c0 + self.PER * h
                for q in (0, 1):
                    self.look_act(act, h, q)

                def value_tiles(j):
                    for t, ps in enumerate(self.V_BANKS[j]):
                        if t < TT - 1:
                            act.wait_ge(sem("r_part"), 8 * h + (2 + 2 * j + t + 1))
                        else:
                            act.wait_ge(multiplied, c + (2 + j + 1))
                        act.activation(vh[:, t, j * 2 * P:(j + 1) * 2 * P], ps[:, 0:2 * P], ACT.Copy,
                                       scale=rsb[:, T + t:T + t + 1]).then_inc(sem("r_v"), 1)

                def silu(e):
                    act.wait_ge(sem("r_gt"), E * h + (e + 1))
                    act.activation(sg[:, e, :], gt[:, e % 2, :], ACT.Silu).then_inc(sem("r_sg"), 1)

                def z_hi(e):
                    act.wait_ge(sem("r_z"), E * h + (e + 1))
                    act.activation(zh[:, e, :], zf[:, e % 2, :], ACT.Copy).then_inc(sem("r_zh"), 1)

                value_tiles(0)
                self.look_act(act, h, 2)
                value_tiles(1)
                act.wait_ge(sem("r_hc_in"), 16 * h + 16)
                act.wait_ge(sem("r_k_turned"), h + 1)
                for i, src in enumerate(self.turned_keys()):
                    act.activation(kh[:, i, :], src, ACT.Copy, scale=hc[:, ZETA + i:ZETA + i + 1]).then_inc(sem("r_kh"), 1)
                act.wait_ge(sem("r_at"), h + 1)
                act.activation(ah[:, :], at_, ACT.Copy).then_inc(sem("r_ah"), 1)
                self.look_act(act, h, 3)
                act.wait_ge(sem("r_o"), h + 1)
                for t in range(TT):
                    act.activation(on[:, t, :], self.O_BANKS[t][:, :], ACT.Square, accum_out=rst[:, 0, t:t + 1]).then_inc(sem("r_sq"), 1)
                act.wait_ge(sem("r_var"), 2 * h + 2)
                act.activation(rst[:, 2, 0:TT], rst[:, 1, 0:TT], ACT.Sqrt).then_inc(sem("r_root"), 1)
                act.wait_ge(sem("r_root"), h + 1)
                for t in range(TT):
                    act.activation(on[:, t, :], self.O_BANKS[t][:, :], ACT.Copy, scale=rst[:, 2, t:t + 1]).then_inc(sem("r_on"), 1)
                silu(0)
                silu(1)
                self.look_act(act, h, 4)
                silu(2)
                z_hi(0)
                z_hi(1)
                silu(3)
                z_hi(2)
                z_hi(3)
                for q in (5, 6):
                    self.look_act(act, h, q)

            def dve(self, dve):
                dve.wait_ge(sem("rs"), self.s + 1)
                for i in range(2):
                    dve.wait_ge(self.stored[i], 16)
                    ins = dve.tensor_tensor(rturn[:, i, :], rturn[:, i, :], rsb[:, 0:T], ALU.mult)
                    ins.then_inc(sem("r_rturn"), 1)
                dve.wait_ge(sem("r_rturn"), 2)
                with dve.Fori(0, RET_HEADS - 1) as h:
                    self.dve_head(dve, h)
                    self.look_dve(dve, h, self.PER - 1)
                self.dve_head(dve, RET_HEADS - 1)
                for m in range(KD):
                    norm_tile_dve(dve, self.s + 1, m, gain(KD * (self.s + 1) + m))
                self.look_dve(dve, RET_HEADS - 1, self.PER - 1)
                for i in range(2):
                    dve.wait_ge(self.stored[i], self.STORES[i] * RET_HEADS + 16)
                norm_root_dve(dve, self.s + 1)

            def dve_head(self, dve, h):
                c = self.c0 + self.PER * h
                cos, sin = rturn[:, 0, :], rturn[:, 1, :]
                for i in range(2):
                    dve.wait_ge(sem("r_part"), 8 * h + (i + 1))
                    if i:
                        dve.wait_ge(sem("r_T"), 4 * h + 2)
                    x1, x2 = (self.Q_BANKS, self.K_BANKS)[i]
                    dve.tensor_tensor(rot4[:, 0, :], x1[:, 0:T], cos, ALU.mult).then_inc(sem("r_rot"), 1)
                    dve.tensor_tensor(rot4[:, 1, :], x1[:, 0:T], sin, ALU.mult).then_inc(sem("r_rot"), 1)
                    dve.wait_ge(multiplied, c + (i + 1))
                    dve.tensor_tensor(rot4[:, 2, :], x2[:, 0:T], sin, ALU.mult).then_inc(sem("r_rot"), 1)
                    dve.tensor_tensor(rot4[:, 3, :], x2[:, 0:T], cos, ALU.mult).then_inc(sem("r_rot"), 1)
                    self.look_dve(dve, h, i)
                def value_rests(j):
                    for t, ps in enumerate(self.V_BANKS[j]):
                        dve.wait_ge(sem("r_v"), 6 * h + (3 * j + t + 1))
                        cols = slice(j * 2 * P, (j + 1) * 2 * P)
                        dve.scalar_tensor_tensor(vl[:, t, cols], ps[:, 0:2 * P], rsb[:, T + t:T + t + 1],
                                                 vh[:, t, cols].bitcast(F32), ALU.mult, ALU.subtract).then_inc(sem("r_vl"), 1)
                value_rests(0)
                self.look_dve(dve, h, 2)
                value_rests(1)
                dve.wait_ge(sem("r_hc_in"), 16 * h + 16)
                dve.wait_ge(sem("r_scores"), h + 1)
                dve.tensor_tensor(at_, self.SCORES[:, :], hc[:, DECAY], ALU.mult).then_inc(sem("r_at"), 1)
                for i, src in enumerate(self.turned_keys()):
                    dve.wait_ge(sem("r_kh"), 4 * h + (2, 4)[i // 2])
                    dve.scalar_tensor_tensor(kl[:, i, :], src, hc[:, ZETA + i:ZETA + i + 1], kh[:, i, :].bitcast(F32),
                                             ALU.mult, ALU.subtract).then_inc(sem("r_kl"), 1)
                dve.wait_ge(sem("r_ah"), h + 1)
                dve.tensor_tensor(al[:, :], at_, ah[:, :].bitcast(F32), ALU.subtract).then_inc(sem("r_al"), 1)
                self.look_dve(dve, h, 3)
                dve.wait_ge(sem("r_sq"), TT * h + TT)
                dve.tensor_scalar(rst[:, 1, 0:TT], rst[:, 0, 0:TT], 1.0 / HV, EPS, ALU.mult, ALU.add).then_inc(sem("r_var"), 1)
                dve.wait_ge(sem("r_var"), 2 * h + 1)
                dve.reciprocal(rst[:, 1, 0:TT], rst[:, 1, 0:TT]).then_inc(sem("r_var"), 1)

                def gate(e):
                    if e % 2:
                        dve.wait_ge(multiplied, c + (4 + e // 2 + 1))
                    else:
                        dve.wait_ge(sem("r_part"), 8 * h + (6 + e // 2 + 1))
                    if e >= 2:
                        dve.wait_ge(sem("r_sg"), E * h + (e - 1))
                    dve.tensor_tensor(gt[:, e % 2, :], self.G_BANKS[e][:, 0:T], rsb[:, 0:T], ALU.mult).then_inc(sem("r_gt"), 1)

                def new_states(part):
                    odd, d = part // D, part % D
                    dve.wait_ge(sem("r_new"), (4 + D) * h + (part + 1))
                    for j in range(PAIRS):
                        n = PAIRS * part + j
                        old = st[:, 2 * j + odd, d, :]
                        dve.scalar_tensor_tensor(old, old, hc[:, G16:G16 + 1], self.NEW_BANKS[n][:, :],
                                                 ALU.mult, ALU.add).then_inc(sem("r_ns"), 1)

                def z(e):
                    dve.wait_ge(sem("r_o_turned"), E * h + (e + 1))
                    dve.wait_ge(sem("r_sg"), E * h + (e + 1))
                    if e >= 2:
                        dve.wait_ge(sem("r_zl"), E * h + (e - 1))
                    dve.scalar_tensor_tensor(zf[:, e % 2, :], self.TURNED_O[e][:, 0:T], gain(E * h + (RET_GAIN + e)),
                                             sg[:, e, :], ALU.mult, ALU.mult).then_inc(sem("r_z"), 1)

                for e in range(2):
                    gate(e)
                    new_states(e)
                self.look_dve(dve, h, 4)
                gate(2)
                new_states(2)
                z(0)
                z(1)
                self.dve_zl(dve, h, 0)
                self.dve_zl(dve, h, 1)
                gate(3)
                z(2)
                z(3)
                self.dve_zl(dve, h, 2)
                self.dve_zl(dve, h, 3)
                new_states(3)
                dve.wait_ge(self.stored[1], self.STORES[1] * h + 16)
                for d in range(D):
                    n = 4 * PAIRS + d
                    dve.wait_ge(sem("r_new"), (4 + D) * h + (4 + d + 1))
                    dve.tensor_copy(nsp[:, d, :], self.NEW_BANKS[n][:, :]).then_inc(sem("r_ns"), 1)
                self.look_dve(dve, h, 5)
                for m, ps in enumerate(self.OUT_BANKS):
                    if m % 4 < 3:
                        dve.wait_ge(sem("r_out"), 6 * h + (3 * (m // 4) + m % 4 + 1))
                    else:
                        dve.wait_ge(multiplied, c + (6 + m // 4 + 1))
                    dve.tensor_tensor(X[:, m, :], X[:, m, :], ps[:, 0:T], ALU.add).then_inc(self.x_done, 1)
                    if m == 3:
                        self.look_dve(dve, h, 6)

            def dve_zl(self, dve, h, e):
                dve.wait_ge(sem("r_zh"), E * h + (e + 1))
                dve.tensor_tensor(zl[:, e, :], zf[:, e % 2, :], zh[:, e, :].bitcast(F32), ALU.subtract).then_inc(sem("r_zl"), 1)

            def pool(self, pool):
                pool.wait_ge(multiplied, self.c0)
                for i in range(2):
                    pool.dma_start(rturn[:, i, :], a["c_rtab"][:, i * T:(i + 1) * T]).then_inc(self.stored[i], 16)
                pool.memset(rst[:, 2, 3:4], 0.0).then_inc(self.x_done, 1)
                pool.memset(qz[:, :, :], 0.0).then_inc(sem("r_zero"), 1)
                pool.wait_ge(sem("r_zero"), 1)

                def head_of(x, h):
                    return x.rearrange("h (d p) e -> p (h d) e", p=P)[:, bass.ds(h * D, D), :]

                def wait_at_mark(i, count, value):
                    pool.wait_ge(count, value)
                    pool.tensor_tensor(mark[:, i:i + 1], ones[:, 0:1], ones[:, 0:1], ALU.mult).then_inc(sem("r_mark"), 1)

                with pool.Fori(0, RET_HEADS) as h:
                    pool.dma_start(hc[:, :], a["c_ret"][:, bass.ds(h * HC, HC)]).then_inc(sem("r_hc_in"), 16)
                    for odd in range(2):
                        wait_at_mark(odd, self.stored[odd], self.STORES[odd] * h + 16)
                        for b in range(odd, DEC_BATCH, 2):
                            pool.dma_start(st[:, b, :, :], head_of(a["state_ret"][0, b], h)).then_inc(self.st_in[odd], 16)
                    for i, dst in enumerate((qT, kT)):
                        pool.wait_ge(sem("r_rot"), 8 * h + (4 * i + 4))
                        pool.tensor_tensor(dst[:, 0, :], rot4[:, 0, :], rot4[:, 2, :], ALU.subtract).then_inc(sem("r_T"), 1)
                        pool.tensor_tensor(dst[:, 1, :], rot4[:, 1, :], rot4[:, 3, :], ALU.add).then_inc(sem("r_T"), 1)
                        if i == 0:
                            pool.wait_ge(sem("r_hc_in"), 16 * h + 16)
                            pool.wait_ge(sem("r_T"), 4 * h + 2)
                            for d in range(D):
                                def runs(x, n):
                                    return x.rearrange("p (j e n) -> p j e n", e=n, n=DEC_SEQ)
                                pool.tensor_tensor(runs(qz[:, d, :], 4)[:, :, 0:4:3, :], runs(qT[:, d, SEQ:T], 2),
                                                   runs(hc[:, XI], 2), ALU.mult).then_inc(sem("r_qz"), 1)
                    for odd in range(2):
                        wait_at_mark(2 + odd, sem("r_ns"), N_NEW * h + 2 * PAIRS * (odd + 1))
                        for b in range(odd, DEC_BATCH, 2):
                            pool.dma_start(head_of(out["new_state_sample"][0, b], h), st[:, b, :, :])\
                                .then_inc(self.stored[odd], 16)
                    wait_at_mark(4, sem("r_ns"), N_NEW * h + N_NEW)
                    pool.dma_start(head_of(out["new_state_prompt"][0, 0], h), nsp[:, :, :]).then_inc(self.stored[1], 16)
                norm_sums_pool(pool, self.s + 1, self.x_base)

        C = 2 * KD + KF
        c_mla, c_ret = C, 3 * C + Mla.N_CHUNKS
        c_last = c_ret + Retention.PER * RET_HEADS
        whole, half = (SLOT, SLOT), (0, 0)
        phases = [Ffn(0, 0, 1, 0, 0, whole), Mla(1, c_mla, whole), Ffn(1, 0, 2, 2, c_mla + Mla.N_CHUNKS, whole),
                  Ffn(2, 1, 1, 3, c_mla + Mla.N_CHUNKS + C, whole), Retention(4, c_ret), Ffn(3, 1, 2, 5, c_last, half)]

        block = ctx.enter_context(nc.Block())

        @block.sync
        def _(sp):
            start_sp(sp, phases[0])
            for ph in phases:
                ph.sp(sp)
            end_sp(sp)
            for ph in phases:
                if isinstance(ph, Retention):
                    ph.sp_end(sp)
            sp.wait_ge(sem("stored"), 16 * STORES)

        @block.gpsimd
        def _(pool):
            start_pool(pool)
            for ph in phases:
                ph.pool(pool)

        @block.scalar
        def _(act):
            start_act(act)
            for ph in phases:
                ph.act(act)
            end_act(act)

        @block.vector
        def _(dve):
            start_dve(dve)
            for ph in phases:
                ph.dve(dve)
            end_dve(dve)

        @block.tensor
        def _(pe):
            start_pe(pe)
            for ph in phases:
                ph.pe(pe)
            end_pe(pe)


def constants():
    f = np.float32
    pos = np.concatenate([np.arange(SEQ), np.tile(PAST_LEN + np.arange(DEC_SEQ), DEC_BATCH)]).astype(f)

    def angles(d):
        inv = f(1.0) / (f(ROPE_THETA) ** (np.arange(0, d, 2, dtype=f) / f(d)))
        ang = (inv[:, None] * pos[None, :]).astype(f).astype(np.float64)
        return np.cos(ang).astype(f), np.sin(ang).astype(f)

    turn, half = np.zeros((P, P), f), ROPE // 2
    for base in range(0, P, ROPE):
        for i in range(half):
            turn[base + half + i, base + i] = -1.0
            turn[base + i, base + half + i] = 1.0
    cos, sin = angles(ROPE)
    mla = np.concatenate([turn, np.tile(cos, (4, 1)), np.tile(sin, (4, 1))], axis=1)
    lg = np.log(f(1.0) - f(2.0) ** (-5.0 - np.arange(RET_HEADS, dtype=f))).astype(f).astype(np.float64)
    scale = RET_DK ** -0.5
    p, i = np.arange(P)[:, None], np.arange(SEQ)[None, :]
    s, j = p % DEC_SEQ, np.arange(P)[None, :]
    heads = []
    for g in lg:
        prompt = np.where(i >= p, np.exp(g * np.maximum(i - p, 0)), 0.0) * scale
        mine = (p // DEC_SEQ == j // DEC_SEQ) & (j % DEC_SEQ >= s)
        sample = np.where(mine, np.exp(g * np.maximum(j % DEC_SEQ - s, 0)), 0.0) * scale
        xi = np.broadcast_to(np.exp(g * (j % DEC_SEQ + 1)), (P, P))
        z = np.exp(g * (DEC_SEQ - 1 - s)) * scale
        even = p // DEC_SEQ % 2 == 0
        zeta = [np.exp(g * (SEQ - 1 - p)) * scale, np.exp(g * (SEQ - 1 - P - p)) * scale, z * even, z * ~even,
                np.full((P, 1), np.exp(g * DEC_SEQ)), np.zeros((P, 3))]
        heads.append(np.concatenate([prompt, prompt[:, 0:P], sample, xi] + zeta, axis=1))
    return {"c_ident": np.eye(P, dtype=f), "c_mla": mla, "c_rtab": np.concatenate(angles(RET_DK), axis=1),
            "c_ret": np.concatenate(heads, axis=1).astype(f)}


INPUTS = ["x_prompt", "x_sample", "cache_ckv", "cache_kpe", "state_ret", "norm_ffn1", "w_ffn1_gate", "w_ffn1_up",
          "w_ffn1_down", "norm_mix", "w_dq", "q_norm", "w_uq", "w_dkv", "kv_norm", "w_uk", "w_uv", "w_o_mla",
          "w_ret_in", "ret_gn", "w_ret_out", "norm_ffn2", "w_ffn2_gate", "w_ffn2_up", "w_ffn2_down", "norm_final"]
OUTPUTS = [("y_prompt", (1, SEQ, D_MODEL)), ("y_sample", (DEC_BATCH, DEC_SEQ, D_MODEL)),
           ("new_ckv_prompt", (1, 1, SEQ, KV_LORA)), ("new_kpe_prompt", (1, 1, SEQ, ROPE)),
           ("new_state_prompt", (1, 1, RET_HEADS, RET_DK, RET_DV)),
           ("new_ckv_sample", (1, DEC_BATCH, DEC_SEQ, KV_LORA)), ("new_kpe_sample", (1, DEC_BATCH, DEC_SEQ, ROPE)),
           ("new_state_sample", (1, DEC_BATCH, RET_HEADS, RET_DK, RET_DV))]


def kernel(**inputs):
    import concourse.bacc as bacc
    from concourse.bass_utils import run_bass_kernel_spmd

    nc = bacc.Bacc("TRN2", target_bir_lowering=False, num_devices=1)
    arrays = {f"{n}_dram": np.ascontiguousarray(inputs[n]) for n in INPUTS}
    arrays.update({f"{n}_dram": x for n, x in constants().items()})
    a = {n[:-5]: nc.dram_tensor(n, x.shape, mybir.dt.from_np(x.dtype), kind="ExternalInput").ap()
         for n, x in arrays.items()}
    out = {n: nc.dram_tensor(f"{n}_dram", shape, F32, kind="ExternalOutput").ap() for n, shape in OUTPUTS}
    stream_kernel(nc, a, out)
    r = run_bass_kernel_spmd(nc, [arrays], core_ids=[0]).results[0]
    return tuple(r[f"{n}_dram"] for n, _ in OUTPUTS)
```
